# Optimizing a Trainium2 kernel written in Bass

```python
import math
import jax, jax.numpy as jnp
from jax import lax
import numpy as np

D_MODEL = 1024
BATCH = 1
SEQ = 512
DEPTH = 2
DEC_BATCH = 8
DEC_SEQ = 8
PAST_LEN = 256
PAGE_SIZE = 128

N_MIXERS = 2
N_SSD_LAYERS = (DEPTH + 1) // 2
N_ATTN_LAYERS = DEPTH // 2
EPS = 1e-6
D_FF = 2816
D_INNER = 2 * D_MODEL
SSD_HEADDIM = 64
SSD_HEADS = D_INNER // SSD_HEADDIM
SSD_GROUPS = 8
SSD_HPG = SSD_HEADS // SSD_GROUPS
D_STATE = 128
CONV_W = 4
CONV_DIM = D_INNER + 2 * SSD_GROUPS * D_STATE
D_IN_PROJ = D_INNER + CONV_DIM + SSD_HEADS
SSD_CHUNK = 128
ATTN_PATTERNS = ((128, 1), (512, 4), (2048, 16))
N_ATTN_GROUPS = 3
ATTN_HPG = 8
ATTN_HEAD_DIM = 64
N_ATTN_HEADS = N_ATTN_GROUPS * ATTN_HPG
ATTN_WIDTH = ATTN_HPG * ATTN_HEAD_DIM
QKV_WIDTH = N_ATTN_GROUPS * 3 * ATTN_WIDTH
ATTN_QBLOCK = 128
NEG_INF = -1e30

kernel_name = 'hybrid_ssd_dilated_swa_macaron_step'

def rms_norm(x, g):
    xf = x.astype(jnp.float32)
    y = xf * lax.rsqrt(jnp.mean(xf * xf, axis=-1, keepdims=True) + EPS)
    return (y * g.astype(jnp.float32)).astype(x.dtype)

def half_swiglu(x, g, w_in, w_out):
    a, b = jnp.split(rms_norm(x, g) @ w_in, 2, axis=-1)
    return x + 0.5 * ((jax.nn.silu(a) * b) @ w_out)

def alibi_slopes():
    h = jnp.arange(1, N_ATTN_HEADS + 1, dtype=jnp.float32)
    return (2.0 ** (-8.0 * h / N_ATTN_HEADS)).reshape(N_ATTN_GROUPS, ATTN_HPG)

def ssd_chunked(x, dt, a, bm, cm, h0):
    b, l = x.shape[:2]
    q = SSD_CHUNK if l % SSD_CHUNK == 0 else l
    nc = l // q
    f32 = jnp.float32
    x = x.reshape(b, nc, q, SSD_GROUPS, SSD_HPG, SSD_HEADDIM).astype(f32)
    dt = dt.reshape(b, nc, q, SSD_GROUPS, SSD_HPG)
    bm = bm.reshape(b, nc, q, SSD_GROUPS, D_STATE).astype(f32)
    cm = cm.reshape(b, nc, q, SSD_GROUPS, D_STATE).astype(f32)
    a_cum = jnp.cumsum(dt * a, axis=2)
    causal = jnp.tril(jnp.ones((q, q), dtype=bool))[:, :, None, None]
    seg = a_cum[:, :, :, None] - a_cum[:, :, None, :]
    decay = jnp.exp(jnp.where(causal, seg, -jnp.inf))
    cb = jnp.einsum('bcqgn,bcsgn->bcqsg', cm, bm)
    wts = cb[..., None] * decay * dt[:, :, None]
    y_diag = jnp.einsum('bcqsgj,bcsgjp->bcqgjp', wts, x)
    xw = (jnp.exp(a_cum[:, :, -1:] - a_cum) * dt)[..., None] * x
    states = jnp.einsum('bcsgn,bcsgjp->bcgjpn', bm, xw)
    chunk_decay = jnp.exp(a_cum[:, :, -1])

    def step(h, inp):
        st, dec = inp
        return dec[..., None, None] * h + st, h

    h_last, h_prev = lax.scan(step, h0.astype(f32), (jnp.moveaxis(states, 1, 0), jnp.moveaxis(chunk_decay, 1, 0)))
    h_prev = jnp.moveaxis(h_prev, 0, 1)
    y_off = jnp.einsum('bcqgn,bcgjpn->bcqgjp', cm, h_prev) * jnp.exp(a_cum)[..., None]
    y = (y_diag + y_off).reshape(b, l, SSD_GROUPS, SSD_HPG, SSD_HEADDIM)
    return y, h_last

def ssd_mixer(u, conv_state, ssm_state, w_in, conv_w, conv_b, dt_bias, a_log, d_skip, norm_g, w_out):
    b, l, _ = u.shape
    f32 = jnp.float32
    proj = u @ w_in
    z = proj[..., :D_INNER]
    xbc = proj[..., D_INNER:D_INNER + CONV_DIM]
    dt_raw = proj[..., D_INNER + CONV_DIM:]
    xpad = jnp.concatenate([conv_state.astype(xbc.dtype), xbc], axis=1)
    xc = conv_b + sum(xpad[:, k:k + l] * conv_w[k] for k in range(CONV_W))
    xc = jax.nn.silu(xc)
    new_conv = xpad[:, l:]
    xs = xc[..., :D_INNER].reshape(b, l, SSD_GROUPS, SSD_HPG, SSD_HEADDIM)
    bm = xc[..., D_INNER:D_INNER + SSD_GROUPS * D_STATE].reshape(b, l, SSD_GROUPS, D_STATE)
    cm = xc[..., D_INNER + SSD_GROUPS * D_STATE:].reshape(b, l, SSD_GROUPS, D_STATE)
    dt = jax.nn.softplus(dt_raw.astype(f32) + dt_bias.astype(f32)).reshape(b, l, SSD_GROUPS, SSD_HPG)
    a = -jnp.exp(a_log.astype(f32)).reshape(SSD_GROUPS, SSD_HPG)
    h0 = ssm_state.reshape(b, SSD_GROUPS, SSD_HPG, SSD_HEADDIM, D_STATE)
    y, h_last = ssd_chunked(xs, dt, a, bm, cm, h0)
    y = y + d_skip.astype(f32).reshape(SSD_GROUPS, SSD_HPG)[:, :, None] * xs.astype(f32)
    gz = (y.reshape(b, l, D_INNER) * jax.nn.silu(z.astype(f32))).reshape(b, l, SSD_GROUPS, D_INNER // SSD_GROUPS)
    gz = gz * lax.rsqrt(jnp.mean(gz * gz, axis=-1, keepdims=True) + EPS)
    gz = (gz.reshape(b, l, D_INNER) * norm_g.astype(f32)).astype(u.dtype)
    new_ssm = h_last.reshape(b, SSD_HEADS, SSD_HEADDIM, D_STATE).astype(ssm_state.dtype)
    return gz @ w_out, new_conv, new_ssm

def dilated_group_attention(q, kvbuf, offset, win, dil, slopes):
    b, l, h, hd = q.shape
    nk = win // dil + 1
    qb = ATTN_QBLOCK if l % ATTN_QBLOCK == 0 else l
    starts = jnp.arange(l // qb) * qb
    j = jnp.arange(nk)
    bias = -(slopes.astype(jnp.float32) * dil)[:, None, None] * j.astype(jnp.float32)

    def block(start):
        qi = start + jnp.arange(qb)
        q_blk = lax.dynamic_slice_in_dim(q, start, qb, axis=1)
        idx = offset + qi[:, None] - dil * j[None, :]
        kv = jnp.take(kvbuf, jnp.maximum(idx, 0), axis=1)
        s = jnp.einsum('bqhd,bqkhd->bhqk', q_blk, kv[:, :, :, 0]).astype(jnp.float32) + bias
        s = jnp.where((idx >= 0)[None, None], s, NEG_INF)
        lse = jax.nn.logsumexp(s, axis=-1)
        p = jnp.exp(s - lse[..., None]).astype(kv.dtype)
        o = jnp.einsum('bhqk,bqkhd->bqhd', p, kv[:, :, :, 1])
        return o, lse

    o, lse = lax.map(block, starts)
    o = jnp.moveaxis(o, 0, 1).reshape(b, l, h, hd)
    lse = jnp.transpose(lse, (1, 0, 3, 2)).reshape(b, l, h)
    return o, lse

def dilated_mixer(u, past, w_qkv, w_o):
    b, l, _ = u.shape
    qkv = (u @ w_qkv).reshape(b, l, N_ATTN_GROUPS, 3, ATTN_HPG, ATTN_HEAD_DIM)
    slopes = alibi_slopes()
    outs, lses, new_rows = [], [], []
    for g, (win, dil) in enumerate(ATTN_PATTERNS):
        q = qkv[:, :, g, 0] * (ATTN_HEAD_DIM ** -0.5)
        kv_new = qkv[:, :, g, 1:]
        kvbuf = jnp.concatenate([past[g].astype(kv_new.dtype), kv_new], axis=1)
        o, lse = dilated_group_attention(q, kvbuf, past[g].shape[1], win, dil, slopes[g])
        outs.append(o)
        lses.append(lse)
        new_rows.append(kv_new)
    w = jax.nn.softmax(jnp.stack(lses), axis=0)
    o = jnp.sum(w[..., None] * jnp.stack(outs).astype(jnp.float32), axis=0).astype(u.dtype)
    return o.reshape(b, l, ATTN_WIDTH) @ w_o, new_rows

def setup_inputs(seed: int = 0) -> dict:
    key = jax.random.key(seed)
    ks = jax.random.split(key, 24)

    def nrm(k, shape, scale):
        return jax.random.normal(k, shape, jnp.float32) * scale

    dt0 = jnp.exp(jax.random.uniform(ks[13], (N_SSD_LAYERS, SSD_HEADS), jnp.float32, math.log(1e-3), math.log(1e-1)))
    return {
        'x_prompt': nrm(ks[0], (BATCH, SEQ, D_MODEL), 1.0),
        'x_sample': nrm(ks[1], (DEC_BATCH, DEC_SEQ, D_MODEL), 1.0),
        'state_conv': nrm(ks[2], (N_SSD_LAYERS, DEC_BATCH, CONV_W - 1, CONV_DIM), 1.0),
        'state_ssm': nrm(ks[3], (N_SSD_LAYERS, DEC_BATCH, SSD_HEADS, SSD_HEADDIM, D_STATE), 0.1),
        'cache_kv_g0': nrm(ks[4], (N_ATTN_LAYERS, DEC_BATCH, min(ATTN_PATTERNS[0][0], PAST_LEN), 2, ATTN_HPG, ATTN_HEAD_DIM), 1.0),
        'cache_kv_g1': nrm(ks[5], (N_ATTN_LAYERS, DEC_BATCH, min(ATTN_PATTERNS[1][0], PAST_LEN), 2, ATTN_HPG, ATTN_HEAD_DIM), 1.0),
        'cache_kv_g2': nrm(ks[6], (N_ATTN_LAYERS, DEC_BATCH, min(ATTN_PATTERNS[2][0], PAST_LEN), 2, ATTN_HPG, ATTN_HEAD_DIM), 1.0),
        'norm_w': 1.0 + nrm(ks[7], (DEPTH, 3, D_MODEL), 0.02),
        'w_ffn_in': nrm(ks[8], (DEPTH, 2, D_MODEL, 2 * D_FF), D_MODEL ** -0.5),
        'w_ffn_out': nrm(ks[9], (DEPTH, 2, D_FF, D_MODEL), D_FF ** -0.5),
        'ssm_w_in': nrm(ks[10], (N_SSD_LAYERS, D_MODEL, D_IN_PROJ), D_MODEL ** -0.5),
        'ssm_conv_w': nrm(ks[11], (N_SSD_LAYERS, CONV_W, CONV_DIM), CONV_W ** -0.5),
        'ssm_conv_b': nrm(ks[12], (N_SSD_LAYERS, CONV_DIM), 0.02),
        'ssm_dt_bias': dt0 + jnp.log(-jnp.expm1(-dt0)),
        'ssm_a_log': jnp.log(jax.random.uniform(ks[14], (N_SSD_LAYERS, SSD_HEADS), jnp.float32, 1.0, 16.0)),
        'ssm_d': 1.0 + nrm(ks[15], (N_SSD_LAYERS, SSD_HEADS), 0.1),
        'ssm_norm_w': 1.0 + nrm(ks[16], (N_SSD_LAYERS, D_INNER), 0.02),
        'ssm_w_out': nrm(ks[17], (N_SSD_LAYERS, D_INNER, D_MODEL), D_INNER ** -0.5),
        'attn_w_qkv': nrm(ks[18], (N_ATTN_LAYERS, D_MODEL, QKV_WIDTH), D_MODEL ** -0.5),
        'attn_w_o': nrm(ks[19], (N_ATTN_LAYERS, ATTN_WIDTH, D_MODEL), ATTN_WIDTH ** -0.5),
        'norm_f': 1.0 + nrm(ks[20], (D_MODEL,), 0.02),
    }

def reference(x_prompt, x_sample, state_conv, state_ssm, cache_kv_g0, cache_kv_g1, cache_kv_g2,
              norm_w, w_ffn_in, w_ffn_out, ssm_w_in, ssm_conv_w, ssm_conv_b, ssm_dt_bias, ssm_a_log,
              ssm_d, ssm_norm_w, ssm_w_out, attn_w_qkv, attn_w_o, norm_f):
    xp, xs = x_prompt, x_sample
    bp = xp.shape[0]
    caches = (cache_kv_g0, cache_kv_g1, cache_kv_g2)
    conv_p, conv_s, ssm_p, ssm_s = [], [], [], []
    kv_p = [[] for _ in range(N_ATTN_GROUPS)]
    kv_s = [[] for _ in range(N_ATTN_GROUPS)]
    for i in range(DEPTH):
        xp = half_swiglu(xp, norm_w[i, 0], w_ffn_in[i, 0], w_ffn_out[i, 0])
        xs = half_swiglu(xs, norm_w[i, 0], w_ffn_in[i, 0], w_ffn_out[i, 0])
        li = i // N_MIXERS
        up, us = rms_norm(xp, norm_w[i, 1]), rms_norm(xs, norm_w[i, 1])
        if i % N_MIXERS == 0:
            prm = (ssm_w_in[li], ssm_conv_w[li], ssm_conv_b[li], ssm_dt_bias[li], ssm_a_log[li],
                   ssm_d[li], ssm_norm_w[li], ssm_w_out[li])
            zc = jnp.zeros((bp, CONV_W - 1, CONV_DIM), xp.dtype)
            zh = jnp.zeros((bp, SSD_HEADS, SSD_HEADDIM, D_STATE), jnp.float32)
            yp, cp, hp = ssd_mixer(up, zc, zh, *prm)
            ys, cs, hs = ssd_mixer(us, state_conv[li], state_ssm[li], *prm)
            conv_p.append(cp)
            conv_s.append(cs)
            ssm_p.append(hp)
            ssm_s.append(hs)
        else:
            empty = [jnp.zeros((bp, 0, 2, ATTN_HPG, ATTN_HEAD_DIM), xp.dtype) for _ in range(N_ATTN_GROUPS)]
            yp, rows_p = dilated_mixer(up, empty, attn_w_qkv[li], attn_w_o[li])
            ys, rows_s = dilated_mixer(us, [c[li] for c in caches], attn_w_qkv[li], attn_w_o[li])
            for g, (win, _) in enumerate(ATTN_PATTERNS):
                lp = rows_p[g].shape[1]
                kv_p[g].append(rows_p[g][:, lp - min(win, lp):])
                kv_s[g].append(rows_s[g])
        xp = xp + yp
        xs = xs + ys
        xp = half_swiglu(xp, norm_w[i, 2], w_ffn_in[i, 1], w_ffn_out[i, 1])
        xs = half_swiglu(xs, norm_w[i, 2], w_ffn_in[i, 1], w_ffn_out[i, 1])
    y_prompt = rms_norm(xp, norm_f)
    y_sample = rms_norm(xs, norm_f)
    return (y_prompt, y_sample,
            jnp.stack(conv_p), jnp.stack(conv_s), jnp.stack(ssm_p), jnp.stack(ssm_s),
            jnp.stack(kv_p[0]), jnp.stack(kv_s[0]), jnp.stack(kv_p[1]), jnp.stack(kv_s[1]),
            jnp.stack(kv_p[2]), jnp.stack(kv_s[2]))


_drawn_inputs = setup_inputs


def setup_inputs(seed=0):
    import zlib

    import numpy as np

    out = dict(_drawn_inputs(seed))
    spreads = {}
    factors = {}
    for name, (base, spread) in spreads.items():
        noise = np.random.default_rng([zlib.crc32(name.encode()), seed]).standard_normal(out[name].shape)
        drawn = base * np.exp(spread * noise) if base else spread * noise
        out[name] = __import__('jax').numpy.asarray(drawn.astype(out[name].dtype))
    for name, factor in factors.items():
        out[name] = (out[name] * factor).astype(out[name].dtype)
    return out
```

```python
from contextlib import ExitStack, contextmanager

import numpy as np

import concourse.bass as bass
from concourse import mybir

F32 = mybir.dt.float32
F32R = mybir.dt.float32r
ALU = mybir.AluOpType
ACT = mybir.ActivationFunctionType
AX = mybir.AxisListType

P = 128
D = 1024
KD = D // P
SEQ, NB, NS = 512, 8, 8
SMP = NB * NS
TOK = SEQ + SMP
HALF = TOK // 2
QTR = SEQ // 2
FF = 2816
KF = FF // P
EPS = 1e-6
HEADS, GROUPS, HPG, PD, NST = 32, 8, 4, 64, 128
DI = HEADS * PD
CH = SEQ // P
CONV = 4
XW = CONV - 1 + SEQ + NB * (CONV - 1 + NS)
XO = XW - (CONV - 1)
XS = CONV - 1 + SEQ
SW = CONV - 1 + NS
UW = 8 * P
UF = KF // 2 * P
AG, AH, HD, DIL = 3, 8, 64, 4
PAIRS = AH // 2
KEYC = 512
KEYR = ((0, 128), (128, 256), (384, 128))
BIG = 1e30

FFN_UNITS = 2 * KF + 2 * KD
U_SSD = FFN_UNITS
U_GRP = U_SSD + 1
U_FFN1 = U_SSD + 1 + 8 * GROUPS
U_ATT = U_FFN1 + 2 * FFN_UNITS
U_FFN = (0, U_FFN1, U_FFN1 + FFN_UNITS, U_ATT + 10 * PAIRS)
NORM_OF_FFN = (0, 2, 3, 5)
SSD_DVE_STEPS = 19
ATT_DVE_STEPS = 27


class Steps:

    def __init__(self, eng, sem):
        self.eng, self.sem, self.base, self.n = eng, sem, 0, 0

    def done(self, ins):
        ins.then_inc(self.sem, 1)
        self.n += 1

    def wait(self):
        self.eng.wait_ge(self.sem, self.base + self.n)

    @contextmanager
    def loop(self, first, last, per):
        start, self.n = self.n, 0
        with self.eng.Fori(first, last) as i:
            self.base = (i - first) * per + start
            yield i
        assert self.n == per, f"{self.n} signals in a turn, not {per}"
        self.base, self.n = 0, start + (last - first) * per


def step_kernel(nc, io, phases=7):
    with ExitStack() as ctx:
        def sb(name, shape, dt=F32):
            return ctx.enter_context(nc.sbuf_tensor("sb_" + name, shape, dt))

        def sem(name):
            return ctx.enter_context(nc.semaphore(name))

        x = sb("x", [P, KD, TOK])
        uh = sb("uh", [P, KD, TOK], F32R)
        ul = sb("ul", [P, KD, TOK], F32R)
        raw = sb("raw", [P, 2, UF])
        wh = sb("wh", [P, 2, UF], F32R)
        wl = sb("wl", [P, 2, UF], F32R)
        rms = sb("rms", [P, TOK])
        ssq = sb("ssq", [P, TOK])
        sqx = sb("sqx", [P, TOK])
        ones = sb("ones", [P, P])
        ident = sb("ident", [P, P])
        gains = sb("gains", [P, 7, KD])
        ps = ctx.enter_context(nc.psum_tensor("ps", [P, 8, 512], F32))

        with ExitStack() as region:
            def at(name, shape, dt=F32):
                return region.enter_context(nc.sbuf_tensor("sb_" + name, shape, dt))
            hh = at("hh", [P, KF, TOK], F32R)
            hl = at("hl", [P, KF, TOK], F32R)
            gate = at("gate", [P, TOK])
            up = at("up", [P, TOK])
        with ExitStack() as region:
            xp = at("xp", [P, 4, SEQ + (NB + 1) * SW + 1])
            acc = at("acc", [P, 2, XW + 1])
            xc = at("xc", [P, 4, TOK])
            zs = at("zs", [P, 2, TOK])
            er = at("er", [P, HPG * SEQ])
            ers = at("ers", [P, HPG * SMP])
            sg = at("sg", [P, HPG * SEQ])
            sgs = at("sgs", [SMP, HPG, SMP])
            xd = at("xd", [P, CH, HPG, PD])
            xds = at("xds", [SMP, HPG, PD])
            xw = at("xw", [P, CH, HPG, PD])
            xws = at("xws", [SMP, HPG, PD])
            bt = at("bt", [P, SEQ])
            bd = at("bd", [SMP, NB, NST])
            cbm = at("cbm", [P, SEQ])
            cbs = at("cbs", [SMP, SMP])
            hst = at("hst", [P, CH, HPG * PD])
            h0 = at("h0", [P, NB, HPG * PD])
            ysb = at("ysb", [P, 2, TOK])
            yof = at("yof", [P, 2, SMP])
            gh = at("gh", [P, 2, TOK], F32R)
            gl = at("gl", [P, 2, TOK], F32R)
            gr = at("gr", [P, TOK])
            keep = gr[0:HEADS, :]
            acT = at("acT", [HEADS, TOK])
            acm = at("acm", [HEADS, HPG, TOK])
            tok = at("tok", [P, 3, CH + 1, HEADS])
            gtok = at("gtok", [P, 3, CH + 1, HPG])
            dec = at("dec", [P, HPG, CH])
            decs = at("decs", [P, HPG, NB])
            ncv = at("ncv", [P, 4, NB + 1, CONV - 1])
            cst = at("cst", [P, GROUPS, 4, NB * (CONV - 1)])
            cw = at("cw", [P, GROUPS * 4 * (CONV + 1)])
            dsk = at("dsk", [P, GROUPS * 2])
            ng = at("ng", [P, GROUPS * 2])
            dtb = at("dtb", [HEADS, 1])
            alog = at("alog", [HEADS, 1])
            ea = at("ea", [HEADS, 1])
            mask = at("mask", [P, P])
            masks = at("masks", [SMP, SMP])
            maskb = at("maskb", [SMP, NB])
        with ExitStack() as region:
            qkv = at("qkv", [P, 9, TOK])
            vt = at("vt", [P, AG, CH, P])
            vts = at("vts", [SMP, AG, P])
            pr = at("pr", [P, 2, 768])
            pt = at("pt", [P, 2, 768])
            un = at("un", [P, CH, P])
            oh = at("oh", [P, TOK], F32R)
            ol = at("ol", [P, TOK], F32R)
            kc = at("kc", [P, NB, KEYC])
            vc = at("vc", [P, NB, 4, P])
            qz = at("qz", [P, AG, NB * (P + 2 * NS)])
            qa = at("qa", [P, AG, P])
            prs = at("prs", [P, KEYC + AG * SMP])
            pts = at("pts", [P, 4, P])
            ptn = at("ptn", [SMP, AG, P])
            d0 = at("d0", [P, CH, SEQ])
            d12 = at("d12", [P, 2, P])
            dsm = at("dsm", [P, KEYC + AG * SMP])
            slp = at("slp", [P, AG * AH])
            sls = at("sls", [P, AG * PAIRS])
            nmx = at("nmx", [P, 16])
            den = at("den", [P, 16])
            rcp = at("rcp", [P, 16])
            rmp = sqx

        const_in = sem("const_in")
        raw_in = [sem("raw_in0"), sem("raw_in1")]
        wh_done, wl_done, unit_done = sem("wh_done"), sem("wl_done"), sem("unit_done")
        x_done = sem("x_done")
        xa_done = sem("xa_done")
        u_ready = sem("u_ready")
        stat_mm, var_ready, sqrt_ready = sem("stat_mm"), sem("var_ready"), sem("sqrt_ready")
        rms_ready = sem("rms_ready")
        gate_scaled, silu_done, h_high, h_ready = sem("gate_scaled"), sem("silu_done"), sem("h_high"), sem("h_ready")
        act_self, dve_self, pool_self = sem("act_self"), sem("dve_self"), sem("pool_self")
        ssd_const, att_const = sem("ssd_const"), sem("att_const")
        dt_scaled, dt_abs, dt_exp, ea_ready = sem("dt_scaled"), sem("dt_abs"), sem("dt_exp"), sem("ea_ready")
        coef_in, coef_exp, dtok_in, dtok_mm = sem("coef_in"), sem("coef_exp"), sem("dtok_in"), sem("dtok_mm")
        tok_ready = sem("tok_ready")
        state_in, cs_in, pj_evac, nc_ready = sem("state_in"), sem("cs_in"), sem("pj_evac"), sem("nc_ready")
        conv_done, xc_ready, zs_ready = sem("conv_done"), sem("xc_ready"), sem("zs_ready")
        acm_ready, rs_mm, r_mm = sem("acm_ready"), sem("rs_mm"), sem("r_mm")
        er_done, seg_done, ers_done, segs_done = sem("er_done"), sem("seg_done"), sem("ers_done"), sem("segs_done")
        e_done, es_done, dec_ready, cp_done = sem("e_done"), sem("es_done"), sem("dec_ready"), sem("cp_done")
        t_mm, xd_done, xs_done, bt_done = sem("t_mm"), sem("xd_done"), sem("xs_done"), sem("bt_done")
        cb_mm, cbm_done, w_done = sem("cb_mm"), sem("cbm_done"), sem("w_done")
        st_mm, hst_done, y_mm, y_evac = sem("st_mm"), sem("hst_done"), sem("y_mm"), sem("y_evac")
        hm_done, ss_mm, ss_evac = sem("hm_done"), sem("ss_mm"), sem("ss_evac")
        gsq_done, gn_mm, gvar_ready, gsqrt_ready = sem("gsq_done"), sem("gn_mm"), sem("gvar_ready"), sem("gsqrt_ready")
        gz_ready = sem("gz_ready")
        gn_ready, gh_done, g_ready = sem("gn_ready"), sem("gh_done"), sem("g_ready")
        so_mm, so_evac = sem("so_mm"), sem("so_evac")
        st_h, st_hs, st_nc = sem("st_h"), sem("st_hs"), sem("st_nc")
        q_evac, vt_mm, vt_done = sem("q_evac"), sem("vt_mm"), sem("vt_done")
        cache_in, qz_done, sc_mm, max_done, exp_done = sem("cache_in"), sem("qz_done"), sem("sc_mm"), sem("max_done"), sem("exp_done")
        pt_mm, pt_done, pv_mm, un_done = sem("pt_mm"), sem("pt_done"), sem("pv_mm"), sem("un_done")
        ssc_mm, smax_done, sexp_done, snorm_done = sem("ssc_mm"), sem("smax_done"), sem("sexp_done"), sem("snorm_done")
        spt_mm, spt_done, spv_mm = sem("spt_mm"), sem("spt_done"), sem("spv_mm")
        ot_mm, oh_done, ol_done = sem("ot_mm"), sem("oh_done"), sem("ol_done")
        ao_mm, ao_evac, st_kv, qz_zero = sem("ao_mm"), sem("ao_evac"), sem("st_kv"), sem("qz_zero")
        y_ready, st_y = sem("y_ready"), sem("st_y")

        HALVES = ((0, HALF), (HALF, HALF))
        SPLIT = ((0, QTR), (QTR, TOK - QTR))
        last_norm = 6

        def one(i):
            return slice(i, i + 1) if isinstance(i, int) else bass.ds(i, 1)

        def smp(ap, q=NS):
            return ap.rearrange("p (b q) -> p b q", q=q)

        def two(ap):
            return ap.rearrange("p (h n) -> p h n", h=2)

        def perm(ap):
            return ap.rearrange("p (a t) -> p t a", t=DIL)

        block = ctx.enter_context(nc.Block())

        @block.sync
        def _(sp):
            def unit(u, parity, src, width):
                if not (isinstance(u, int) and u < 2):
                    sp.wait_ge(wl_done, u - 1)
                sp.dma_start(raw[:, parity, 0:width], src).then_inc(raw_in[parity], 16)

            def load(dst, src, signal):
                sp.dma_start(dst, src).then_inc(signal, 16)

            load(x[:, :, :], io["xT"][:, :, :], const_in)
            load(gains[:, :, :], io["gains"][:, :, :], const_in)
            load(ones[:, :], io["ones"][:, :], const_in)
            load(ident[:, :], io["ident"][:, :], const_in)

            def ffn(f):
                u0 = U_FFN[f]
                def four(i):
                    for k in range(4):
                        unit(i * 4 + (u0 + k), (u0 + k) % 2, io["w_ffn_in"][f, i * 4 + k], UW)

                four(0)
                with sp.Fori(1, KF // 2) as i:
                    four(i)
                with sp.Fori(0, KD) as m:
                    for k in range(2):
                        u = u0 + 2 * KF + k
                        unit(m * 2 + u, u % 2, io["w_ffn_out"][f, m, k], UF)

            def ssd():
                unit(U_SSD, U_SSD % 2, io["w_dt"][:, :], UW)
                sp.wait_ge(unit_done, U_SSD)
                for dst, name in ((cst, "conv_state"), (cw, "conv_w"), (dsk, "d_skip"), (ng, "ssm_gain"),
                                  (dtb, "dt_bias"), (alog, "a_log"), (mask, "mask"), (masks, "mask_smp"),
                                  (maskb, "mask_block"), (keep, "keep")):
                    ap = dst[:, :, :, :] if len(dst.shape) == 4 else dst[:, :]
                    src = io[name][:, :, :, :] if len(dst.shape) == 4 else io[name][:, :]
                    load(ap, src, ssd_const)
                for k in range(6):
                    unit(U_GRP + k, (U_GRP + k) % 2, io["w_ssd"][k // 6, k], UW)
                load(h0[:, :, :], io["state"][0], state_in)

                def stores(g):
                    sp.wait_ge(hst_done, g + 1)
                    sp.dma_start(io["ssm_prompt"][g], hst[:, CH - 1, :]).then_inc(st_h, 16)
                    sp.wait_ge(ss_evac, g * 4 + 4)
                    sp.dma_start(io["ssm_sample"][g], h0[:, :, :]).then_inc(st_hs, 16)

                def store_conv(g):
                    sp.wait_ge(nc_ready, g + 1 + 1)
                    sp.dma_start(io["conv_new"][g], ncv[:, :, :, :].rearrange("p t b k -> p (t b k)")).then_inc(st_nc, 16)

                store_conv(0)
                with sp.Fori(0, GROUPS - 1) as g:
                    for k in range(8):
                        u = U_GRP + 6 + k
                        unit(g * 8 + u, u % 2, io["w_ssd"][g + 1, k] if k < 6 else io["w_ssd"][g, k], UW)
                        if k == 6:
                            stores(g)
                    store_conv(g + 1)
                    sp.wait_ge(st_hs, g * 16 + 32)
                    load(h0[:, :, :], io["state"][g + 1], state_in)
                for k in range(2):
                    u = U_GRP + 8 * GROUPS - 2 + k
                    unit(u, u % 2, io["w_ssd"][GROUPS - 1, 6 + k], UW)
                stores(GROUPS - 1)

            def attention():
                sp.wait_ge(unit_done, U_ATT)
                load(d0[:, :, :], io["dist0"][:, :, :], att_const)
                load(d12[:, :, :], io["dist12"][:, :, :], att_const)
                for dst, name in ((dsm, "dist_smp"), (slp, "slopes"), (sls, "slopes_smp")):
                    load(dst[:, :], io[name][:, :], att_const)
                with sp.Fori(0, PAIRS) as c:
                    for k in range(10):
                        u = U_ATT + k
                        unit(c * 10 + u, u % 2, io["w_att"][c, k], UW)
                        if k == 2:
                            sp.wait_ge(spv_mm, c + 1)
                            load(kc[:, :, :], io["k_cache"][c], cache_in)
                            load(vc[:, :, :, :].rearrange("p b k f -> p (b k f)"), io["v_cache"][c], cache_in)
                    sp.wait_ge(q_evac, c * 9 + 9)
                    for g in range(AG):
                        for j in range(2):
                            sp.dma_start(io["kv_new"][c, g * 2 + j], qkv[:, 3 * g + 1 + j, :]).then_inc(st_kv, 16)

            ffn(0)
            if phases > 1:
                ssd()
            if phases > 2:
                ffn(1)
                ffn(2)
            if phases > 3:
                attention()
            if phases > 4:
                ffn(3)
            if phases < 5:
                u = {1: U_SSD, 2: U_FFN1, 3: U_ATT, 4: U_FFN[3]}[phases]
                unit(u, u % 2, io["w_ffn_in"][0, 0], UW)
            for m in range(KD):
                sp.wait_ge(y_ready, m + 1)
                sp.dma_start(io["yT"][:, m, :], x[:, m, :]).then_inc(st_y, 16)
            sp.wait_ge(st_y, 16 * KD)
            if phases > 1:
                sp.wait_ge(st_h, 16 * GROUPS + 16)
                sp.wait_ge(st_hs, 16 * GROUPS + 16)
                sp.wait_ge(st_nc, 16 * GROUPS + 16)
            if phases > 3:
                sp.wait_ge(st_kv, 16 * PAIRS * AG * 2 + 16)

        @block.gpsimd
        def _(pool):
            self_ = Steps(pool, pool_self)

            def low_part(u, parity, width):
                pool.wait_ge(wh_done, u + 1)
                pool.tensor_tensor(wl[:, parity, 0:width], raw[:, parity, 0:width],
                                   wh[:, parity, 0:width].bitcast(F32), ALU.subtract).then_inc(wl_done, 1)

            def ffn(f):
                u0 = U_FFN[f]
                with pool.Fori(0, KF // 2) as i:
                    for k in range(4):
                        low_part(i * 4 + (u0 + k), (u0 + k) % 2, UW)
                with pool.Fori(0, KD) as m:
                    for k in range(2):
                        u = u0 + 2 * KF + k
                        low_part(m * 2 + u, u % 2, UF)

            def ssd():
                low_part(U_SSD, U_SSD % 2, UW)
                pool.wait_ge(ssd_const, 160)
                for t in range(4):
                    pool.memset(xp[:, t, 0:CONV - 1], 0.0)

                def conv_state(g):
                    pool.wait_ge(conv_done, g * 4 + 1)
                    for t in range(4):
                        dst = xp[:, t, XS:XS + NB * SW].rearrange("p (b s) -> p b s", s=SW)[:, :, 0:CONV - 1]
                        src = cst[:, g, t, :].rearrange("p (b s) -> p b s", s=CONV - 1)
                        pool.tensor_copy(dst, src).then_inc(cs_in, 1)

                def new_conv_state(g, low):
                    pool.wait_ge(pj_evac, g * 6 + 4)
                    pool.wait_ge(st_nc, g * 16 + 16)
                    low()
                    for t in range(4):
                        src = xp[:, t, SEQ:SEQ + (NB + 1) * SW].rearrange("p (b s) -> p b s", s=SW)[:, :, 0:CONV - 1]
                        ins = pool.tensor_copy(ncv[:, t, :, :], src)
                    ins.then_inc(nc_ready, 1)

                def part(g, k):
                    u = U_GRP + 6 + k
                    low_part(g * 8 + u, u % 2, UW)

                def group(g, last):
                    if not last:
                        conv_state(g + 1)
                        for k in range(1, 3):
                            part(g, k)
                    pool.wait_ge(dec_ready, g + 1)
                    pool.wait_ge(xc_ready, g * 4 + 4)
                    for j in range(HPG):
                        e = er[:, j * SEQ:(j + 1) * SEQ]
                        pool.tensor_tensor(e, e, xc[:, 3, 0:SEQ], ALU.mult).then_inc(cp_done, 1)
                    if not last:
                        for k in range(3, 5):
                            part(g, k)
                    pool.wait_ge(y_mm, g * 2 + 2)
                    for b in range(NB):
                        hv = h0[:, b, :].rearrange("p (j d) -> p j d", j=HPG)
                        dv = decs[:, :, b:b + 1].broadcast_to([P, HPG, PD])
                        pool.tensor_tensor(hv, hv, dv, ALU.mult).then_inc(hm_done, 1)
                    if not last:
                        new_conv_state(g + 1, lambda: part(g, 5))
                        for k in range(6, 9):
                            part(g, k)
                    else:
                        low_part(U_FFN1 - 1, (U_FFN1 - 1) % 2, UW)

                conv_state(0)
                for k in range(5):
                    low_part(U_GRP + k, (U_GRP + k) % 2, UW)
                new_conv_state(0, lambda: low_part(U_GRP + 5, (U_GRP + 5) % 2, UW))
                low_part(U_GRP + 6, (U_GRP + 6) % 2, UW)
                with pool.Fori(0, GROUPS - 1) as g:
                    group(g, False)
                group(GROUPS - 1, True)

            def attention():
                pool.wait_ge(att_const, 80)
                pool.memset(qz[:, :, :].rearrange("p g r -> p (g r)"), 0.0)
                pool.memset(qa[:, :, :].rearrange("p g r -> p (g r)"), 0.0).then_inc(qz_zero, 1)
                with pool.Fori(0, PAIRS) as c:
                    for k in range(10):
                        u = U_ATT + k
                        low_part(c * 10 + u, u % 2, UW)

            ffn(0)
            if phases > 1:
                ssd()
            if phases > 2:
                ffn(1)
                ffn(2)
            if phases > 3:
                attention()
            if phases > 4:
                ffn(3)

        @block.scalar
        def _(act):
            self_ = Steps(act, act_self)

            def high_part(i, per, u, width):
                act.wait_ge(raw_in[u % 2], i * (8 * per) + 16 * (u // 2 + 1))
                if not isinstance(i, int) or u + per * i >= 2:
                    act.wait_ge(unit_done, i * per + (u - 1))
                nc.scalar.copy(wh[:, u % 2, 0:width], raw[:, u % 2, 0:width]).then_inc(wh_done, 1)

            def stat(n):
                act.wait_ge(var_ready, n + 1)
                nc.scalar.activation(rms[:, :], rms[:, :], ACT.Sqrt).then_inc(sqrt_ready, 1)

            def next_u(n, m):
                act.wait_ge(u_ready, m + 8 * n + 1)
                if n != last_norm:
                    g = gains[:, n, one(m)]
                    if n == 4:
                        dst = uh[:, m, 0:SEQ].rearrange("p (t a) -> p t a", t=DIL)
                        nc.scalar.activation(dst, perm(x[:, m, 0:SEQ]), ACT.Copy, scale=g)
                        nc.scalar.activation(uh[:, m, SEQ:TOK], x[:, m, SEQ:TOK], ACT.Copy, scale=g)
                    else:
                        nc.scalar.activation(uh[:, m, :], x[:, m, :], ACT.Copy, scale=g)
                nc.scalar.activation(sqx[:, :], x[:, m, :], ACT.Square).then_inc(xa_done, 1)

            def ffn(f, next_n):
                u0 = U_FFN[f]

                def pairs(i, first, last):
                    for p in range(2):
                        high_part(i, 4, u0 + 2 * p + 1, UW)
                        if first and p == 0:
                            stat(NORM_OF_FFN[f])
                        high_part(i, 4, u0 + 2 * p + 2, UF if last and p == 1 else UW)
                        act.wait_ge(gate_scaled, i * 2 + (KF * f + p + 1))
                        nc.scalar.activation(gate[:, :], gate[:, :], ACT.Silu).then_inc(silu_done, 1)

                pairs(0, True, False)
                with act.Fori(1, KF // 2 - 1) as i:
                    pairs(i, False, False)
                pairs(KF // 2 - 1, False, True)

                def outs(m, last):
                    u = u0 + 2 * KF
                    high_part(m, 2, u + 1, UF)
                    if not last or f < 3:
                        high_part(m, 2, u + 2, UW if last else UF)
                    act.wait_ge(x_done, m + (8 * f + 2) + 1)
                    next_u(next_n, m)

                with act.Fori(0, KD - 1) as m:
                    outs(m, False)
                outs(KD - 1, True)

            def ssd():
                high_part(0, 8, U_SSD + 1, UW)
                stat(1)
                act.wait_ge(ssd_const, 160)
                nc.scalar.activation(ea[:, :], alog[:, :], ACT.Exp).then_inc(ea_ready, 1)
                act.wait_ge(dt_abs, 1)
                t1, t2 = er[0:HEADS, TOK:2 * TOK], er[0:HEADS, 2 * TOK:3 * TOK]
                nc.scalar.activation(t1, t1, ACT.Exp, scale=-1.0).then_inc(dt_exp, 1)
                act.wait_ge(coef_in, 1)
                nc.scalar.activation(t2, t2, ACT.Exp).then_inc(coef_exp, 1)

                def conv_out(g, k):
                    act.wait_ge(conv_done, g * 4 + (k + 1) + 1)
                    bias = cw[:, one(g * 20 + (k * 5 + 4))]
                    nc.scalar.activation(xc[:, k, 0:SEQ], acc[:, k % 2, 0:SEQ], ACT.Silu, bias=bias)
                    nc.scalar.activation(smp(xc[:, k, SEQ:TOK]), smp(acc[:, k % 2, XS:XW], SW)[:, :, 0:NS],
                                         ACT.Silu, bias=bias).then_inc(xc_ready, 1)

                def gate_out(g, k):
                    act.wait_ge(pj_evac, g * 6 + (k + 5))
                    nc.scalar.activation(zs[:, k, :], zs[:, k, :], ACT.Silu).then_inc(zs_ready, 1)

                def part(g, k):
                    high_part(g, 8, U_GRP + 6 + k, UW)

                def group(g, last):
                    if last:
                        high_part(0, 8, U_FFN1 - 1, UW)
                    else:
                        part(g, 1)
                    act.wait_ge(segs_done, g + 1)
                    nc.scalar.activation(ers[:, :], ps[:, 7, 0:HPG * SMP], ACT.Exp).then_inc(ers_done, 1)
                    s2 = sgs[:, :, :].rearrange("p j q -> p (j q)")
                    nc.scalar.activation(s2, s2, ACT.Exp).then_inc(es_done, 1)
                    for j in range(HPG):
                        if j == 3 and not last:
                            part(g, 2)
                        act.wait_ge(seg_done, g * 4 + (j + 1))
                        nc.scalar.activation(er[:, j * SEQ:(j + 1) * SEQ], ps[:, (4, 5, 6, 4)[j], :],
                                             ACT.Exp).then_inc(er_done, 1)
                        e = sg[:, j * SEQ:(j + 1) * SEQ]
                        nc.scalar.activation(e, e, ACT.Exp).then_inc(e_done, 1)
                    act.wait_ge(t_mm, g * 4 + 3)
                    nc.scalar.copy(bt[:, :], ps[:, 7, :]).then_inc(bt_done, 1)
                    if not last:
                        part(g, 3)
                        part(g, 4)
                    for i in range(2):
                        act.wait_ge(gz_ready, g * 2 + (i + 1))
                        nc.scalar.activation(zs[:, i, :], ysb[:, i, :], ACT.Square).then_inc(gsq_done, 1)
                    if not last:
                        conv_out(g + 1, 0)
                        conv_out(g + 1, 1)
                        part(g, 5)
                        conv_out(g + 1, 2)
                        conv_out(g + 1, 3)
                    act.wait_ge(gvar_ready, g + 1)
                    nc.scalar.activation(gr[:, :], gr[:, :], ACT.Sqrt).then_inc(gsqrt_ready, 1)
                    if not last:
                        part(g, 6)
                    for i in range(2):
                        act.wait_ge(gn_ready, g * 2 + (i + 1))
                        nc.scalar.copy(gh[:, i, :], ysb[:, i, :]).then_inc(gh_done, 1)
                    if not last:
                        gate_out(g + 1, 0)
                        part(g, 7)
                        gate_out(g + 1, 1)
                        part(g, 8)
                    else:
                        high_part(0, 8, U_FFN1, UW)

                for k in range(6):
                    high_part(0, 8, U_GRP + 1 + k, UW)
                    if k < 4:
                        conv_out(0, k)
                    else:
                        gate_out(0, k - 4)
                with act.Fori(0, GROUPS - 1) as g:
                    group(g, False)
                group(GROUPS - 1, True)
                act.wait_ge(so_evac, KD * GROUPS + 1)
                with act.Fori(0, KD) as m:
                    next_u(2, m)

            def attention():
                u0 = U_ATT
                stat(4)
                with act.Fori(0, PAIRS) as c:
                    for k in range(9):
                        high_part(c, 10, u0 + k + 1, UW)
                    for g in range(AG):
                        act.wait_ge(vt_mm, c * 4 + (g + 1))
                        nc.scalar.copy(vt[:, g, :, :].rearrange("p t f -> p (t f)"), ps[:, 4 + g, :]).then_inc(vt_done, 1)
                    act.wait_ge(vt_mm, c * 4 + 4)
                    nc.scalar.copy(vts[:, :, :].rearrange("p g f -> p (g f)"), ps[0:SMP, 7, 0:AG * P]).then_inc(vt_done, 1)

                    def exps(e):
                        act.wait_ge(max_done, c * 8 + (e + 1))
                        nc.scalar.activation(pr[:, e % 2, :], pr[:, e % 2, :], ACT.Exp, bias=nmx[:, e:e + 1],
                                             accum_out=den[:, e:e + 1]).then_inc(exp_done, 1)

                    exps(0)
                    for e in range(8):
                        if e < 7:
                            exps(e + 1)
                        act.wait_ge(pt_mm, c * 8 + (e + 1))
                        if e >= 2:
                            act.wait_ge(pv_mm, c * 8 + (e - 1))
                        nc.scalar.copy(pt[:, e % 2, 0:512], ps[:, 0, :])
                        nc.scalar.copy(pt[:, e % 2, 512:768], ps[:, 1, 0:256]).then_inc(pt_done, 1)
                    act.wait_ge(smax_done, c + 1)
                    nc.scalar.activation(prs[:, :], prs[:, :], ACT.Exp, bias=nmx[:, 8:9],
                                         accum_out=den[:, 8:9]).then_inc(sexp_done, 1)
                    act.wait_ge(spt_mm, c + 1)
                    nc.scalar.copy(pts[:, :, :].rearrange("p k r -> p (k r)"), ps[:, 6, :])
                    nc.scalar.copy(ptn[:, :, :].rearrange("p g r -> p (g r)"), ps[0:SMP, 7, 0:AG * P]).then_inc(spt_done, 1)
                    act.wait_ge(ot_mm, c + 1)
                    nc.scalar.copy(oh[:, 0:SEQ], ps[:, 0, :])
                    act.wait_ge(spv_mm, c + 1 + 1)
                    for j in range(2):
                        r = slice(HD * j, HD * j + HD)
                        ins = nc.scalar.copy(smp(oh[r, SEQ:TOK]), smp(ps[r, 1, 0:P], 2 * NS)[:, :, j * NS:(j + 1) * NS])
                    ins.then_inc(oh_done, 1)
                    high_part(c, 10, u0 + 10, UW)
                act.wait_ge(ao_evac, KD * PAIRS + 1)
                with act.Fori(0, KD) as m:
                    next_u(5, m)

            high_part(0, 4, 0, UW)
            act.wait_ge(x_done, 1 + 1)
            with act.Fori(0, KD) as m:
                next_u(0, m)
            ffn(0, 1)
            if phases > 1:
                ssd()
            if phases > 2:
                ffn(1, 3)
                ffn(2, 4)
            if phases > 3:
                attention()
            if phases > 4:
                ffn(3, 6)
                stat(last_norm)

        @block.tensor
        def _(pe):
            def product(u, parity, nk, rh, rl, banks, split, first=True, last=True, chunk=None):
                pe.wait_ge(wh_done, u + 1)
                for k in range(nk):
                    if chunk is not None:
                        pe.wait_ge(u_ready, chunk + k + 1 + 1)
                    w = wh[:, parity, k * P:(k + 1) * P]
                    for b, (t0, n) in zip(banks, split):
                        pe.matmul(ps[:, b, 0:n], w, rh[:, k, t0:t0 + n], start=first and k == 0, stop=False)
                        pe.matmul(ps[:, b, 0:n], w, rl[:, k, t0:t0 + n], start=False, stop=False)
                pe.wait_ge(wl_done, u + 1)
                for k in range(nk):
                    w = wl[:, parity, k * P:(k + 1) * P]
                    for b, (t0, n) in zip(banks, split):
                        ins = pe.matmul(ps[:, b, 0:n], w, rh[:, k, t0:t0 + n], start=False,
                                        stop=last and k == nk - 1)
                ins.then_inc(unit_done, 1)

            def stat():
                for h, (t0, n) in enumerate(HALVES):
                    ins = pe.matmul(ps[:, 6 + h, 0:n], ones[:, :], ssq[:, t0:t0 + n], start=True, stop=True)
                ins.then_inc(stat_mm, 1)

            def ffn(f):
                u0, n = U_FFN[f], NORM_OF_FFN[f]

                def pairs(i, first):
                    for p in range(2):
                        for k in range(2):
                            if not first and k == 0:
                                pe.wait_ge(h_ready, i * 2 + (KF * f + p - 1) + 1)
                            if first and p == 1 and k == 1:
                                pe.wait_ge(var_ready, n + 1)
                            product(i * 4 + (u0 + 2 * p + k), (u0 + 2 * p + k) % 2, KD, uh, ul,
                                    (4 * p + 2 * k, 4 * p + 2 * k + 1), HALVES,
                                    chunk=8 * n if first and p == 0 and k == 0 else None)
                            if first and p == 0 and k == 0:
                                stat()

                pairs(0, True)
                with pe.Fori(1, KF // 2) as i:
                    pairs(i, False)

                pe.wait_ge(h_ready, KF * (f + 1) + 1)
                with pe.Fori(0, KD // 2) as i:
                    for p in range(2):
                        pe.wait_ge(x_done, i * 2 + (8 * f + p) + 1)
                        for k in range(2):
                            u = u0 + 2 * KF + 2 * p + k
                            r = slice(k * KF // 2, (k + 1) * KF // 2)
                            product(i * 4 + u, u % 2, KF // 2, hh[:, r, :], hl[:, r, :], (2 * p, 2 * p + 1), HALVES,
                                    first=k == 0, last=k == 1)

            def rows(c):
                return slice(c * P, (c + 1) * P)

            def ssd():
                product(U_SSD, U_SSD % 2, KD, uh, ul, (4, 5), HALVES, chunk=8)
                stat()
                pe.wait_ge(dtok_in, 3)
                srcs = (acT[:, :], er[0:HEADS, 0:TOK], er[0:HEADS, 2 * TOK:3 * TOK])
                for q, src in enumerate(srcs):
                    for c in range(CH + 1):
                        n = P if c < CH else SMP
                        col = (q * (CH + 1) + c) * HEADS
                        ins = pe.transpose(ps[0:n, 4, col:col + HEADS], src[:, c * P:c * P + n], ident[0:HEADS, 0:HEADS])
                ins.then_inc(dtok_mm, 1)
                pe.wait_ge(tok_ready, 1)

                def project(g, k, u):
                    if k == 0:
                        pe.wait_ge(so_evac, (g - 1) * 8 + 1 if not isinstance(g, int) else 1)
                    if k >= 2:
                        pe.wait_ge(pj_evac, g * 6 + (k - 1))
                    product(u, (U_GRP + k) % 2, KD, uh, ul, (2 * (k % 2), 2 * (k % 2) + 1), SPLIT)

                def decays(g):
                    pe.wait_ge(acm_ready, g * 4 + 4)
                    for j in range(HPG):
                        ins = pe.matmul(ps[:, 7, j * SMP:(j + 1) * SMP], ones[0:HEADS, :], acm[:, j, SEQ:TOK],
                                        start=True, stop=True)
                    ins.then_inc(rs_mm, 1)
                    for j in range(3):
                        pe.matmul(ps[:, 4 + j, :], ones[0:HEADS, :], acm[:, j, 0:SEQ], start=True, stop=True).then_inc(r_mm, 1)

                def turn(g):
                    pe.wait_ge(er_done, g * 4 + 1)
                    pe.matmul(ps[:, 4, :], ones[0:HEADS, :], acm[:, 3, 0:SEQ], start=True, stop=True).then_inc(r_mm, 1)
                    for i in range(3):
                        pe.wait_ge(xc_ready, g * 4 + (i + 1))
                        if i < 2:
                            pe.wait_ge(er_done, g * 4 + (i + 2))
                        else:
                            pe.wait_ge(ers_done, g + 1)
                            pe.wait_ge(er_done, g * 4 + 4)
                        for c in range(CH):
                            ins = pe.transpose(ps[:, 5 + i, rows(c)], xc[:, i, rows(c)], ident[:, :])
                        ins.then_inc(t_mm, 1)
                    for i in range(3):
                        ins = pe.transpose(ps[0:SMP, 4, rows(i)], xc[:, i, SEQ:TOK], ident[:, :])
                    ins.then_inc(t_mm, 1)

                def chunk_sums(g):
                    pe.wait_ge(xc_ready, g * 4 + 4)
                    pe.wait_ge(xd_done, g * 2 + 1)
                    for c in range(CH):
                        pe.matmul(ps[:, 5, rows(c)], xc[:, 2, rows(c)], xc[:, 3, rows(c)], start=True, stop=True)
                    pe.wait_ge(xs_done, g + 1)
                    pe.matmul(ps[0:SMP, 4, 0:SMP], xc[:, 2, SEQ:TOK], xc[:, 3, SEQ:TOK],
                              start=True, stop=True).then_inc(cb_mm, 1)
                    pe.wait_ge(xd_done, g * 2 + 2)
                    pe.wait_ge(bt_done, g + 1)
                    for c in range(CH):
                        ins = pe.matmul(ps[:, 6 + c // 2, (c % 2) * 256:(c % 2) * 256 + 256], bt[:, rows(c)],
                                        xw[:, c, :, :].rearrange("p j d -> p (j d)"), start=True, stop=True)
                        if c % 2:
                            ins.then_inc(st_mm, 1)

                def outputs(g):
                    pe.wait_ge(w_done, g + 1)
                    pe.wait_ge(cp_done, g * 4 + 4)
                    pe.wait_ge(hst_done, g + 1)
                    pe.wait_ge(state_in, g * 16 + 16)
                    for i in range(2):
                        for c in range(CH):
                            for jj in range(2):
                                j = 2 * i + jj
                                out = ps[PD * jj:PD * jj + PD, 5 + i, rows(c)]
                                pe.matmul(out, xd[:, c, j, :], sg[:, j * SEQ + c * P:j * SEQ + (c + 1) * P],
                                          start=True, stop=c == 0)
                                if c:
                                    pe.matmul(out, hst[:, c - 1, j * PD:(j + 1) * PD],
                                              er[:, j * SEQ + c * P:j * SEQ + (c + 1) * P], start=False, stop=True)
                        for jj in range(2):
                            j = 2 * i + jj
                            pe.matmul(ps[PD * jj:PD * jj + PD, 4, 2 * i * SMP:(2 * i + 1) * SMP], xds[:, j, :],
                                      sgs[:, j, :], start=True, stop=True)
                        for b in range(NB):
                            col = (2 * i + 1) * SMP + b * NS
                            ins = pe.matmul(ps[:, 4, col:col + NS], h0[:, b, i * P:(i + 1) * P],
                                            xc[:, 3, SEQ + b * NS:SEQ + (b + 1) * NS], start=True, stop=True)
                        ins.then_inc(y_mm, 1)

                def states(g):
                    for k, bank in enumerate((7, 5, 6, 7)):
                        if k == 1 or k == 2:
                            pe.wait_ge(y_evac, g * 2 + k)
                        if k == 3:
                            pe.wait_ge(ss_evac, g * 4 + 1)
                        for b in (2 * k, 2 * k + 1):
                            ins = pe.matmul(ps[:, bank, (b % 2) * 256:(b % 2) * 256 + 256], bd[:, b, :],
                                            xws[:, :, :].rearrange("p j d -> p (j d)"), start=True, stop=True)
                        ins.then_inc(ss_mm, 1)
                    pe.wait_ge(gsq_done, g * 2 + 2)
                    pe.wait_ge(ss_evac, g * 4 + 2)
                    for h, (t0, n) in enumerate(HALVES):
                        for i in range(2):
                            ins = pe.matmul(ps[:, 4 + h, 0:n], ones[:, :], zs[:, i, t0:t0 + n], start=i == 0, stop=i == 1)
                    ins.then_inc(gn_mm, 1)

                def project_out(g, u0):
                    pe.wait_ge(g_ready, g * 2 + 2)
                    for m in range(KD):
                        u = u0 + m // 4
                        if m == 0:
                            pe.wait_ge(pj_evac, g * 6 + 12 if not isinstance(g, int) else 6 * GROUPS)
                        elif m == 1:
                            pass
                        else:
                            pe.wait_ge(so_evac, g * 8 + (m - 1) + 1)
                        pe.wait_ge(wh_done, u + 1)
                        pe.wait_ge(wl_done, u + 1)
                        for k in range(2):
                            w = slice(((m % 4) * 2 + k) * P, ((m % 4) * 2 + k + 1) * P)
                            for h, (t0, n) in enumerate(SPLIT):
                                out = ps[:, 2 * (m % 2) + h, 0:n]
                                pe.matmul(out, wh[:, (U_GRP + m // 4) % 2, w], gh[:, k, t0:t0 + n], start=k == 0, stop=False)
                                pe.matmul(out, wh[:, (U_GRP + m // 4) % 2, w], gl[:, k, t0:t0 + n], start=False, stop=False)
                                ins = pe.matmul(out, wl[:, (U_GRP + m // 4) % 2, w], gh[:, k, t0:t0 + n], start=False, stop=k == 1)
                        ins.then_inc(unit_done if m % 4 == 3 else so_mm, 1)

                for k in range(6):
                    project(0, k, U_GRP + k)
                with pe.Fori(0, GROUPS - 1) as g:
                    def ahead(k):
                        project(g + 1, k, g * 8 + (U_GRP + 6 + k))

                    decays(g)
                    ahead(0)
                    turn(g)
                    ahead(1)
                    chunk_sums(g)
                    ahead(2)
                    outputs(g)
                    ahead(3)
                    states(g)
                    ahead(4)
                    ahead(5)
                    project_out(g, g * 8 + (U_GRP + 12))
                g = GROUPS - 1
                for stage in (decays, turn, chunk_sums, outputs, states):
                    stage(g)
                project_out(g, U_FFN1 - 2)

            def attention():
                u0 = U_ATT
                pe.wait_ge(u_ready, 40 + 1)
                stat()
                with pe.Fori(0, PAIRS) as c:
                    pe.wait_ge(ao_evac, c * 8 + 1)
                    for k in range(9):
                        if k >= 2:
                            pe.wait_ge(q_evac, c * 9 + (k - 1))
                        product(c * 10 + (u0 + k), (u0 + k) % 2, KD, uh, ul,
                                (2 * (k % 2), 2 * (k % 2) + 1), SPLIT)
                    for g in range(AG):
                        pe.wait_ge(q_evac, c * 9 + (3 * g + 3))
                        for t in range(CH):
                            ins = pe.transpose(ps[:, 4 + g, rows(t)], qkv[:, 3 * g + 2, rows(t)], ident[:, :])
                        ins.then_inc(vt_mm, 1)
                    for g in range(AG):
                        ins = pe.transpose(ps[0:SMP, 7, rows(g)], qkv[:, 3 * g + 2, SEQ:TOK], ident[:, :])
                    ins.then_inc(vt_mm, 1)
                    pe.wait_ge(vt_done, c * 4 + 4)

                    def scores(e):
                        t, r, bank = e // 2, slice(HD * (e % 2), HD * (e % 2) + HD), 4 + 2 * (e % 2)
                        if e >= 2:
                            pe.wait_ge(max_done, c * 8 + (e - 1))
                        pe.matmul(ps[:, bank, :], qkv[r, 0, rows(t)], qkv[r, 1, 0:SEQ], start=True, stop=True)
                        pe.matmul(ps[:, bank + 1, 0:P], qkv[r, 3, rows(t)], qkv[r, 4, rows(t)], start=True, stop=True)
                        pe.matmul(ps[:, bank + 1, P:2 * P], qkv[r, 6, rows(t)], qkv[r, 7, rows(t)],
                                  start=True, stop=True).then_inc(sc_mm, 1)

                    scores(0)
                    for e in range(8):
                        if e < 7:
                            scores(e + 1)
                        t, r = e // 2, slice(HD * (e % 2), HD * (e % 2) + HD)
                        pe.wait_ge(exp_done, c * 8 + (e + 1))
                        if e >= 1:
                            pe.wait_ge(pt_done, c * 8 + e)
                        else:
                            pe.wait_ge(q_evac, c * 9 + 9)
                        for k in range(6):
                            ins = pe.transpose(ps[:, k // 4, rows(k % 4)], pr[:, e % 2, rows(k)], ident[:, :])
                        ins.then_inc(pt_mm, 1)
                        pe.wait_ge(pt_done, c * 8 + (e + 1))
                        if e >= 2:
                            pe.wait_ge(un_done, c * 8 + (e - 1))
                        for k in range(6):
                            v = vt[:, max(0, k - 3), k if k < 4 else t, r]
                            ins = pe.matmul(ps[:, 2 + e % 2, 0:HD], pt[:, e % 2, rows(k)], v, start=k == 0, stop=k == 5)
                        ins.then_inc(pv_mm, 1)
                        if e == 6:
                            pe.wait_ge(qz_done, c + 1)
                            pe.wait_ge(cache_in, c * 32 + 32)
                            pe.wait_ge(max_done, c * 8 + 7)
                            for b in range(NB):
                                for g, (k0, n) in enumerate(KEYR):
                                    pe.matmul(ps[:, 4, k0:k0 + n], qz[:, g, b * P:(b + 1) * P], kc[:, b, k0:k0 + n],
                                              start=b == 0 and g == 0, stop=b == NB - 1, skip_group_check=True)
                            for g in range(AG):
                                ins = pe.matmul(ps[:, 5, g * SMP:(g + 1) * SMP], qa[:, g, :], qkv[:, 3 * g + 1, SEQ:TOK],
                                                start=True, stop=True)
                            ins.then_inc(ssc_mm, 1)
                    pe.wait_ge(snorm_done, c + 1)
                    pe.wait_ge(max_done, c * 8 + 8)
                    for k in range(4):
                        pe.transpose(ps[:, 6, rows(k)], prs[:, rows(k)], ident[:, :])
                    for g in range(AG):
                        ins = pe.transpose(ps[0:SMP, 7, rows(g)], prs[:, KEYC + g * SMP:KEYC + (g + 1) * SMP], ident[:, :])
                    ins.then_inc(spt_mm, 1)
                    pe.wait_ge(un_done, c * 8 + 8)
                    for t in range(CH):
                        ins = pe.transpose(ps[:, 0, rows(t)], un[:, t, :], ident[:, :])
                    ins.then_inc(ot_mm, 1)
                    pe.wait_ge(spt_done, c + 1)
                    for g in range(AG):
                        pe.matmul(ps[:, 1, 0:P], vts[:, g, :], ptn[:, g, :], start=g == 0, stop=False, skip_group_check=True)
                    for b in range(NB):
                        q = slice(b * 2 * NS, (b + 1) * 2 * NS)
                        for k in range(4):
                            ins = pe.matmul(ps[:, 1, q], vc[:, b, k, :], pts[:, k, q], start=False,
                                            stop=k == 3, skip_group_check=True)
                    ins.then_inc(spv_mm, 1)
                    pe.wait_ge(ol_done, c + 1)
                    u = u0 + 9
                    pe.wait_ge(wh_done, c * 10 + (u + 1))
                    pe.wait_ge(wl_done, c * 10 + (u + 1))
                    for m in range(KD):
                        if m >= 2:
                            pe.wait_ge(ao_evac, c * 8 + (m - 1) + 1)
                        for h, (t0, n) in enumerate(SPLIT):
                            out = ps[:, 2 * (m % 2) + h, 0:n]
                            pe.matmul(out, wh[:, u % 2, rows(m)], oh[:, t0:t0 + n], start=True, stop=False)
                            pe.matmul(out, wh[:, u % 2, rows(m)], ol[:, t0:t0 + n], start=False, stop=False)
                            ins = pe.matmul(out, wl[:, u % 2, rows(m)], oh[:, t0:t0 + n], start=False, stop=True)
                        ins.then_inc(unit_done if m == KD - 1 else ao_mm, 1)

            ffn(0)
            if phases > 1:
                ssd()
            if phases > 2:
                ffn(1)
                ffn(2)
            if phases > 3:
                attention()
            if phases > 4:
                ffn(3)
                pe.wait_ge(u_ready, 56 + 1)
                stat()

        @block.vector
        def _(dve):
            self_ = Steps(dve, dve_self)
            V = nc.vector

            def step(ins):
                self_.done(ins)
                self_.wait()

            def next_u(n, m):
                dve.wait_ge(xa_done, m + (8 * n + 1))
                step(V.tensor_tensor(ssq[:, :], ssq[:, :], sqx[:, :], ALU.add))
                g = gains[:, n, one(m)]
                if n == last_norm:
                    V.tensor_copy(sqx[:, 0:1], ssq[:, 0:1]).then_inc(u_ready, 1)
                elif n == 4:
                    for v in ((lambda a: perm(a[:, m, 0:SEQ]), lambda a: a[:, m, 0:SEQ].rearrange("p (t a) -> p t a", t=DIL)),
                              (lambda a: a[:, m, SEQ:TOK],) * 2):
                        ins = V.scalar_tensor_tensor(v[1](ul), v[0](x), g, v[1](uh).bitcast(F32), ALU.mult, ALU.subtract)
                    ins.then_inc(u_ready, 1)
                else:
                    V.scalar_tensor_tensor(ul[:, m, :], x[:, m, :], g, uh[:, m, :].bitcast(F32),
                                           ALU.mult, ALU.subtract).then_inc(u_ready, 1)

            def stat(n):
                dve.wait_ge(stat_mm, n + 1)
                V.tensor_scalar(two(rms[:, :]), ps[:, 6:8, 0:HALF], 1.0 / D, EPS, ALU.mult, ALU.add).then_inc(var_ready, 1)
                V.memset(ssq[:, :], 0.0)
                dve.wait_ge(sqrt_ready, n + 1)
                V.reciprocal(rms[:, :], rms[:, :]).then_inc(rms_ready, 1)
                dve.wait_ge(rms_ready, n + 1)

            def ffn(f, next_n):
                u0 = U_FFN[f]
                stat(NORM_OF_FFN[f])
                with self_.loop(0, KF // 2, 4) as i:
                    for p in range(2):
                        u = u0 + 2 * p
                        dve.wait_ge(unit_done, i * 4 + (u + 1))
                        dve.wait_ge(h_ready, i * 2 + (KF * f + p) + 1)
                        V.tensor_tensor(two(gate[:, :]), ps[:, 4 * p:4 * p + 2, 0:HALF], two(rms[:, :]),
                                        ALU.mult).then_inc(gate_scaled, 1)
                        dve.wait_ge(unit_done, i * 4 + (u + 2))
                        step(V.tensor_tensor(two(up[:, :]), ps[:, 4 * p + 2:4 * p + 4, 0:HALF], two(rms[:, :]), ALU.mult))
                        dve.wait_ge(silu_done, i * 2 + (KF * f + p + 1))
                        step(V.tensor_tensor(up[:, :], up[:, :], gate[:, :], ALU.mult))
                        j = bass.ds(i * 2 + p, 1)
                        hi = hh[:, j, :].rearrange("p j t -> p (j t)")
                        lo = hl[:, j, :].rearrange("p j t -> p (j t)")
                        V.tensor_copy(hi, up[:, :]).then_inc(h_high, 1)
                        dve.wait_ge(h_high, i * 2 + (KF * f + p + 1))
                        V.tensor_tensor(lo, up[:, :], hi.bitcast(F32), ALU.subtract).then_inc(h_ready, 1)
                with self_.loop(0, KD // 2, 2) as i:
                    for p in range(2):
                        m = i * 2 + p
                        dve.wait_ge(unit_done, i * 4 + (u0 + 2 * KF + 2 * p + 2))
                        xm = x[:, bass.ds(m, 1), :].rearrange("p j (h n) -> p (j h) n", h=2)
                        V.scalar_tensor_tensor(xm, ps[:, 2 * p:2 * p + 2, 0:HALF], 0.5, xm,
                                               ALU.mult, ALU.add).then_inc(x_done, 1)
                        next_u(next_n, m)

            def ssd():
                t0, t1, t2 = (er[0:HEADS, k * TOK:(k + 1) * TOK] for k in range(3))
                t3, t4, t5 = (sg[0:HEADS, k * TOK:(k + 1) * TOK] for k in range(3))
                stat(1)
                dve.wait_ge(ssd_const, 160)
                step(V.tensor_tensor(two(t0), ps[0:HEADS, 4:6, 0:HALF], two(rms[0:HEADS, :]), ALU.mult))
                step(V.tensor_scalar(t0, t0, dtb[:, 0:1], None, ALU.add))
                V.scalar_tensor_tensor(t1, t0, -1.0, t0, ALU.mult, ALU.max).then_inc(dt_abs, 1)
                V.memset(tok[:, :, :, :].rearrange("p q c h -> p (q c h)"), 0.0)
                dve.wait_ge(dt_exp, 1)
                step(V.tensor_scalar(t2, t1, 2.0, None, ALU.add))
                step(V.reciprocal(t2, t2))
                step(V.tensor_tensor(t3, t1, t2, ALU.mult))
                step(V.tensor_tensor(t4, t3, t3, ALU.mult))
                step(V.tensor_scalar(t5, t4, 1.0 / 17, None, ALU.mult))
                for k in range(7, 0, -1):
                    step(V.scalar_tensor_tensor(t5, t5, 1.0 / (2 * k + 1), t4, ALU.add, ALU.mult))
                step(V.scalar_tensor_tensor(t5, t5, 1.0, t3, ALU.add, ALU.mult))
                step(V.tensor_scalar(t0, t0, 0.0, None, ALU.max))
                step(V.scalar_tensor_tensor(t0, t5, 2.0, t0, ALU.mult, ALU.add))
                dve.wait_ge(ea_ready, 1)
                step(V.tensor_scalar(t3, t0, ea[:, 0:1], -1.0, ALU.mult, ALU.mult))
                step(V.tensor_tensor_scan(acT[:, :], keep[:, :], t3, 0.0, ALU.mult, ALU.add))
                for a, b, n in ((0, SEQ, P), (SEQ, TOK, NS)):
                    v, o = smp(acT[:, a:b], n), smp(t2[:, a:b], n)
                    ins = V.tensor_tensor(o, v[:, :, n - 1:n].broadcast_to([HEADS, (b - a) // n, n]), v, ALU.subtract)
                ins.then_inc(coef_in, 1)
                dve.wait_ge(coef_exp, 1)
                step(V.tensor_tensor(t2, t2, t0, ALU.mult))
                V.tensor_copy(dec[0:1, 0, 0:1], t2[0:1, 0:1]).then_inc(dtok_in, 3)
                dve.wait_ge(dtok_mm, 1)
                v = ps[:, 4, 0:3 * (CH + 1) * HEADS].rearrange("p (q c h) -> p q c h", q=3, c=CH + 1)
                V.tensor_copy(tok[:, :, 0:CH, :], v[:, :, 0:CH, :])
                V.tensor_copy(tok[0:SMP, :, CH, :], v[0:SMP, :, CH, :]).then_inc(tok_ready, 1)
                dve.wait_ge(tok_ready, 1)

                def conv_in(g, k, u):
                    dve.wait_ge(unit_done, u + 1)
                    b = 2 * (k % 2)
                    if k == 0:
                        dve.wait_ge(nc_ready, g + 1)
                    V.tensor_tensor(two(xp[:, k, CONV - 1:XS]), ps[:, b:b + 2, 0:QTR], two(rms[:, 0:SEQ]), ALU.mult)
                    V.tensor_tensor(smp(xp[:, k, XS:XW], SW)[:, :, CONV - 1:SW], smp(ps[:, b + 1, QTR:QTR + SMP]),
                                    smp(rms[:, SEQ:TOK]), ALU.mult).then_inc(pj_evac, 1)

                def conv(g, k):
                    dve.wait_ge(pj_evac, g * 6 + (k + 1))
                    dve.wait_ge(cs_in, g * 4 + (k + 1))
                    if k >= 2:
                        dve.wait_ge(xc_ready, g * 4 + (k - 1))
                    w = [cw[:, one(g * 20 + (k * 5 + t))] for t in range(CONV)]
                    step(V.tensor_scalar(acc[:, k % 2, 0:XO], xp[:, k, 0:XO], w[0], None, ALU.mult))
                    for t in range(1, CONV):
                        ins = V.scalar_tensor_tensor(acc[:, k % 2, 0:XO], xp[:, k, t:t + XO], w[t], acc[:, k % 2, 0:XO],
                                                     ALU.mult, ALU.add)
                        if t < CONV - 1:
                            step(ins)
                    ins.then_inc(conv_done, 1)

                def gate_in(g, k, u):
                    dve.wait_ge(unit_done, u + 1)
                    b = 2 * (k % 2)
                    V.tensor_tensor(two(zs[:, k, 0:SEQ]), ps[:, b:b + 2, 0:QTR], two(rms[:, 0:SEQ]), ALU.mult)
                    V.tensor_tensor(zs[:, k, SEQ:TOK], ps[:, b + 1, QTR:QTR + SMP], rms[:, SEQ:TOK],
                                    ALU.mult).then_inc(pj_evac, 1)

                def head_rows(g):
                    step(V.tensor_copy(gtok[:, :, :, :].rearrange("p q c j -> p (q c) j"),
                                       tok[:, :, :, bass.ds(g * HPG, HPG)].rearrange("p q c j -> p (q c) j")))
                    for j in range(HPG):
                        V.tensor_scalar(acm[:, j, :], acT[:, :], ident[0:HEADS, one(g * HPG + j)], None,
                                        ALU.mult).then_inc(acm_ready, 1)

                def seg(g, j):
                    dve.wait_ge(r_mm, g * 4 + (j + 1))
                    for c in range(CH):
                        ins = V.tensor_scalar(sg[:, j * SEQ + c * P:j * SEQ + (c + 1) * P],
                                              ps[:, (4, 5, 6, 4)[j], c * P:(c + 1) * P], gtok[:, 0, c, j:j + 1],
                                              0.0, ALU.subtract, ALU.min)
                    ins.then_inc(seg_done, 1)

                def group(g, last):
                    def ahead(k):
                        u = g * 8 + (U_GRP + 6 + k)
                        if k < 4:
                            conv_in(g + 1, k, u)
                        else:
                            gate_in(g + 1, k - 4, u)

                    dve.wait_ge(rs_mm, g + 1)
                    for j in range(HPG):
                        ins = V.tensor_scalar(sgs[:, j, :], ps[0:SMP, 7, j * SMP:(j + 1) * SMP], gtok[0:SMP, 0, CH, j:j + 1],
                                              0.0, ALU.subtract, ALU.min)
                    ins.then_inc(segs_done, 1)
                    for j in range(3):
                        seg(g, j)
                    if not last:
                        ahead(0)
                    seg(g, 3)
                    if not last:
                        conv(g + 1, 0)
                    dve.wait_ge(er_done, g * 4 + 4)
                    V.tensor_copy(dec[:, :, :], er[:, :].rearrange("p (j c q) -> p j c q", j=HPG, c=CH)[:, :, :, P - 1])
                    dve.wait_ge(ers_done, g + 1)
                    V.tensor_copy(decs[:, :, :], ers[:, :].rearrange("p (j b q) -> p j b q", j=HPG, b=NB)[:, :, :, NS - 1]
                                  ).then_inc(dec_ready, 1)
                    for i in range(2):
                        dve.wait_ge(t_mm, g * 4 + (i + 1))
                        src = ps[:, 5 + i, :].rearrange("p (c d) -> p c d", c=CH)
                        for q, dst in ((1, xd), (2, xw)):
                            for jj in range(2):
                                j = 2 * i + jj
                                ins = V.tensor_tensor(dst[:, :, j, :], src[:, :, jj * PD:(jj + 1) * PD],
                                                      gtok[:, q, 0:CH, j:j + 1].broadcast_to([P, CH, PD]), ALU.mult)
                        ins.then_inc(xd_done, 1)
                    dve.wait_ge(t_mm, g * 4 + 4)
                    for q, dst in ((1, xds), (2, xws)):
                        V.tensor_tensor(dst[:, :, :], ps[0:SMP, 4, 0:2 * P].rearrange("p (j d) -> p j d", j=HPG),
                                        gtok[0:SMP, q, CH, :].unsqueeze(2).broadcast_to([SMP, HPG, PD]), ALU.mult)
                    V.tensor_tensor(bd[:, :, :], ps[0:SMP, 4, 2 * P:3 * P].unsqueeze(1).broadcast_to([SMP, NB, NST]),
                                    maskb[:, :].unsqueeze(2).broadcast_to([SMP, NB, NST]), ALU.mult).then_inc(xs_done, 1)
                    if not last:
                        ahead(1)
                    dve.wait_ge(cb_mm, g + 1)
                    V.tensor_tensor(cbs[:, :], ps[0:SMP, 4, 0:SMP], masks[:, :], ALU.mult)
                    V.tensor_tensor(cbm[:, :].rearrange("p (c q) -> p c q", c=CH), ps[:, 5, :].rearrange("p (c q) -> p c q", c=CH),
                                    mask[:, :].unsqueeze(1).broadcast_to([P, CH, P]), ALU.mult).then_inc(cbm_done, 1)
                    dve.wait_ge(cbm_done, g + 1)
                    for j in range(HPG):
                        dve.wait_ge(e_done, g * 4 + (j + 1))
                        e = sg[:, j * SEQ:(j + 1) * SEQ]
                        V.tensor_tensor(e, e, cbm[:, :], ALU.mult)
                    dve.wait_ge(es_done, g + 1)
                    V.tensor_tensor(sgs[:, :, :], sgs[:, :, :], cbs[:, :].unsqueeze(1).broadcast_to([SMP, HPG, SMP]),
                                    ALU.mult).then_inc(w_done, 1)
                    dve.wait_ge(st_mm, g * 2 + 1)
                    dve.wait_ge(st_h, g * 16 + 16)
                    step(V.tensor_copy(hst[:, 0, :], ps[:, 6, 0:256]))
                    for c in range(1, CH):
                        if c == 2:
                            dve.wait_ge(st_mm, g * 2 + 2)
                        for j in range(HPG):
                            d = slice(j * PD, (j + 1) * PD)
                            ins = V.scalar_tensor_tensor(hst[:, c, d], hst[:, c - 1, d], dec[:, j, c:c + 1],
                                                         ps[:, 6 + c // 2, (c % 2) * 256 + j * PD:(c % 2) * 256 + (j + 1) * PD],
                                                         ALU.mult, ALU.add)
                        if c < CH - 1:
                            step(ins)
                    ins.then_inc(hst_done, 1)
                    if not last:
                        conv(g + 1, 1)
                        ahead(2)
                        head_rows(g + 1)
                    for i in range(2):
                        dve.wait_ge(y_mm, g * 2 + 2)
                        dk = dsk[:, one(g * 2 + i)]
                        for jj in range(2):
                            r = slice(PD * jj, PD * jj + PD)
                            j = 2 * i + jj
                            V.tensor_tensor(yof[r, i, :], ps[r, 4, (2 * i + 1) * SMP:(2 * i + 2) * SMP],
                                            ers[r, j * SMP:(j + 1) * SMP], ALU.mult)
                        V.scalar_tensor_tensor(ysb[:, i, 0:SEQ], xc[:, i, 0:SEQ], dk, ps[:, 5 + i, :], ALU.mult, ALU.add)
                        ins = V.scalar_tensor_tensor(ysb[:, i, SEQ:TOK], xc[:, i, SEQ:TOK], dk,
                                                     ps[:, 4, 2 * i * SMP:(2 * i + 1) * SMP], ALU.mult, ALU.add)
                        ins.then_inc(y_evac, 1)
                        dve.wait_ge(y_evac, g * 2 + (i + 1))
                        step(V.tensor_tensor(ysb[:, i, SEQ:TOK], ysb[:, i, SEQ:TOK], yof[:, i, :], ALU.add))
                        dve.wait_ge(zs_ready, g * 2 + (i + 1))
                        V.tensor_tensor(ysb[:, i, :], ysb[:, i, :], zs[:, i, :], ALU.mult).then_inc(gz_ready, 1)
                    if not last:
                        ahead(3)
                        conv(g + 1, 2)
                    for k, bank in enumerate((7, 5, 6, 7)):
                        dve.wait_ge(ss_mm, g * 4 + (k + 1))
                        dve.wait_ge(hm_done, g * 8 + (2 * k + 2))
                        V.tensor_tensor(h0[:, 2 * k:2 * k + 2, :], h0[:, 2 * k:2 * k + 2, :],
                                        two(ps[:, bank, :]), ALU.add).then_inc(ss_evac, 1)
                    dve.wait_ge(gn_mm, g + 1)
                    V.tensor_scalar(two(gr[:, :]), ps[:, 4:6, 0:HALF], 1.0 / (2 * P), EPS, ALU.mult, ALU.add).then_inc(gvar_ready, 1)
                    if not last:
                        conv(g + 1, 3)
                    dve.wait_ge(gsqrt_ready, g + 1)
                    dve.wait_ge(gz_ready, g * 2 + 2)
                    step(V.reciprocal(gr[:, :], gr[:, :]))
                    for i in range(2):
                        V.scalar_tensor_tensor(ysb[:, i, :], ysb[:, i, :], ng[:, one(g * 2 + i)], gr[:, :],
                                               ALU.mult, ALU.mult).then_inc(gn_ready, 1)
                    if not last:
                        ahead(4)
                    for i in range(2):
                        dve.wait_ge(gn_ready, g * 2 + (i + 1))
                        dve.wait_ge(gh_done, g * 2 + (i + 1))
                        V.tensor_tensor(gl[:, i, :], ysb[:, i, :], gh[:, i, :].bitcast(F32), ALU.subtract).then_inc(g_ready, 1)
                    if not last:
                        ahead(5)
                    for m in range(KD):
                        if m % 4 == 3:
                            dve.wait_ge(unit_done, (U_FFN1 - 1 if last else g * 8 + (U_GRP + 13)) + m // 4)
                        else:
                            dve.wait_ge(so_mm, g * 6 + (m - m // 4 + 1))
                        b = 2 * (m % 2)
                        V.tensor_tensor(two(x[:, m, 0:SEQ]), two(x[:, m, 0:SEQ]), ps[:, b:b + 2, 0:QTR], ALU.add)
                        V.tensor_tensor(x[:, m, SEQ:TOK], x[:, m, SEQ:TOK], ps[:, b + 1, QTR:QTR + SMP],
                                        ALU.add).then_inc(so_evac, 1)

                for k in range(4):
                    conv_in(0, k, U_GRP + k)
                    conv(0, k)
                for k in range(2):
                    gate_in(0, k, U_GRP + 4 + k)
                head_rows(0)
                with self_.loop(0, GROUPS - 1, SSD_DVE_STEPS) as g:
                    group(g, False)
                group(GROUPS - 1, True)
                with self_.loop(0, KD, 1) as m:
                    next_u(2, m)

            def attention():
                stat(4)
                dve.wait_ge(att_const, 80)
                dve.wait_ge(qz_zero, 1)
                V.tensor_copy(rmp[:, 0:SEQ].rearrange("p (t a) -> p t a", t=DIL), perm(rms[:, 0:SEQ]))
                step(V.tensor_copy(rmp[:, SEQ:TOK], rms[:, SEQ:TOK]))
                with self_.loop(0, PAIRS, ATT_DVE_STEPS) as c:
                    dve.wait_ge(st_kv, c * (16 * 2 * AG) + 16)
                    for k in range(9):
                        dve.wait_ge(unit_done, c * 10 + (U_ATT + k + 1))
                        b = 2 * (k % 2)
                        views = ((two(qkv[:, k, 0:SEQ]), ps[:, b:b + 2, 0:QTR], two(rmp[:, 0:SEQ])),
                                 (qkv[:, k, SEQ:TOK], ps[:, b + 1, QTR:QTR + SMP], rmp[:, SEQ:TOK]))
                        for dst, src, r in views:
                            if k % 3 == 0:
                                ins = V.scalar_tensor_tensor(dst, src, HD ** -0.5, r, ALU.mult, ALU.mult)
                            else:
                                ins = V.tensor_tensor(dst, src, r, ALU.mult)
                        ins.then_inc(q_evac, 1)
                    dve.wait_ge(q_evac, c * 9 + 9)
                    for g in range(AG):
                        for j in range(2):
                            r = slice(HD * j, HD * j + HD)
                            src = smp(qkv[r, 3 * g, SEQ:TOK])
                            V.tensor_copy(qz[r, g, :].rearrange("p (b s) -> p b s", b=NB)[:, :, j * NS:(j + 1) * NS], src)
                            ins = V.tensor_copy(smp(qa[r, g, :], 2 * NS)[:, :, j * NS:(j + 1) * NS], src)
                    ins.then_inc(qz_done, 1)

                    def softmax_in(e):
                        t, j, bank = e // 2, e % 2, 4 + 2 * (e % 2)
                        dve.wait_ge(sc_mm, c * 8 + (e + 1))
                        if e >= 2:
                            dve.wait_ge(pt_mm, c * 8 + (e - 1))
                        V.scalar_tensor_tensor(pr[:, j, 0:SEQ], d0[:, t, :], slp[:, bass.ds(c * 2 + j, 1)], ps[:, bank, :],
                                               ALU.mult, ALU.add)
                        for g in (1, 2):
                            o = slice(SEQ + (g - 1) * P, SEQ + g * P)
                            ins = V.scalar_tensor_tensor(pr[:, j, o], d12[:, g - 1, :], slp[:, bass.ds(c * 2 + (AH * g + j), 1)],
                                                         ps[:, bank + 1, (g - 1) * P:g * P], ALU.mult, ALU.add)
                        step(ins)
                        step(V.reduce_max(nmx[:, e:e + 1], pr[:, j, :], AX.X))
                        V.tensor_scalar(nmx[:, e:e + 1], nmx[:, e:e + 1], -1.0, None, ALU.mult).then_inc(max_done, 1)

                    def head_out(e):
                        dve.wait_ge(exp_done, c * 8 + (e + 1))
                        step(V.reciprocal(rcp[:, e:e + 1], den[:, e:e + 1]))
                        dve.wait_ge(pv_mm, c * 8 + (e + 1))
                        V.tensor_scalar(un[:, e // 2, HD * (e % 2):HD * (e % 2) + HD], ps[:, 2 + e % 2, 0:HD],
                                        rcp[:, e:e + 1], None, ALU.mult).then_inc(un_done, 1)

                    softmax_in(0)
                    for e in range(8):
                        if e < 7:
                            softmax_in(e + 1)
                        else:
                            dve.wait_ge(ssc_mm, c + 1)
                            for g, (k0, n) in enumerate(KEYR):
                                V.scalar_tensor_tensor(prs[:, k0:k0 + n], dsm[:, k0:k0 + n], sls[:, bass.ds(c * AG + g, 1)],
                                                       ps[:, 4, k0:k0 + n], ALU.mult, ALU.add)
                                k1 = KEYC + g * SMP
                                ins = V.scalar_tensor_tensor(prs[:, k1:k1 + SMP], dsm[:, k1:k1 + SMP], sls[:, bass.ds(c * AG + g, 1)],
                                                             ps[:, 5, g * SMP:(g + 1) * SMP], ALU.mult, ALU.add)
                            step(ins)
                            step(V.reduce_max(nmx[:, 8:9], prs[:, :], AX.X))
                            V.tensor_scalar(nmx[:, 8:9], nmx[:, 8:9], -1.0, None, ALU.mult).then_inc(smax_done, 1)
                        head_out(e)
                    dve.wait_ge(sexp_done, c + 1)
                    step(V.reciprocal(rcp[:, 8:9], den[:, 8:9]))
                    V.tensor_scalar(prs[:, :], prs[:, :], rcp[:, 8:9], None, ALU.mult).then_inc(snorm_done, 1)
                    dve.wait_ge(oh_done, c + 1)
                    V.tensor_tensor(ol[:, 0:SEQ], ps[:, 0, :], oh[:, 0:SEQ].bitcast(F32), ALU.subtract)
                    for j in range(2):
                        r = slice(HD * j, HD * j + HD)
                        ins = V.tensor_tensor(smp(ol[r, SEQ:TOK]), smp(ps[r, 1, 0:P], 2 * NS)[:, :, j * NS:(j + 1) * NS],
                                              smp(oh[r, SEQ:TOK]).bitcast(F32), ALU.subtract)
                    ins.then_inc(ol_done, 1)
                    for m in range(KD):
                        if m == KD - 1:
                            dve.wait_ge(unit_done, c * 10 + (U_ATT + 10))
                        else:
                            dve.wait_ge(ao_mm, c * 7 + (m + 1))
                        b = 2 * (m % 2)
                        xm = x[:, m, 0:SEQ].rearrange("p (a h t) -> p h t a", h=2, t=2)
                        V.tensor_tensor(xm, xm, ps[:, b:b + 2, 0:QTR].rearrange("p h (t a) -> p h t a", t=2), ALU.add)
                        V.tensor_tensor(x[:, m, SEQ:TOK], x[:, m, SEQ:TOK], ps[:, b + 1, QTR:QTR + SMP],
                                        ALU.add).then_inc(ao_evac, 1)
                with self_.loop(0, KD, 1) as m:
                    next_u(5, m)

            for k, (s, by) in enumerate(((st_hs, 16), (st_nc, 16), (st_h, 16), (st_kv, 16), (spv_mm, 1), (conv_done, 1),
                                         (u_ready, 1), (so_evac, 1), (ao_evac, 1), (x_done, 1), (h_ready, 1), (nc_ready, 1))):
                V.memset(rms[:, k:k + 1], 0.0).then_inc(s, by)
            dve.wait_ge(const_in, 64)
            step(V.memset(ssq[:, :], 0.0))
            V.memset(sqx[:, :], 0.0).then_inc(x_done, 1)
            with self_.loop(0, KD, 1) as m:
                next_u(0, m)
            ffn(0, 1)
            if phases > 1:
                ssd()
            if phases > 2:
                dve.wait_ge(st_h, 16 * GROUPS + 16)
                dve.wait_ge(st_hs, 16 * GROUPS + 16)
                dve.wait_ge(st_nc, 16 * GROUPS + 16)
                ffn(1, 3)
                ffn(2, 4)
            if phases > 3:
                attention()
            if phases > 4:
                dve.wait_ge(st_kv, 16 * PAIRS * AG * 2 + 16)
                ffn(3, 6)
                stat(last_norm)
                for m in range(KD):
                    V.scalar_tensor_tensor(x[:, m, :], x[:, m, :], gains[:, last_norm, m:m + 1], rms[:, :],
                                           ALU.mult, ALU.mult).then_inc(y_ready, 1)
            else:
                self_.wait()
                V.tensor_copy(dec[0:1, 0, 0:1], rms[0:1, 0:1]).then_inc(y_ready, KD)


def constants():
    a = np.arange(P)
    tok = DIL * a[:, None, None]
    keys = (DIL * a[None, :] + np.arange(DIL)[:, None]).reshape(-1)
    f = np.float32
    dist = (DIL * a[:, None, None] + np.arange(DIL)[None, :, None]) - keys[None, None, :]
    dist0 = np.where((dist >= 0) & (dist <= 128), dist, BIG).astype(f)
    d = a[:, None] - a[None, :]
    dist12 = np.stack([np.where(d >= 0, DIL * d, BIG), np.where((d >= 0) & (d % 4 == 0), DIL * d, BIG)], 1).astype(f)
    b, j, q = (v.reshape(-1, 1) for v in np.meshgrid(np.arange(NB), np.arange(2), np.arange(NS), indexing="ij"))
    cols = []
    for g, (win, dil) in enumerate(((128, 1), (512, 4), (2048, 16))):
        i = cached_keys(g)[None, :]
        dd = (128 if g == 0 else 256) + q - i
        cols.append(np.where((dd >= 0) & (dd % dil == 0) & (dd <= win), dd, BIG))
    kb, kq = (v.reshape(1, -1) for v in np.meshgrid(np.arange(NB), np.arange(NS), indexing="ij"))
    for g, dil in enumerate((1, 4, 16)):
        dd = q - kq
        cols.append(np.where((kb == b) & (dd >= 0) & (dd % dil == 0), dd, BIG))
    heads = np.arange(1, AG * AH + 1, dtype=np.float64)
    slopes = (-(2.0 ** (-8.0 * heads / (AG * AH)))).astype(f)
    sls = np.stack([slopes.reshape(AG, AH)[g, 2 * c + j[:, 0]] for c in range(PAIRS) for g in range(AG)], 1)
    s = np.arange(SMP)
    keep = np.ones(TOK, f)
    keep[0:SEQ:P] = 0
    keep[SEQ::NS] = 0
    return {
        "ones": np.ones((P, P), f), "ident": np.eye(P, dtype=f), "mask": np.triu(np.ones((P, P), f)),
        "mask_smp": (np.triu(np.ones((SMP, SMP))) * (s[:, None] // NS == s[None, :] // NS)).astype(f),
        "mask_block": (s[:, None] // NS == np.arange(NB)[None, :]).astype(f),
        "keep": np.tile(keep, (HEADS, 1)), "dist0": dist0, "dist12": dist12,
        "dist_smp": np.concatenate(cols, 1).astype(f), "slopes": np.tile(slopes, (P, 1)), "slopes_smp": sls.astype(f),
    }


def cached_keys(g):
    return np.arange((128, 256, 256)[g]) if g < 2 else np.flatnonzero(np.arange(256) % 16 < NS)


def laid_out(v):
    c = np.ascontiguousarray

    def feature_major(a):
        return a.T.reshape(-1, P, a.shape[0]).transpose(1, 0, 2)

    def per_feature(a):
        return a.reshape(-1, P).T

    def units(w):
        k, n = w.shape[0] // P, w.shape[1] // P
        return w.reshape(k, P, n, P).transpose(2, 1, 0, 3).reshape(n, P, k * P)

    x = np.concatenate([v["x_prompt"][0], v["x_sample"].reshape(SMP, D)])
    gains = np.concatenate([v["norm_w"].reshape(6, D), v["norm_f"][None]])
    w_in = []
    w_out = []
    for i in range(2):
        for j in range(2):
            u = units(v["w_ffn_in"][i, j])
            w_in.append(u.reshape(2, KF, P, UW).transpose(1, 0, 2, 3).reshape(2 * KF, P, UW))
            w_out.append(units(v["w_ffn_out"][i, j]).reshape(KD, P, 2, UF).transpose(0, 2, 1, 3))
    wi = v["ssm_w_in"][0]
    z, xbc, dt = units(wi[:, :DI]), units(wi[:, DI:DI + 4096]), wi[:, DI + 4096:]
    wo = v["ssm_w_out"][0].reshape(GROUPS, 2, P, KD, P).transpose(0, 3, 2, 1, 4)
    wo = wo.reshape(GROUPS, 2, 4, P, 2 * P).transpose(0, 1, 3, 2, 4).reshape(GROUPS, 2, P, UW)
    chunk_of = [[2 * g, 2 * g + 1, 16 + g, 24 + g] for g in range(GROUPS)]
    w_ssd = np.stack([np.concatenate([xbc[chunk_of[g]], z[2 * g:2 * g + 2], wo[g]]) for g in range(GROUPS)])
    dtp = np.zeros((D, P), np.float32)
    dtp[:, :HEADS] = dt
    conv = np.concatenate([v["ssm_conv_w"][0], v["ssm_conv_b"]]).reshape(CONV + 1, 32, P)[:, chunk_of]
    state = v["state_conv"][0].reshape(NB * (CONV - 1), 32, P)[:, chunk_of]
    wq = units(v["attn_w_qkv"][0]).reshape(AG, 3, PAIRS, P, UW).transpose(2, 0, 1, 3, 4).reshape(PAIRS, 9, P, UW)
    w_att = np.concatenate([wq, v["attn_w_o"][0].reshape(PAIRS, 1, P, D)], 1)
    kv = np.concatenate([v[f"cache_kv_g{g}"][0][:, cached_keys(g)] for g in range(AG)], 1)
    kv = kv.reshape(NB, KEYC, 2, PAIRS, P)
    out = {
        "xT": feature_major(x), "gains": per_feature(gains.reshape(-1)).reshape(P, 7, KD),
        "w_ffn_in": np.stack(w_in), "w_ffn_out": np.stack(w_out),
        "w_dt": units(dtp)[0], "w_ssd": w_ssd,
        "conv_w": conv.transpose(3, 1, 2, 0).reshape(P, GROUPS * 4 * (CONV + 1)),
        "conv_state": state.transpose(3, 1, 2, 0),
        "dt_bias": v["ssm_dt_bias"][0][:, None], "a_log": v["ssm_a_log"][0][:, None],
        "d_skip": np.repeat(v["ssm_d"][0].reshape(16, 2), PD, 1).T, "ssm_gain": per_feature(v["ssm_norm_w"][0]),
        "state": v["state_ssm"][0].reshape(NB, GROUPS, HPG * PD, NST).transpose(1, 3, 0, 2),
        "w_att": w_att,
        "k_cache": kv[:, :, 0].transpose(2, 3, 0, 1),
        "v_cache": kv[:, :, 1].reshape(NB, 4, P, PAIRS, P).transpose(3, 2, 0, 1, 4).reshape(PAIRS, P, NB * 4 * P),
    }
    return {k: c(a) for k, a in {**out, **constants()}.items()}


OUTPUTS = {
    "yT": (P, KD, TOK), "conv_new": (GROUPS, P, 4 * (NB + 1) * (CONV - 1)),
    "ssm_prompt": (GROUPS, P, HPG * PD), "ssm_sample": (GROUPS, P, NB, HPG * PD),
    "kv_new": (PAIRS, 2 * AG, P, TOK),
}


def returned(o):
    c = np.ascontiguousarray
    y = o["yT"].transpose(2, 1, 0).reshape(TOK, D)
    conv = o["conv_new"].reshape(GROUPS, P, 4, NB + 1, CONV - 1).transpose(3, 4, 0, 2, 1)
    conv = np.concatenate([conv[:, :, :, 0:2].reshape(NB + 1, 3, -1), conv[:, :, :, 2].reshape(NB + 1, 3, -1),
                           conv[:, :, :, 3].reshape(NB + 1, 3, -1)], 2)
    sp = o["ssm_prompt"].transpose(0, 2, 1).reshape(1, 1, HEADS, PD, NST)
    ss = o["ssm_sample"].transpose(2, 0, 3, 1).reshape(1, NB, HEADS, PD, NST)
    kv = o["kv_new"].reshape(PAIRS, AG, 2, 2, HD, TOK).transpose(1, 5, 2, 0, 3, 4).reshape(AG, TOK, 2, AH, HD)
    prompt = kv[:, :SEQ].reshape(AG, DIL, P, 2, AH, HD).transpose(0, 2, 1, 3, 4, 5).reshape(AG, SEQ, 2, AH, HD)
    sample = kv[:, SEQ:].reshape(AG, NB, NS, 2, AH, HD)
    out = [y[None, :SEQ], y[SEQ:].reshape(NB, NS, D), conv[None, :1], conv[None, 1:], sp, ss]
    for g, n in enumerate((128, SEQ, SEQ)):
        out += [prompt[g, SEQ - n:][None, None], sample[g][None]]
    return tuple(c(a) for a in out)


def kernel(**inputs):
    import concourse.bacc as bacc
    from concourse.bass_utils import run_bass_kernel_spmd

    nc = bacc.Bacc("TRN2", target_bir_lowering=False, num_devices=1)
    arrays = laid_out({k: np.asarray(a) for k, a in inputs.items()})
    io = {k: nc.dram_tensor(k, a.shape, mybir.dt.from_np(a.dtype), kind="ExternalInput").ap() for k, a in arrays.items()}
    for k, shape in OUTPUTS.items():
        io[k] = nc.dram_tensor(k, shape, F32, kind="ExternalOutput").ap()
    step_kernel(nc, io)
    r = run_bass_kernel_spmd(nc, [arrays], core_ids=[0])
    return returned(r.results[0])
```

```python
from contextlib import ExitStack, contextmanager

import numpy as np

import concourse.bass as bass
from concourse import mybir

F32 = mybir.dt.float32
F32R = mybir.dt.float32r
ALU = mybir.AluOpType
ACT = mybir.ActivationFunctionType
AX = mybir.AxisListType

P = 128
D = 1024
KD = D // P
SEQ, NB, NS = 512, 8, 8
SMP = NB * NS
TOK = SEQ + SMP
HALF = TOK // 2
QTR = SEQ // 2
FF = 2816
KF = FF // P
EPS = 1e-6
HEADS, GROUPS, HPG, PD, NST = 32, 8, 4, 64, 128
DI = HEADS * PD
CH = SEQ // P
CONV = 4
XW = CONV - 1 + SEQ + NB * (CONV - 1 + NS)
XO = XW - (CONV - 1)
XS = CONV - 1 + SEQ
SW = CONV - 1 + NS
UW = 8 * P
UF = KF // 2 * P
AG, AH, HD, DIL = 3, 8, 64, 4
PAIRS = AH // 2
KEYC = 512
KEYR = ((0, 128), (128, 256), (384, 128))
BIG = 1e30

FFN_UNITS = 2 * KF + 2 * KD
U_SSD = FFN_UNITS
U_GRP = U_SSD + 1
U_FFN1 = U_SSD + 1 + 8 * GROUPS
U_ATT = U_FFN1 + 2 * FFN_UNITS
U_FFN = (0, U_FFN1, U_FFN1 + FFN_UNITS, U_ATT + 10 * PAIRS)
NORM_OF_FFN = (0, 2, 3, 5)
SSD_DVE_STEPS = 19
ATT_DVE_STEPS = 28
QKV_ORDER = (2, 5, 8, 0, 1, 3, 4, 6, 7)
AHEAD = 3


class Steps:

    def __init__(self, eng, sem):
        self.eng, self.sem, self.base, self.n = eng, sem, 0, 0

    def done(self, ins):
        ins.then_inc(self.sem, 1)
        self.n += 1

    def wait(self):
        self.eng.wait_ge(self.sem, self.base + self.n)

    @contextmanager
    def loop(self, first, last, per):
        start, self.n = self.n, 0
        with self.eng.Fori(first, last) as i:
            self.base = (i - first) * per + start
            yield i
        assert self.n == per, f"{self.n} signals in a turn, not {per}"
        self.base, self.n = 0, start + (last - first) * per


def step_kernel(nc, io, phases=7):
    with ExitStack() as ctx:
        def sb(name, shape, dt=F32):
            return ctx.enter_context(nc.sbuf_tensor("sb_" + name, shape, dt))

        def sem(name):
            return ctx.enter_context(nc.semaphore(name))

        x = sb("x", [P, KD, TOK])
        uh = sb("uh", [P, KD, TOK], F32R)
        ul = sb("ul", [P, KD, TOK], F32R)
        raw = sb("raw", [P, 2, UF])
        wh = sb("wh", [P, 2, UF], F32R)
        wl = sb("wl", [P, 2, UF], F32R)
        rms = sb("rms", [P, TOK])
        ssq = sb("ssq", [P, TOK])
        sqx = sb("sqx", [P, TOK])
        ones = sb("ones", [P, P])
        ident = sb("ident", [P, P])
        gains = sb("gains", [P, 7, KD])
        ps = ctx.enter_context(nc.psum_tensor("ps", [P, 8, 512], F32))

        with ExitStack() as region:
            def at(name, shape, dt=F32):
                return region.enter_context(nc.sbuf_tensor("sb_" + name, shape, dt))
            hh = at("hh", [P, KF, TOK], F32R)
            hl = at("hl", [P, KF, TOK], F32R)
            gate = at("gate", [P, TOK])
            up = at("up", [P, TOK])
        with ExitStack() as region:
            xp = at("xp", [P, 4, SEQ + (NB + 1) * SW + 1])
            acc = at("acc", [P, 2, XW + 1])
            xc = at("xc", [P, 4, TOK])
            zs = at("zs", [P, 2, TOK])
            er = at("er", [P, HPG * SEQ])
            ers = at("ers", [P, HPG * SMP])
            sg = at("sg", [P, HPG * SEQ])
            sgs = at("sgs", [SMP, HPG, SMP])
            xd = at("xd", [P, CH, HPG, PD])
            xds = at("xds", [SMP, HPG, PD])
            xw = at("xw", [P, CH, HPG, PD])
            xws = at("xws", [SMP, HPG, PD])
            bt = at("bt", [P, SEQ])
            bd = at("bd", [SMP, NB, NST])
            cbm = at("cbm", [P, SEQ])
            cbs = at("cbs", [SMP, SMP])
            hst = at("hst", [P, CH, HPG * PD])
            h0 = at("h0", [P, NB, HPG * PD])
            ysb = at("ysb", [P, 2, TOK])
            yof = at("yof", [P, 2, SMP])
            gh = at("gh", [P, 2, TOK], F32R)
            gl = at("gl", [P, 2, TOK], F32R)
            gr = at("gr", [P, TOK])
            keep = gr[0:HEADS, :]
            acT = at("acT", [HEADS, TOK])
            acm = at("acm", [HEADS, HPG, TOK])
            tok = at("tok", [P, 3, CH + 1, HEADS])
            gtok = at("gtok", [P, 3, CH + 1, HPG])
            dec = at("dec", [P, HPG, CH])
            decs = at("decs", [P, HPG, NB])
            ncv = at("ncv", [P, 4, NB + 1, CONV - 1])
            cst = at("cst", [P, GROUPS, 4, NB * (CONV - 1)])
            cw = at("cw", [P, GROUPS * 4 * (CONV + 1)])
            dsk = at("dsk", [P, GROUPS * 2])
            ng = at("ng", [P, GROUPS * 2])
            dtb = at("dtb", [HEADS, 1])
            alog = at("alog", [HEADS, 1])
            ea = at("ea", [HEADS, 1])
            mask = at("mask", [P, P])
            masks = at("masks", [SMP, SMP])
            maskb = at("maskb", [SMP, NB])
        with ExitStack() as region:
            qkv = at("qkv", [P, 9, TOK])
            vt = at("vt", [P, AG, CH, P])
            vts = at("vts", [SMP, AG, P])
            pr = at("pr", [P, 2, 768])
            pt = at("pt", [P, 2, 768])
            un = at("un", [P, CH, P])
            oh = at("oh", [P, TOK], F32R)
            ol = at("ol", [P, TOK], F32R)
            kc = at("kc", [P, NB, KEYC])
            vc = at("vc", [P, NB, 4, P])
            qa = at("qa", [P, AG, P])
            stage = at("stage", [P, AHEAD, TOK])
            prs = at("prs", [P, KEYC + AG * SMP])
            pts = at("pts", [P, 4, P])
            ptn = at("ptn", [SMP, AG, P])
            d0 = at("d0", [P, CH, SEQ])
            d12 = at("d12", [P, 2, P])
            dsm = at("dsm", [P, KEYC + AG * SMP])
            slp = at("slp", [P, AG * AH])
            sls = at("sls", [P, AG * PAIRS])
            nmx = at("nmx", [P, 16])
            den = at("den", [P, 16])
            rcp = at("rcp", [P, 16])
            rmp = sqx

        const_in = sem("const_in")
        raw_in = [sem("raw_in0"), sem("raw_in1")]
        wh_done, wl_done, unit_done = sem("wh_done"), sem("wl_done"), sem("unit_done")
        x_done = sem("x_done")
        xa_done = sem("xa_done")
        u_ready = sem("u_ready")
        stat_mm, var_ready, sqrt_ready = sem("stat_mm"), sem("var_ready"), sem("sqrt_ready")
        rms_ready = sem("rms_ready")
        gate_scaled, silu_done, h_high, h_ready = sem("gate_scaled"), sem("silu_done"), sem("h_high"), sem("h_ready")
        act_self, dve_self, pool_self = sem("act_self"), sem("dve_self"), sem("pool_self")
        ssd_const, att_const = sem("ssd_const"), sem("att_const")
        dt_scaled, dt_abs, dt_exp, ea_ready = sem("dt_scaled"), sem("dt_abs"), sem("dt_exp"), sem("ea_ready")
        coef_in, coef_exp, dtok_in, dtok_mm = sem("coef_in"), sem("coef_exp"), sem("dtok_in"), sem("dtok_mm")
        tok_ready = sem("tok_ready")
        state_in, cs_in, pj_evac, nc_ready = sem("state_in"), sem("cs_in"), sem("pj_evac"), sem("nc_ready")
        conv_done, xc_ready, zs_ready = sem("conv_done"), sem("xc_ready"), sem("zs_ready")
        acm_ready, rs_mm, r_mm = sem("acm_ready"), sem("rs_mm"), sem("r_mm")
        er_done, seg_done, ers_done, segs_done = sem("er_done"), sem("seg_done"), sem("ers_done"), sem("segs_done")
        e_done, es_done, dec_ready, cp_done = sem("e_done"), sem("es_done"), sem("dec_ready"), sem("cp_done")
        t_mm, xd_done, xs_done, bt_done = sem("t_mm"), sem("xd_done"), sem("xs_done"), sem("bt_done")
        cb_mm, cbm_done, w_done = sem("cb_mm"), sem("cbm_done"), sem("w_done")
        st_mm, hst_done, y_mm, y_evac = sem("st_mm"), sem("hst_done"), sem("y_mm"), sem("y_evac")
        hm_done, ss_mm, ss_evac = sem("hm_done"), sem("ss_mm"), sem("ss_evac")
        gsq_done, gn_mm, gvar_ready, gsqrt_ready = sem("gsq_done"), sem("gn_mm"), sem("gvar_ready"), sem("gsqrt_ready")
        gz_ready = sem("gz_ready")
        gn_ready, gh_done, g_ready = sem("gn_ready"), sem("gh_done"), sem("g_ready")
        so_mm, so_evac = sem("so_mm"), sem("so_evac")
        st_h, st_hs, st_nc = sem("st_h"), sem("st_hs"), sem("st_nc")
        q_evac, vt_mm, vt_done = sem("q_evac"), sem("vt_mm"), sem("vt_done")
        qk_ready, sc_mm, max_done, exp_done = sem("qk_ready"), sem("sc_mm"), sem("max_done"), sem("exp_done")
        pt_mm, pt_done, pv_mm, un_done = sem("pt_mm"), sem("pt_done"), sem("pv_mm"), sem("un_done")
        ssc_mm, smax_done, sexp_done, snorm_done = sem("ssc_mm"), sem("smax_done"), sem("sexp_done"), sem("snorm_done")
        spt_mm, spt_done, spv_mm = sem("spt_mm"), sem("spt_done"), sem("spv_mm")
        ot_mm, oh_done, ol_done = sem("ot_mm"), sem("oh_done"), sem("ol_done")
        ao_mm, ao_evac, qa_zero = sem("ao_mm"), sem("ao_evac"), sem("qa_zero")
        st_v, st_k, kc_in, vc_in = sem("st_v"), sem("st_k"), sem("kc_in"), sem("vc_in")
        sst_mm, sst_done, soh_done, sol_done = sem("sst_mm"), sem("sst_done"), sem("soh_done"), sem("sol_done")
        y_ready, st_y = sem("y_ready"), sem("st_y")

        HALVES = ((0, HALF), (HALF, HALF))
        SPLIT = ((0, QTR), (QTR, TOK - QTR))
        last_norm = 6

        def one(i):
            return slice(i, i + 1) if isinstance(i, int) else bass.ds(i, 1)

        def smp(ap, q=NS):
            return ap.rearrange("p (b q) -> p b q", q=q)

        def two(ap):
            return ap.rearrange("p (h n) -> p h n", h=2)

        def perm(ap):
            return ap.rearrange("p (a t) -> p t a", t=DIL)

        def rows(c):
            return slice(c * P, (c + 1) * P)

        block = ctx.enter_context(nc.Block())

        @block.sync
        def _(sp):
            def unit(u, parity, src, width):
                if not (isinstance(u, int) and u < 2):
                    sp.wait_ge(wl_done, u - 1)
                sp.dma_start(raw[:, parity, 0:width], src).then_inc(raw_in[parity], 16)

            def load(dst, src, signal):
                sp.dma_start(dst, src).then_inc(signal, 16)

            load(x[:, :, :], io["xT"][:, :, :], const_in)
            load(gains[:, :, :], io["gains"][:, :, :], const_in)
            load(ones[:, :], io["ones"][:, :], const_in)
            load(ident[:, :], io["ident"][:, :], const_in)

            def ffn(f):
                u0 = U_FFN[f]
                def four(i):
                    for k in range(4):
                        unit(i * 4 + (u0 + k), (u0 + k) % 2, io["w_ffn_in"][f, i * 4 + k], UW)

                four(0)
                with sp.Fori(1, KF // 2) as i:
                    four(i)
                with sp.Fori(0, KD) as m:
                    for k in range(2):
                        u = u0 + 2 * KF + k
                        unit(m * 2 + u, u % 2, io["w_ffn_out"][f, m, k], UF)

            def ssd():
                unit(U_SSD, U_SSD % 2, io["w_dt"][:, :], UW)
                sp.wait_ge(unit_done, U_SSD)
                for dst, name in ((cst, "conv_state"), (cw, "conv_w"), (dsk, "d_skip"), (ng, "ssm_gain"),
                                  (dtb, "dt_bias"), (alog, "a_log"), (mask, "mask"), (masks, "mask_smp"),
                                  (maskb, "mask_block"), (keep, "keep")):
                    ap = dst[:, :, :, :] if len(dst.shape) == 4 else dst[:, :]
                    src = io[name][:, :, :, :] if len(dst.shape) == 4 else io[name][:, :]
                    load(ap, src, ssd_const)
                for k in range(6):
                    unit(U_GRP + k, (U_GRP + k) % 2, io["w_ssd"][k // 6, k], UW)
                load(h0[:, :, :], io["state"][0], state_in)

                def stores(g):
                    sp.wait_ge(hst_done, g + 1)
                    sp.dma_start(io["ssm_prompt"][g], hst[:, CH - 1, :]).then_inc(st_h, 16)
                    sp.wait_ge(ss_evac, g * 4 + 4)
                    sp.dma_start(io["ssm_sample"][g], h0[:, :, :]).then_inc(st_hs, 16)

                def store_conv(g):
                    sp.wait_ge(nc_ready, g + 1 + 1)
                    sp.dma_start(io["conv_new"][g], ncv[:, :, :, :].rearrange("p t b k -> p (t b k)")).then_inc(st_nc, 16)

                store_conv(0)
                with sp.Fori(0, GROUPS - 1) as g:
                    for k in range(8):
                        u = U_GRP + 6 + k
                        unit(g * 8 + u, u % 2, io["w_ssd"][g + 1, k] if k < 6 else io["w_ssd"][g, k], UW)
                        if k == 6:
                            stores(g)
                    store_conv(g + 1)
                    sp.wait_ge(st_hs, g * 16 + 32)
                    load(h0[:, :, :], io["state"][g + 1], state_in)
                for k in range(2):
                    u = U_GRP + 8 * GROUPS - 2 + k
                    unit(u, u % 2, io["w_ssd"][GROUPS - 1, 6 + k], UW)
                stores(GROUPS - 1)

            def attention():
                def load_k(c, i):
                    load(kc[:, 2 * i:2 * i + 2, :], io["k_cache"][c, :, 2 * i:2 * i + 2, :], kc_in)

                def load_v(c, i):
                    load(vc[:, 4 * i:4 * i + 4, :, :].rearrange("p b k f -> p (b k f)"),
                         io["v_cache"][c, :, i * NB * KEYC // 2:(i + 1) * NB * KEYC // 2], vc_in)

                def store_v(c):
                    for g in range(AG):
                        sp.dma_start(io["kv_new"][c, g * 2 + 1], qkv[:, 3 * g + 2, :]).then_inc(st_v, 16)

                def store_k(c):
                    sp.wait_ge(qk_ready, c + 1)
                    for g in range(AG):
                        sp.dma_start(io["kv_new"][c, g * 2], qkv[:, 3 * g + 1, :]).then_inc(st_k, 16)

                for k in range(2):
                    unit(U_ATT + k, (U_ATT + k) % 2, io["w_att"][0, k], UW)
                sp.wait_ge(unit_done, U_ATT)
                for dst, name in ((slp, "slopes"), (sls, "slopes_smp"), (dsm, "dist_smp")):
                    load(dst[:, :], io[name][:, :], att_const)
                load(d12[:, :, :], io["dist12"][:, :, :], att_const)
                load(d0[:, :, :], io["dist0"][:, :, :], att_const)
                for k in range(2, 9):
                    unit(U_ATT + k, (U_ATT + k) % 2, io["w_att"][0, k], UW)
                    if k < 6:
                        load_k(0, k - 2)
                    elif k < 8:
                        load_v(0, k - 6)
                sp.wait_ge(q_evac, 3)
                store_v(0)
                with sp.Fori(0, PAIRS - 1) as c:
                    for k in range(10):
                        u = U_ATT + 9 + k
                        unit(c * 10 + u, u % 2, io["w_att"][c + 1, k] if k < 9 else io["w_att"][c, k], UW)
                        if k == 1:
                            store_k(c)
                        if k == 2:
                            sp.wait_ge(sst_mm, c + 1)
                        if 2 <= k < 6:
                            load_k(c + 1, k - 2)
                        if k == 6:
                            sp.wait_ge(q_evac, c * 9 + 12)
                            store_v(c + 1)
                        if k == 8:
                            sp.wait_ge(spv_mm, c + 1)
                            load_v(c + 1, 0)
                        if k == 9:
                            load_v(c + 1, 1)
                u = U_FFN[3] - 1
                unit(u, u % 2, io["w_att"][PAIRS - 1, 9], UW)
                store_k(PAIRS - 1)

            ffn(0)
            if phases > 1:
                ssd()
            if phases > 2:
                ffn(1)
                ffn(2)
            if phases > 3:
                attention()
            if phases > 4:
                ffn(3)
            if phases < 5:
                u = {1: U_SSD, 2: U_FFN1, 3: U_ATT, 4: U_FFN[3]}[phases]
                unit(u, u % 2, io["w_ffn_in"][0, 0], UW)
            for m in range(KD):
                sp.wait_ge(y_ready, m + 1)
                sp.dma_start(io["yT"][:, m, :], x[:, m, :]).then_inc(st_y, 16)
            sp.wait_ge(st_y, 16 * KD)
            if phases > 1:
                sp.wait_ge(st_h, 16 * GROUPS + 16)
                sp.wait_ge(st_hs, 16 * GROUPS + 16)
                sp.wait_ge(st_nc, 16 * GROUPS + 16)
            if phases > 3:
                sp.wait_ge(st_v, 16 * PAIRS * AG)
                sp.wait_ge(st_k, 16 * PAIRS * AG)

        @block.gpsimd
        def _(pool):
            self_ = Steps(pool, pool_self)

            def low_part(u, parity, width):
                pool.wait_ge(wh_done, u + 1)
                pool.tensor_tensor(wl[:, parity, 0:width], raw[:, parity, 0:width],
                                   wh[:, parity, 0:width].bitcast(F32), ALU.subtract).then_inc(wl_done, 1)

            def ffn(f):
                u0 = U_FFN[f]
                with pool.Fori(0, KF // 2) as i:
                    for k in range(4):
                        low_part(i * 4 + (u0 + k), (u0 + k) % 2, UW)
                with pool.Fori(0, KD) as m:
                    for k in range(2):
                        u = u0 + 2 * KF + k
                        low_part(m * 2 + u, u % 2, UF)

            def ssd():
                low_part(U_SSD, U_SSD % 2, UW)
                pool.wait_ge(ssd_const, 160)
                for t in range(4):
                    pool.memset(xp[:, t, 0:CONV - 1], 0.0)

                def conv_state(g):
                    pool.wait_ge(conv_done, g * 4 + 1)
                    for t in range(4):
                        dst = xp[:, t, XS:XS + NB * SW].rearrange("p (b s) -> p b s", s=SW)[:, :, 0:CONV - 1]
                        src = cst[:, g, t, :].rearrange("p (b s) -> p b s", s=CONV - 1)
                        pool.tensor_copy(dst, src).then_inc(cs_in, 1)

                def new_conv_state(g, low):
                    pool.wait_ge(pj_evac, g * 6 + 4)
                    pool.wait_ge(st_nc, g * 16 + 16)
                    low()
                    for t in range(4):
                        src = xp[:, t, SEQ:SEQ + (NB + 1) * SW].rearrange("p (b s) -> p b s", s=SW)[:, :, 0:CONV - 1]
                        ins = pool.tensor_copy(ncv[:, t, :, :], src)
                    ins.then_inc(nc_ready, 1)

                def part(g, k):
                    u = U_GRP + 6 + k
                    low_part(g * 8 + u, u % 2, UW)

                def group(g, last):
                    if not last:
                        conv_state(g + 1)
                        for k in range(1, 3):
                            part(g, k)
                    pool.wait_ge(dec_ready, g + 1)
                    pool.wait_ge(xc_ready, g * 4 + 4)
                    for j in range(HPG):
                        e = er[:, j * SEQ:(j + 1) * SEQ]
                        pool.tensor_tensor(e, e, xc[:, 3, 0:SEQ], ALU.mult).then_inc(cp_done, 1)
                    if not last:
                        for k in range(3, 5):
                            part(g, k)
                    pool.wait_ge(y_mm, g * 2 + 2)
                    for b in range(NB):
                        hv = h0[:, b, :].rearrange("p (j d) -> p j d", j=HPG)
                        dv = decs[:, :, b:b + 1].broadcast_to([P, HPG, PD])
                        pool.tensor_tensor(hv, hv, dv, ALU.mult).then_inc(hm_done, 1)
                    if not last:
                        new_conv_state(g + 1, lambda: part(g, 5))
                        for k in range(6, 9):
                            part(g, k)
                    else:
                        low_part(U_FFN1 - 1, (U_FFN1 - 1) % 2, UW)

                conv_state(0)
                for k in range(5):
                    low_part(U_GRP + k, (U_GRP + k) % 2, UW)
                new_conv_state(0, lambda: low_part(U_GRP + 5, (U_GRP + 5) % 2, UW))
                low_part(U_GRP + 6, (U_GRP + 6) % 2, UW)
                with pool.Fori(0, GROUPS - 1) as g:
                    group(g, False)
                group(GROUPS - 1, True)

            def attention():
                for k in range(9):
                    low_part(U_ATT + k, (U_ATT + k) % 2, UW)
                    if k == 1:
                        pool.wait_ge(att_const, 80)
                        pool.memset(qa[:, :, :].rearrange("p g r -> p (g r)"), 0.0).then_inc(qa_zero, 1)
                with pool.Fori(0, PAIRS - 1) as c:
                    for k in range(10):
                        u = U_ATT + 9 + k
                        low_part(c * 10 + u, u % 2, UW)
                low_part(U_FFN[3] - 1, (U_FFN[3] - 1) % 2, UW)

            ffn(0)
            if phases > 1:
                ssd()
            if phases > 2:
                ffn(1)
                ffn(2)
            if phases > 3:
                attention()
            if phases > 4:
                ffn(3)

        @block.scalar
        def _(act):
            self_ = Steps(act, act_self)

            def high_part(i, per, u, width):
                act.wait_ge(raw_in[u % 2], i * (8 * per) + 16 * (u // 2 + 1))
                if not isinstance(i, int) or u + per * i >= 2:
                    act.wait_ge(unit_done, i * per + (u - 1))
                nc.scalar.copy(wh[:, u % 2, 0:width], raw[:, u % 2, 0:width]).then_inc(wh_done, 1)

            def stat(n):
                act.wait_ge(var_ready, n + 1)
                nc.scalar.activation(rms[:, :], rms[:, :], ACT.Sqrt).then_inc(sqrt_ready, 1)

            def next_u(n, m):
                act.wait_ge(u_ready, m + 8 * n + 1)
                if n != last_norm:
                    g = gains[:, n, one(m)]
                    if n == 4:
                        dst = uh[:, m, 0:SEQ].rearrange("p (t a) -> p t a", t=DIL)
                        nc.scalar.activation(dst, perm(x[:, m, 0:SEQ]), ACT.Copy, scale=g)
                        nc.scalar.activation(uh[:, m, SEQ:TOK], x[:, m, SEQ:TOK], ACT.Copy, scale=g)
                    else:
                        nc.scalar.activation(uh[:, m, :], x[:, m, :], ACT.Copy, scale=g)
                nc.scalar.activation(sqx[:, :], x[:, m, :], ACT.Square).then_inc(xa_done, 1)

            def ffn(f, next_n):
                u0 = U_FFN[f]

                def pairs(i, first, last):
                    for p in range(2):
                        high_part(i, 4, u0 + 2 * p + 1, UW)
                        if first and p == 0:
                            stat(NORM_OF_FFN[f])
                        high_part(i, 4, u0 + 2 * p + 2, UF if last and p == 1 else UW)
                        act.wait_ge(gate_scaled, i * 2 + (KF * f + p + 1))
                        nc.scalar.activation(gate[:, :], gate[:, :], ACT.Silu).then_inc(silu_done, 1)

                pairs(0, True, False)
                with act.Fori(1, KF // 2 - 1) as i:
                    pairs(i, False, False)
                pairs(KF // 2 - 1, False, True)

                def outs(m, last):
                    u = u0 + 2 * KF
                    high_part(m, 2, u + 1, UF)
                    if not last or f < 3:
                        high_part(m, 2, u + 2, UW if last else UF)
                    act.wait_ge(x_done, m + (8 * f + 2) + 1)
                    next_u(next_n, m)

                with act.Fori(0, KD - 1) as m:
                    outs(m, False)
                outs(KD - 1, True)

            def ssd():
                high_part(0, 8, U_SSD + 1, UW)
                stat(1)
                act.wait_ge(ssd_const, 160)
                nc.scalar.activation(ea[:, :], alog[:, :], ACT.Exp).then_inc(ea_ready, 1)
                act.wait_ge(dt_abs, 1)
                t1, t2 = er[0:HEADS, TOK:2 * TOK], er[0:HEADS, 2 * TOK:3 * TOK]
                nc.scalar.activation(t1, t1, ACT.Exp, scale=-1.0).then_inc(dt_exp, 1)
                act.wait_ge(coef_in, 1)
                nc.scalar.activation(t2, t2, ACT.Exp).then_inc(coef_exp, 1)

                def conv_out(g, k):
                    act.wait_ge(conv_done, g * 4 + (k + 1) + 1)
                    bias = cw[:, one(g * 20 + (k * 5 + 4))]
                    nc.scalar.activation(xc[:, k, 0:SEQ], acc[:, k % 2, 0:SEQ], ACT.Silu, bias=bias)
                    nc.scalar.activation(smp(xc[:, k, SEQ:TOK]), smp(acc[:, k % 2, XS:XW], SW)[:, :, 0:NS],
                                         ACT.Silu, bias=bias).then_inc(xc_ready, 1)

                def gate_out(g, k):
                    act.wait_ge(pj_evac, g * 6 + (k + 5))
                    nc.scalar.activation(zs[:, k, :], zs[:, k, :], ACT.Silu).then_inc(zs_ready, 1)

                def part(g, k):
                    high_part(g, 8, U_GRP + 6 + k, UW)

                def group(g, last):
                    if last:
                        high_part(0, 8, U_FFN1 - 1, UW)
                    else:
                        part(g, 1)
                    act.wait_ge(segs_done, g + 1)
                    nc.scalar.activation(ers[:, :], ps[:, 7, 0:HPG * SMP], ACT.Exp).then_inc(ers_done, 1)
                    s2 = sgs[:, :, :].rearrange("p j q -> p (j q)")
                    nc.scalar.activation(s2, s2, ACT.Exp).then_inc(es_done, 1)
                    for j in range(HPG):
                        if j == 3 and not last:
                            part(g, 2)
                        act.wait_ge(seg_done, g * 4 + (j + 1))
                        nc.scalar.activation(er[:, j * SEQ:(j + 1) * SEQ], ps[:, (4, 5, 6, 4)[j], :],
                                             ACT.Exp).then_inc(er_done, 1)
                        e = sg[:, j * SEQ:(j + 1) * SEQ]
                        nc.scalar.activation(e, e, ACT.Exp).then_inc(e_done, 1)
                    act.wait_ge(t_mm, g * 4 + 3)
                    nc.scalar.copy(bt[:, :], ps[:, 7, :]).then_inc(bt_done, 1)
                    if not last:
                        part(g, 3)
                        part(g, 4)
                    for i in range(2):
                        act.wait_ge(gz_ready, g * 2 + (i + 1))
                        nc.scalar.activation(zs[:, i, :], ysb[:, i, :], ACT.Square).then_inc(gsq_done, 1)
                    if not last:
                        conv_out(g + 1, 0)
                        conv_out(g + 1, 1)
                        part(g, 5)
                        conv_out(g + 1, 2)
                        conv_out(g + 1, 3)
                    act.wait_ge(gvar_ready, g + 1)
                    nc.scalar.activation(gr[:, :], gr[:, :], ACT.Sqrt).then_inc(gsqrt_ready, 1)
                    if not last:
                        part(g, 6)
                    for i in range(2):
                        act.wait_ge(gn_ready, g * 2 + (i + 1))
                        nc.scalar.copy(gh[:, i, :], ysb[:, i, :]).then_inc(gh_done, 1)
                    if not last:
                        gate_out(g + 1, 0)
                        part(g, 7)
                        gate_out(g + 1, 1)
                        part(g, 8)
                    else:
                        high_part(0, 8, U_FFN1, UW)

                for k in range(6):
                    high_part(0, 8, U_GRP + 1 + k, UW)
                    if k < 4:
                        conv_out(0, k)
                    else:
                        gate_out(0, k - 4)
                with act.Fori(0, GROUPS - 1) as g:
                    group(g, False)
                group(GROUPS - 1, True)
                act.wait_ge(so_evac, KD * GROUPS + 1)
                with act.Fori(0, KD) as m:
                    next_u(2, m)

            def attention():
                stat(4)
                for k in range(9):
                    high_part(0, 10, U_ATT + k + 1, UW)

                def turn(c, last):
                    def ahead(k):
                        high_part(c, 10, U_ATT + 9 + k, UW)

                    def v_out(g):
                        act.wait_ge(vt_mm, c * 4 + (g + 1))
                        nc.scalar.copy(vt[:, g, :, :].rearrange("p t f -> p (t f)"), ps[:, g, :]).then_inc(vt_done, 1)

                    def exps(e):
                        act.wait_ge(max_done, c * 8 + (e + 1))
                        nc.scalar.activation(pr[:, e % 2, :], pr[:, e % 2, :], ACT.Exp, bias=nmx[:, e:e + 1],
                                             accum_out=den[:, e:e + 1]).then_inc(exp_done, 1)

                    v_out(0)
                    v_out(1)
                    exps(0)
                    v_out(2)
                    act.wait_ge(vt_mm, c * 4 + 4)
                    nc.scalar.copy(vts[:, :, :].rearrange("p g f -> p (g f)"), ps[0:SMP, 3, 0:AG * P]).then_inc(vt_done, 1)
                    for e in range(8):
                        act.wait_ge(pt_mm, c * 8 + (e + 1))
                        if e >= 2:
                            act.wait_ge(pv_mm, c * 8 + (e - 1))
                        nc.scalar.copy(pt[:, e % 2, 0:512], ps[:, 6, :])
                        nc.scalar.copy(pt[:, e % 2, 512:768], ps[:, 7, 0:256]).then_inc(pt_done, 1)
                        if not last:
                            ahead(e + 1)
                        if e < 7:
                            exps(e + 1)
                        if e == 1:
                            act.wait_ge(smax_done, c + 1)
                            nc.scalar.activation(prs[:, :], prs[:, :], ACT.Exp, bias=nmx[:, 8:9],
                                                 accum_out=den[:, 8:9]).then_inc(sexp_done, 1)
                        if e == 2:
                            act.wait_ge(spt_mm, c * 2 + 1)
                            nc.scalar.copy(pts[:, 0:3, :].rearrange("p k r -> p (k r)"), ps[:, 3, 0:3 * P])
                            nc.scalar.copy(ptn[:, 0, :], ps[0:SMP, 3, rows(3)]).then_inc(spt_done, 1)
                        if e == 3:
                            act.wait_ge(spt_mm, c * 2 + 2)
                            nc.scalar.copy(pts[:, 3, :], ps[:, 3, rows(0)])
                            nc.scalar.copy(ptn[:, 1:3, :].rearrange("p g r -> p (g r)"),
                                           ps[0:SMP, 3, P:3 * P]).then_inc(spt_done, 1)
                        if e == 4:
                            act.wait_ge(spv_mm, c + 1)
                            for j in range(2):
                                r = slice(HD * j, HD * j + HD)
                                ins = nc.scalar.copy(smp(oh[r, SEQ:TOK]), smp(ps[r, 3, 0:P], 2 * NS)[:, :, j * NS:(j + 1) * NS])
                            ins.then_inc(soh_done, 1)
                    act.wait_ge(ot_mm, c + 1)
                    nc.scalar.copy(oh[:, 0:SEQ], ps[:, 3, :]).then_inc(oh_done, 1)
                    if last:
                        high_part(0, 10, U_FFN[3], UW)
                    else:
                        ahead(9)
                        ahead(10)

                with act.Fori(0, PAIRS - 1) as c:
                    turn(c, False)
                turn(PAIRS - 1, True)
                act.wait_ge(ao_evac, KD * PAIRS + 1)
                with act.Fori(0, KD) as m:
                    next_u(5, m)

            high_part(0, 4, 0, UW)
            act.wait_ge(x_done, 1 + 1)
            with act.Fori(0, KD) as m:
                next_u(0, m)
            ffn(0, 1)
            if phases > 1:
                ssd()
            if phases > 2:
                ffn(1, 3)
                ffn(2, 4)
            if phases > 3:
                attention()
            if phases > 4:
                ffn(3, 6)
                stat(last_norm)

        @block.tensor
        def _(pe):
            def product(u, parity, nk, rh, rl, banks, split, first=True, last=True, chunk=None):
                pe.wait_ge(wh_done, u + 1)
                for k in range(nk):
                    if chunk is not None:
                        pe.wait_ge(u_ready, chunk + k + 1 + 1)
                    w = wh[:, parity, k * P:(k + 1) * P]
                    for b, (t0, n) in zip(banks, split):
                        pe.matmul(ps[:, b, 0:n], w, rh[:, k, t0:t0 + n], start=first and k == 0, stop=False)
                        pe.matmul(ps[:, b, 0:n], w, rl[:, k, t0:t0 + n], start=False, stop=False)
                pe.wait_ge(wl_done, u + 1)
                for k in range(nk):
                    w = wl[:, parity, k * P:(k + 1) * P]
                    for b, (t0, n) in zip(banks, split):
                        ins = pe.matmul(ps[:, b, 0:n], w, rh[:, k, t0:t0 + n], start=False,
                                        stop=last and k == nk - 1)
                ins.then_inc(unit_done, 1)

            def stat():
                for h, (t0, n) in enumerate(HALVES):
                    ins = pe.matmul(ps[:, 6 + h, 0:n], ones[:, :], ssq[:, t0:t0 + n], start=True, stop=True)
                ins.then_inc(stat_mm, 1)

            def ffn(f):
                u0, n = U_FFN[f], NORM_OF_FFN[f]

                def pairs(i, first):
                    for p in range(2):
                        for k in range(2):
                            if not first and k == 0:
                                pe.wait_ge(h_ready, i * 2 + (KF * f + p - 1) + 1)
                            if first and p == 1 and k == 1:
                                pe.wait_ge(var_ready, n + 1)
                            product(i * 4 + (u0 + 2 * p + k), (u0 + 2 * p + k) % 2, KD, uh, ul,
                                    (4 * p + 2 * k, 4 * p + 2 * k + 1), HALVES,
                                    chunk=8 * n if first and p == 0 and k == 0 else None)
                            if first and p == 0 and k == 0:
                                stat()

                pairs(0, True)
                with pe.Fori(1, KF // 2) as i:
                    pairs(i, False)

                pe.wait_ge(h_ready, KF * (f + 1) + 1)
                with pe.Fori(0, KD // 2) as i:
                    for p in range(2):
                        pe.wait_ge(x_done, i * 2 + (8 * f + p) + 1)
                        for k in range(2):
                            u = u0 + 2 * KF + 2 * p + k
                            r = slice(k * KF // 2, (k + 1) * KF // 2)
                            product(i * 4 + u, u % 2, KF // 2, hh[:, r, :], hl[:, r, :], (2 * p, 2 * p + 1), HALVES,
                                    first=k == 0, last=k == 1)

            def ssd():
                product(U_SSD, U_SSD % 2, KD, uh, ul, (4, 5), HALVES, chunk=8)
                stat()
                pe.wait_ge(dtok_in, 3)
                srcs = (acT[:, :], er[0:HEADS, 0:TOK], er[0:HEADS, 2 * TOK:3 * TOK])
                for q, src in enumerate(srcs):
                    for c in range(CH + 1):
                        n = P if c < CH else SMP
                        col = (q * (CH + 1) + c) * HEADS
                        ins = pe.transpose(ps[0:n, 4, col:col + HEADS], src[:, c * P:c * P + n], ident[0:HEADS, 0:HEADS])
                ins.then_inc(dtok_mm, 1)
                pe.wait_ge(tok_ready, 1)

                def project(g, k, u):
                    if k == 0:
                        pe.wait_ge(so_evac, (g - 1) * 8 + 1 if not isinstance(g, int) else 1)
                    if k >= 2:
                        pe.wait_ge(pj_evac, g * 6 + (k - 1))
                    product(u, (U_GRP + k) % 2, KD, uh, ul, (2 * (k % 2), 2 * (k % 2) + 1), SPLIT)

                def decays(g):
                    pe.wait_ge(acm_ready, g * 4 + 4)
                    for j in range(HPG):
                        ins = pe.matmul(ps[:, 7, j * SMP:(j + 1) * SMP], ones[0:HEADS, :], acm[:, j, SEQ:TOK],
                                        start=True, stop=True)
                    ins.then_inc(rs_mm, 1)
                    for j in range(3):
                        pe.matmul(ps[:, 4 + j, :], ones[0:HEADS, :], acm[:, j, 0:SEQ], start=True, stop=True).then_inc(r_mm, 1)

                def turn(g):
                    pe.wait_ge(er_done, g * 4 + 1)
                    pe.matmul(ps[:, 4, :], ones[0:HEADS, :], acm[:, 3, 0:SEQ], start=True, stop=True).then_inc(r_mm, 1)
                    for i in range(3):
                        pe.wait_ge(xc_ready, g * 4 + (i + 1))
                        if i < 2:
                            pe.wait_ge(er_done, g * 4 + (i + 2))
                        else:
                            pe.wait_ge(ers_done, g + 1)
                            pe.wait_ge(er_done, g * 4 + 4)
                        for c in range(CH):
                            ins = pe.transpose(ps[:, 5 + i, rows(c)], xc[:, i, rows(c)], ident[:, :])
                        ins.then_inc(t_mm, 1)
                    for i in range(3):
                        ins = pe.transpose(ps[0:SMP, 4, rows(i)], xc[:, i, SEQ:TOK], ident[:, :])
                    ins.then_inc(t_mm, 1)

                def chunk_sums(g):
                    pe.wait_ge(xc_ready, g * 4 + 4)
                    pe.wait_ge(xd_done, g * 2 + 1)
                    for c in range(CH):
                        pe.matmul(ps[:, 5, rows(c)], xc[:, 2, rows(c)], xc[:, 3, rows(c)], start=True, stop=True)
                    pe.wait_ge(xs_done, g + 1)
                    pe.matmul(ps[0:SMP, 4, 0:SMP], xc[:, 2, SEQ:TOK], xc[:, 3, SEQ:TOK],
                              start=True, stop=True).then_inc(cb_mm, 1)
                    pe.wait_ge(xd_done, g * 2 + 2)
                    pe.wait_ge(bt_done, g + 1)
                    for c in range(CH):
                        ins = pe.matmul(ps[:, 6 + c // 2, (c % 2) * 256:(c % 2) * 256 + 256], bt[:, rows(c)],
                                        xw[:, c, :, :].rearrange("p j d -> p (j d)"), start=True, stop=True)
                        if c % 2:
                            ins.then_inc(st_mm, 1)

                def outputs(g):
                    pe.wait_ge(w_done, g + 1)
                    pe.wait_ge(cp_done, g * 4 + 4)
                    pe.wait_ge(hst_done, g + 1)
                    pe.wait_ge(state_in, g * 16 + 16)
                    for i in range(2):
                        for c in range(CH):
                            for jj in range(2):
                                j = 2 * i + jj
                                out = ps[PD * jj:PD * jj + PD, 5 + i, rows(c)]
                                pe.matmul(out, xd[:, c, j, :], sg[:, j * SEQ + c * P:j * SEQ + (c + 1) * P],
                                          start=True, stop=c == 0)
                                if c:
                                    pe.matmul(out, hst[:, c - 1, j * PD:(j + 1) * PD],
                                              er[:, j * SEQ + c * P:j * SEQ + (c + 1) * P], start=False, stop=True)
                        for jj in range(2):
                            j = 2 * i + jj
                            pe.matmul(ps[PD * jj:PD * jj + PD, 4, 2 * i * SMP:(2 * i + 1) * SMP], xds[:, j, :],
                                      sgs[:, j, :], start=True, stop=True)
                        for b in range(NB):
                            col = (2 * i + 1) * SMP + b * NS
                            ins = pe.matmul(ps[:, 4, col:col + NS], h0[:, b, i * P:(i + 1) * P],
                                            xc[:, 3, SEQ + b * NS:SEQ + (b + 1) * NS], start=True, stop=True)
                        ins.then_inc(y_mm, 1)

                def states(g):
                    for k, bank in enumerate((7, 5, 6, 7)):
                        if k == 1 or k == 2:
                            pe.wait_ge(y_evac, g * 2 + k)
                        if k == 3:
                            pe.wait_ge(ss_evac, g * 4 + 1)
                        for b in (2 * k, 2 * k + 1):
                            ins = pe.matmul(ps[:, bank, (b % 2) * 256:(b % 2) * 256 + 256], bd[:, b, :],
                                            xws[:, :, :].rearrange("p j d -> p (j d)"), start=True, stop=True)
                        ins.then_inc(ss_mm, 1)
                    pe.wait_ge(gsq_done, g * 2 + 2)
                    pe.wait_ge(ss_evac, g * 4 + 2)
                    for h, (t0, n) in enumerate(HALVES):
                        for i in range(2):
                            ins = pe.matmul(ps[:, 4 + h, 0:n], ones[:, :], zs[:, i, t0:t0 + n], start=i == 0, stop=i == 1)
                    ins.then_inc(gn_mm, 1)

                def project_out(g, u0):
                    pe.wait_ge(g_ready, g * 2 + 2)
                    for m in range(KD):
                        u = u0 + m // 4
                        if m == 0:
                            pe.wait_ge(pj_evac, g * 6 + 12 if not isinstance(g, int) else 6 * GROUPS)
                        elif m == 1:
                            pass
                        else:
                            pe.wait_ge(so_evac, g * 8 + (m - 1) + 1)
                        pe.wait_ge(wh_done, u + 1)
                        pe.wait_ge(wl_done, u + 1)
                        for k in range(2):
                            w = slice(((m % 4) * 2 + k) * P, ((m % 4) * 2 + k + 1) * P)
                            for h, (t0, n) in enumerate(SPLIT):
                                out = ps[:, 2 * (m % 2) + h, 0:n]
                                pe.matmul(out, wh[:, (U_GRP + m // 4) % 2, w], gh[:, k, t0:t0 + n], start=k == 0, stop=False)
                                pe.matmul(out, wh[:, (U_GRP + m // 4) % 2, w], gl[:, k, t0:t0 + n], start=False, stop=False)
                                ins = pe.matmul(out, wl[:, (U_GRP + m // 4) % 2, w], gh[:, k, t0:t0 + n], start=False, stop=k == 1)
                        ins.then_inc(unit_done if m % 4 == 3 else so_mm, 1)

                for k in range(6):
                    project(0, k, U_GRP + k)
                with pe.Fori(0, GROUPS - 1) as g:
                    def ahead(k):
                        project(g + 1, k, g * 8 + (U_GRP + 6 + k))

                    decays(g)
                    ahead(0)
                    turn(g)
                    ahead(1)
                    chunk_sums(g)
                    ahead(2)
                    outputs(g)
                    ahead(3)
                    states(g)
                    ahead(4)
                    ahead(5)
                    project_out(g, g * 8 + (U_GRP + 12))
                g = GROUPS - 1
                for stage in (decays, turn, chunk_sums, outputs, states):
                    stage(g)
                project_out(g, U_FFN1 - 2)

            def attention():
                pe.wait_ge(ao_evac, 1)
                for k in range(9):
                    if k >= 2:
                        pe.wait_ge(q_evac, k - 1)
                    product(U_ATT + k, (U_ATT + k) % 2, KD, uh, ul, (2 * (k % 2), 2 * (k % 2) + 1), SPLIT,
                            chunk=32 if k == 0 else None)
                    if k == 0:
                        stat()

                def turn(c, last):
                    def ahead(k):
                        u = U_ATT + 9 + k
                        product(c * 10 + u, u % 2, KD, uh, ul, (0, 1), SPLIT)

                    def scores(e):
                        t, r = e // 2, slice(HD * (e % 2), HD * (e % 2) + HD)
                        if e:
                            pe.wait_ge(max_done, c * 8 + e)
                        pe.matmul(ps[:, 4, :], qkv[r, 0, rows(t)], qkv[r, 1, 0:SEQ], start=True, stop=True)
                        if e == 1:
                            for g in range(AG):
                                pe.matmul(ps[:, 5, 2 * P + g * SMP:2 * P + (g + 1) * SMP], qa[:, g, :],
                                          qkv[:, 3 * g + 1, SEQ:TOK], start=True, stop=True)
                        pe.matmul(ps[:, 5, 0:P], qkv[r, 3, rows(t)], qkv[r, 4, rows(t)], start=True, stop=True)
                        pe.matmul(ps[:, 5, P:2 * P], qkv[r, 6, rows(t)], qkv[r, 7, rows(t)],
                                  start=True, stop=True).then_inc(sc_mm, 1)

                    pe.wait_ge(qk_ready, c + 1)
                    pe.wait_ge(ao_evac, c * 8 + 1)
                    scores(0)
                    for g in range(AG):
                        for t in range(CH):
                            ins = pe.transpose(ps[:, g, rows(t)], qkv[:, 3 * g + 2, rows(t)], ident[:, :])
                        ins.then_inc(vt_mm, 1)
                    for g in range(AG):
                        ins = pe.transpose(ps[0:SMP, 3, rows(g)], qkv[:, 3 * g + 2, SEQ:TOK], ident[:, :])
                    ins.then_inc(vt_mm, 1)
                    pe.wait_ge(kc_in, c * 64 + 64)
                    for b in range(NB):
                        for k in range(4):
                            ins = pe.matmul(ps[:, 6, k * P + b * 2 * NS:k * P + (b + 1) * 2 * NS], kc[:, b, rows(k)],
                                            qa[:, (0, 1, 1, 2)[k], b * 2 * NS:(b + 1) * 2 * NS], start=True, stop=True)
                    ins.then_inc(sst_mm, 1)

                    for e in range(8):
                        if e < 7:
                            scores(e + 1)
                        t, r = e // 2, slice(HD * (e % 2), HD * (e % 2) + HD)
                        pe.wait_ge(exp_done, c * 8 + (e + 1))
                        if e == 0:
                            pe.wait_ge(sst_done, c + 1)
                        for k in range(6):
                            ins = pe.transpose(ps[:, 6 + k // 4, rows(k % 4)], pr[:, e % 2, rows(k)], ident[:, :])
                        ins.then_inc(pt_mm, 1)
                        if not last:
                            if e == 0:
                                pe.wait_ge(vt_done, c * 4 + 2)
                            else:
                                pe.wait_ge(q_evac, c * 9 + (9 + e))
                            ahead(e)
                        if e == 0:
                            pe.wait_ge(vt_done, c * 4 + 4)
                        else:
                            pe.wait_ge(un_done, c * 8 + e)
                        pe.wait_ge(pt_done, c * 8 + (e + 1))
                        for k in range(6):
                            v = vt[:, max(0, k - 3), k if k < 4 else t, r]
                            ins = pe.matmul(ps[:, 2, 0:HD], pt[:, e % 2, rows(k)], v, start=k == 0, stop=k == 5)
                        ins.then_inc(pv_mm, 1)
                        if e == 0:
                            for k in range(4):
                                ins = pe.transpose(ps[:, 3, rows(k)], pts[:, k, :], ident[:, :])
                            ins.then_inc(ssc_mm, 1)
                        if e == 2 or e == 3:
                            if e == 2:
                                pe.wait_ge(snorm_done, c + 1)
                            else:
                                pe.wait_ge(spt_done, c * 2 + 1)
                            blocks = (0, 1, 2, 4) if e == 2 else (3, 5, 6)
                            for i, k in enumerate(blocks):
                                if k < 4:
                                    ins = pe.transpose(ps[:, 3, rows(i)], prs[:, rows(k)], ident[:, :])
                                else:
                                    own = slice(KEYC + (k - 4) * SMP, KEYC + (k - 3) * SMP)
                                    ins = pe.transpose(ps[0:SMP, 3, rows(i)], prs[:, own], ident[:, :])
                            ins.then_inc(spt_mm, 1)
                        if e == 4:
                            pe.wait_ge(spt_done, c * 2 + 2)
                            pe.wait_ge(vc_in, c * 32 + 32)
                            for g in range(AG):
                                pe.matmul(ps[:, 3, 0:P], vts[:, g, :], ptn[:, g, :], start=g == 0, stop=False, skip_group_check=True)
                            for b in range(NB):
                                q = slice(b * 2 * NS, (b + 1) * 2 * NS)
                                for k in range(4):
                                    ins = pe.matmul(ps[:, 3, q], vc[:, b, k, :], pts[:, k, q], start=False,
                                                    stop=k == 3, skip_group_check=True)
                            ins.then_inc(spv_mm, 1)
                    pe.wait_ge(sol_done, c + 1)
                    pe.wait_ge(un_done, c * 8 + 8)
                    for t in range(CH):
                        ins = pe.transpose(ps[:, 3, rows(t)], un[:, t, :], ident[:, :])
                    ins.then_inc(ot_mm, 1)
                    if not last:
                        pe.wait_ge(q_evac, c * 9 + 17)
                        ahead(8)
                    u = U_FFN[3] - 1 if last else c * 10 + (U_ATT + 18)
                    parity = (U_ATT + 18) % 2 if not last else u % 2
                    pe.wait_ge(wh_done, u + 1)
                    pe.wait_ge(wl_done, u + 1)
                    pe.wait_ge(ol_done, c + 1)
                    for m in range(KD):
                        if m >= 2:
                            pe.wait_ge(ao_evac, c * 8 + (m - 1) + 1)
                        for h, (t0, n) in enumerate(SPLIT):
                            out = ps[:, 4 + 2 * (m % 2) + h, 0:n]
                            pe.matmul(out, wh[:, parity, rows(m)], oh[:, t0:t0 + n], start=True, stop=False)
                            pe.matmul(out, wh[:, parity, rows(m)], ol[:, t0:t0 + n], start=False, stop=False)
                            ins = pe.matmul(out, wl[:, parity, rows(m)], oh[:, t0:t0 + n], start=False, stop=True)
                        ins.then_inc(unit_done if m == KD - 1 else ao_mm, 1)

                with pe.Fori(0, PAIRS - 1) as c:
                    turn(c, False)
                turn(PAIRS - 1, True)

            ffn(0)
            if phases > 1:
                ssd()
            if phases > 2:
                ffn(1)
                ffn(2)
            if phases > 3:
                attention()
            if phases > 4:
                ffn(3)
                pe.wait_ge(u_ready, 56 + 1)
                stat()

        @block.vector
        def _(dve):
            self_ = Steps(dve, dve_self)
            V = nc.vector

            def step(ins):
                self_.done(ins)
                self_.wait()

            def next_u(n, m):
                dve.wait_ge(xa_done, m + (8 * n + 1))
                step(V.tensor_tensor(ssq[:, :], ssq[:, :], sqx[:, :], ALU.add))
                g = gains[:, n, one(m)]
                if n == last_norm:
                    V.tensor_copy(sqx[:, 0:1], ssq[:, 0:1]).then_inc(u_ready, 1)
                elif n == 4:
                    for v in ((lambda a: perm(a[:, m, 0:SEQ]), lambda a: a[:, m, 0:SEQ].rearrange("p (t a) -> p t a", t=DIL)),
                              (lambda a: a[:, m, SEQ:TOK],) * 2):
                        ins = V.scalar_tensor_tensor(v[1](ul), v[0](x), g, v[1](uh).bitcast(F32), ALU.mult, ALU.subtract)
                    ins.then_inc(u_ready, 1)
                else:
                    V.scalar_tensor_tensor(ul[:, m, :], x[:, m, :], g, uh[:, m, :].bitcast(F32),
                                           ALU.mult, ALU.subtract).then_inc(u_ready, 1)

            def stat(n):
                dve.wait_ge(stat_mm, n + 1)
                V.tensor_scalar(two(rms[:, :]), ps[:, 6:8, 0:HALF], 1.0 / D, EPS, ALU.mult, ALU.add).then_inc(var_ready, 1)
                V.memset(ssq[:, :], 0.0)
                dve.wait_ge(sqrt_ready, n + 1)
                V.reciprocal(rms[:, :], rms[:, :]).then_inc(rms_ready, 1)
                dve.wait_ge(rms_ready, n + 1)

            def ffn(f, next_n):
                u0 = U_FFN[f]
                stat(NORM_OF_FFN[f])
                with self_.loop(0, KF // 2, 4) as i:
                    for p in range(2):
                        u = u0 + 2 * p
                        dve.wait_ge(unit_done, i * 4 + (u + 1))
                        dve.wait_ge(h_ready, i * 2 + (KF * f + p) + 1)
                        V.tensor_tensor(two(gate[:, :]), ps[:, 4 * p:4 * p + 2, 0:HALF], two(rms[:, :]),
                                        ALU.mult).then_inc(gate_scaled, 1)
                        dve.wait_ge(unit_done, i * 4 + (u + 2))
                        step(V.tensor_tensor(two(up[:, :]), ps[:, 4 * p + 2:4 * p + 4, 0:HALF], two(rms[:, :]), ALU.mult))
                        dve.wait_ge(silu_done, i * 2 + (KF * f + p + 1))
                        step(V.tensor_tensor(up[:, :], up[:, :], gate[:, :], ALU.mult))
                        j = bass.ds(i * 2 + p, 1)
                        hi = hh[:, j, :].rearrange("p j t -> p (j t)")
                        lo = hl[:, j, :].rearrange("p j t -> p (j t)")
                        V.tensor_copy(hi, up[:, :]).then_inc(h_high, 1)
                        dve.wait_ge(h_high, i * 2 + (KF * f + p + 1))
                        V.tensor_tensor(lo, up[:, :], hi.bitcast(F32), ALU.subtract).then_inc(h_ready, 1)
                with self_.loop(0, KD // 2, 2) as i:
                    for p in range(2):
                        m = i * 2 + p
                        dve.wait_ge(unit_done, i * 4 + (u0 + 2 * KF + 2 * p + 2))
                        xm = x[:, bass.ds(m, 1), :].rearrange("p j (h n) -> p (j h) n", h=2)
                        V.scalar_tensor_tensor(xm, ps[:, 2 * p:2 * p + 2, 0:HALF], 0.5, xm,
                                               ALU.mult, ALU.add).then_inc(x_done, 1)
                        next_u(next_n, m)

            def ssd():
                t0, t1, t2 = (er[0:HEADS, k * TOK:(k + 1) * TOK] for k in range(3))
                t3, t4, t5 = (sg[0:HEADS, k * TOK:(k + 1) * TOK] for k in range(3))
                stat(1)
                dve.wait_ge(ssd_const, 160)
                step(V.tensor_tensor(two(t0), ps[0:HEADS, 4:6, 0:HALF], two(rms[0:HEADS, :]), ALU.mult))
                step(V.tensor_scalar(t0, t0, dtb[:, 0:1], None, ALU.add))
                V.scalar_tensor_tensor(t1, t0, -1.0, t0, ALU.mult, ALU.max).then_inc(dt_abs, 1)
                V.memset(tok[:, :, :, :].rearrange("p q c h -> p (q c h)"), 0.0)
                dve.wait_ge(dt_exp, 1)
                step(V.tensor_scalar(t2, t1, 2.0, None, ALU.add))
                step(V.reciprocal(t2, t2))
                step(V.tensor_tensor(t3, t1, t2, ALU.mult))
                step(V.tensor_tensor(t4, t3, t3, ALU.mult))
                step(V.tensor_scalar(t5, t4, 1.0 / 17, None, ALU.mult))
                for k in range(7, 0, -1):
                    step(V.scalar_tensor_tensor(t5, t5, 1.0 / (2 * k + 1), t4, ALU.add, ALU.mult))
                step(V.scalar_tensor_tensor(t5, t5, 1.0, t3, ALU.add, ALU.mult))
                step(V.tensor_scalar(t0, t0, 0.0, None, ALU.max))
                step(V.scalar_tensor_tensor(t0, t5, 2.0, t0, ALU.mult, ALU.add))
                dve.wait_ge(ea_ready, 1)
                step(V.tensor_scalar(t3, t0, ea[:, 0:1], -1.0, ALU.mult, ALU.mult))
                step(V.tensor_tensor_scan(acT[:, :], keep[:, :], t3, 0.0, ALU.mult, ALU.add))
                for a, b, n in ((0, SEQ, P), (SEQ, TOK, NS)):
                    v, o = smp(acT[:, a:b], n), smp(t2[:, a:b], n)
                    ins = V.tensor_tensor(o, v[:, :, n - 1:n].broadcast_to([HEADS, (b - a) // n, n]), v, ALU.subtract)
                ins.then_inc(coef_in, 1)
                dve.wait_ge(coef_exp, 1)
                step(V.tensor_tensor(t2, t2, t0, ALU.mult))
                V.tensor_copy(dec[0:1, 0, 0:1], t2[0:1, 0:1]).then_inc(dtok_in, 3)
                dve.wait_ge(dtok_mm, 1)
                v = ps[:, 4, 0:3 * (CH + 1) * HEADS].rearrange("p (q c h) -> p q c h", q=3, c=CH + 1)
                V.tensor_copy(tok[:, :, 0:CH, :], v[:, :, 0:CH, :])
                V.tensor_copy(tok[0:SMP, :, CH, :], v[0:SMP, :, CH, :]).then_inc(tok_ready, 1)
                dve.wait_ge(tok_ready, 1)

                def conv_in(g, k, u):
                    dve.wait_ge(unit_done, u + 1)
                    b = 2 * (k % 2)
                    if k == 0:
                        dve.wait_ge(nc_ready, g + 1)
                    V.tensor_tensor(two(xp[:, k, CONV - 1:XS]), ps[:, b:b + 2, 0:QTR], two(rms[:, 0:SEQ]), ALU.mult)
                    V.tensor_tensor(smp(xp[:, k, XS:XW], SW)[:, :, CONV - 1:SW], smp(ps[:, b + 1, QTR:QTR + SMP]),
                                    smp(rms[:, SEQ:TOK]), ALU.mult).then_inc(pj_evac, 1)

                def conv(g, k):
                    dve.wait_ge(pj_evac, g * 6 + (k + 1))
                    dve.wait_ge(cs_in, g * 4 + (k + 1))
                    if k >= 2:
                        dve.wait_ge(xc_ready, g * 4 + (k - 1))
                    w = [cw[:, one(g * 20 + (k * 5 + t))] for t in range(CONV)]
                    step(V.tensor_scalar(acc[:, k % 2, 0:XO], xp[:, k, 0:XO], w[0], None, ALU.mult))
                    for t in range(1, CONV):
                        ins = V.scalar_tensor_tensor(acc[:, k % 2, 0:XO], xp[:, k, t:t + XO], w[t], acc[:, k % 2, 0:XO],
                                                     ALU.mult, ALU.add)
                        if t < CONV - 1:
                            step(ins)
                    ins.then_inc(conv_done, 1)

                def gate_in(g, k, u):
                    dve.wait_ge(unit_done, u + 1)
                    b = 2 * (k % 2)
                    V.tensor_tensor(two(zs[:, k, 0:SEQ]), ps[:, b:b + 2, 0:QTR], two(rms[:, 0:SEQ]), ALU.mult)
                    V.tensor_tensor(zs[:, k, SEQ:TOK], ps[:, b + 1, QTR:QTR + SMP], rms[:, SEQ:TOK],
                                    ALU.mult).then_inc(pj_evac, 1)

                def head_rows(g):
                    step(V.tensor_copy(gtok[:, :, :, :].rearrange("p q c j -> p (q c) j"),
                                       tok[:, :, :, bass.ds(g * HPG, HPG)].rearrange("p q c j -> p (q c) j")))
                    for j in range(HPG):
                        V.tensor_scalar(acm[:, j, :], acT[:, :], ident[0:HEADS, one(g * HPG + j)], None,
                                        ALU.mult).then_inc(acm_ready, 1)

                def seg(g, j):
                    dve.wait_ge(r_mm, g * 4 + (j + 1))
                    for c in range(CH):
                        ins = V.tensor_scalar(sg[:, j * SEQ + c * P:j * SEQ + (c + 1) * P],
                                              ps[:, (4, 5, 6, 4)[j], c * P:(c + 1) * P], gtok[:, 0, c, j:j + 1],
                                              0.0, ALU.subtract, ALU.min)
                    ins.then_inc(seg_done, 1)

                def group(g, last):
                    def ahead(k):
                        u = g * 8 + (U_GRP + 6 + k)
                        if k < 4:
                            conv_in(g + 1, k, u)
                        else:
                            gate_in(g + 1, k - 4, u)

                    dve.wait_ge(rs_mm, g + 1)
                    for j in range(HPG):
                        ins = V.tensor_scalar(sgs[:, j, :], ps[0:SMP, 7, j * SMP:(j + 1) * SMP], gtok[0:SMP, 0, CH, j:j + 1],
                                              0.0, ALU.subtract, ALU.min)
                    ins.then_inc(segs_done, 1)
                    for j in range(3):
                        seg(g, j)
                    if not last:
                        ahead(0)
                    seg(g, 3)
                    if not last:
                        conv(g + 1, 0)
                    dve.wait_ge(er_done, g * 4 + 4)
                    V.tensor_copy(dec[:, :, :], er[:, :].rearrange("p (j c q) -> p j c q", j=HPG, c=CH)[:, :, :, P - 1])
                    dve.wait_ge(ers_done, g + 1)
                    V.tensor_copy(decs[:, :, :], ers[:, :].rearrange("p (j b q) -> p j b q", j=HPG, b=NB)[:, :, :, NS - 1]
                                  ).then_inc(dec_ready, 1)
                    for i in range(2):
                        dve.wait_ge(t_mm, g * 4 + (i + 1))
                        src = ps[:, 5 + i, :].rearrange("p (c d) -> p c d", c=CH)
                        for q, dst in ((1, xd), (2, xw)):
                            for jj in range(2):
                                j = 2 * i + jj
                                ins = V.tensor_tensor(dst[:, :, j, :], src[:, :, jj * PD:(jj + 1) * PD],
                                                      gtok[:, q, 0:CH, j:j + 1].broadcast_to([P, CH, PD]), ALU.mult)
                        ins.then_inc(xd_done, 1)
                    dve.wait_ge(t_mm, g * 4 + 4)
                    for q, dst in ((1, xds), (2, xws)):
                        V.tensor_tensor(dst[:, :, :], ps[0:SMP, 4, 0:2 * P].rearrange("p (j d) -> p j d", j=HPG),
                                        gtok[0:SMP, q, CH, :].unsqueeze(2).broadcast_to([SMP, HPG, PD]), ALU.mult)
                    V.tensor_tensor(bd[:, :, :], ps[0:SMP, 4, 2 * P:3 * P].unsqueeze(1).broadcast_to([SMP, NB, NST]),
                                    maskb[:, :].unsqueeze(2).broadcast_to([SMP, NB, NST]), ALU.mult).then_inc(xs_done, 1)
                    if not last:
                        ahead(1)
                    dve.wait_ge(cb_mm, g + 1)
                    V.tensor_tensor(cbs[:, :], ps[0:SMP, 4, 0:SMP], masks[:, :], ALU.mult)
                    V.tensor_tensor(cbm[:, :].rearrange("p (c q) -> p c q", c=CH), ps[:, 5, :].rearrange("p (c q) -> p c q", c=CH),
                                    mask[:, :].unsqueeze(1).broadcast_to([P, CH, P]), ALU.mult).then_inc(cbm_done, 1)
                    dve.wait_ge(cbm_done, g + 1)
                    for j in range(HPG):
                        dve.wait_ge(e_done, g * 4 + (j + 1))
                        e = sg[:, j * SEQ:(j + 1) * SEQ]
                        V.tensor_tensor(e, e, cbm[:, :], ALU.mult)
                    dve.wait_ge(es_done, g + 1)
                    V.tensor_tensor(sgs[:, :, :], sgs[:, :, :], cbs[:, :].unsqueeze(1).broadcast_to([SMP, HPG, SMP]),
                                    ALU.mult).then_inc(w_done, 1)
                    dve.wait_ge(st_mm, g * 2 + 1)
                    dve.wait_ge(st_h, g * 16 + 16)
                    step(V.tensor_copy(hst[:, 0, :], ps[:, 6, 0:256]))
                    for c in range(1, CH):
                        if c == 2:
                            dve.wait_ge(st_mm, g * 2 + 2)
                        for j in range(HPG):
                            d = slice(j * PD, (j + 1) * PD)
                            ins = V.scalar_tensor_tensor(hst[:, c, d], hst[:, c - 1, d], dec[:, j, c:c + 1],
                                                         ps[:, 6 + c // 2, (c % 2) * 256 + j * PD:(c % 2) * 256 + (j + 1) * PD],
                                                         ALU.mult, ALU.add)
                        if c < CH - 1:
                            step(ins)
                    ins.then_inc(hst_done, 1)
                    if not last:
                        conv(g + 1, 1)
                        ahead(2)
                        head_rows(g + 1)
                    for i in range(2):
                        dve.wait_ge(y_mm, g * 2 + 2)
                        dk = dsk[:, one(g * 2 + i)]
                        for jj in range(2):
                            r = slice(PD * jj, PD * jj + PD)
                            j = 2 * i + jj
                            V.tensor_tensor(yof[r, i, :], ps[r, 4, (2 * i + 1) * SMP:(2 * i + 2) * SMP],
                                            ers[r, j * SMP:(j + 1) * SMP], ALU.mult)
                        V.scalar_tensor_tensor(ysb[:, i, 0:SEQ], xc[:, i, 0:SEQ], dk, ps[:, 5 + i, :], ALU.mult, ALU.add)
                        ins = V.scalar_tensor_tensor(ysb[:, i, SEQ:TOK], xc[:, i, SEQ:TOK], dk,
                                                     ps[:, 4, 2 * i * SMP:(2 * i + 1) * SMP], ALU.mult, ALU.add)
                        ins.then_inc(y_evac, 1)
                        dve.wait_ge(y_evac, g * 2 + (i + 1))
                        step(V.tensor_tensor(ysb[:, i, SEQ:TOK], ysb[:, i, SEQ:TOK], yof[:, i, :], ALU.add))
                        dve.wait_ge(zs_ready, g * 2 + (i + 1))
                        V.tensor_tensor(ysb[:, i, :], ysb[:, i, :], zs[:, i, :], ALU.mult).then_inc(gz_ready, 1)
                    if not last:
                        ahead(3)
                        conv(g + 1, 2)
                    for k, bank in enumerate((7, 5, 6, 7)):
                        dve.wait_ge(ss_mm, g * 4 + (k + 1))
                        dve.wait_ge(hm_done, g * 8 + (2 * k + 2))
                        V.tensor_tensor(h0[:, 2 * k:2 * k + 2, :], h0[:, 2 * k:2 * k + 2, :],
                                        two(ps[:, bank, :]), ALU.add).then_inc(ss_evac, 1)
                    dve.wait_ge(gn_mm, g + 1)
                    V.tensor_scalar(two(gr[:, :]), ps[:, 4:6, 0:HALF], 1.0 / (2 * P), EPS, ALU.mult, ALU.add).then_inc(gvar_ready, 1)
                    if not last:
                        conv(g + 1, 3)
                    dve.wait_ge(gsqrt_ready, g + 1)
                    dve.wait_ge(gz_ready, g * 2 + 2)
                    step(V.reciprocal(gr[:, :], gr[:, :]))
                    for i in range(2):
                        V.scalar_tensor_tensor(ysb[:, i, :], ysb[:, i, :], ng[:, one(g * 2 + i)], gr[:, :],
                                               ALU.mult, ALU.mult).then_inc(gn_ready, 1)
                    if not last:
                        ahead(4)
                    for i in range(2):
                        dve.wait_ge(gn_ready, g * 2 + (i + 1))
                        dve.wait_ge(gh_done, g * 2 + (i + 1))
                        V.tensor_tensor(gl[:, i, :], ysb[:, i, :], gh[:, i, :].bitcast(F32), ALU.subtract).then_inc(g_ready, 1)
                    if not last:
                        ahead(5)
                    for m in range(KD):
                        if m % 4 == 3:
                            dve.wait_ge(unit_done, (U_FFN1 - 1 if last else g * 8 + (U_GRP + 13)) + m // 4)
                        else:
                            dve.wait_ge(so_mm, g * 6 + (m - m // 4 + 1))
                        b = 2 * (m % 2)
                        V.tensor_tensor(two(x[:, m, 0:SEQ]), two(x[:, m, 0:SEQ]), ps[:, b:b + 2, 0:QTR], ALU.add)
                        V.tensor_tensor(x[:, m, SEQ:TOK], x[:, m, SEQ:TOK], ps[:, b + 1, QTR:QTR + SMP],
                                        ALU.add).then_inc(so_evac, 1)

                for k in range(4):
                    conv_in(0, k, U_GRP + k)
                    conv(0, k)
                for k in range(2):
                    gate_in(0, k, U_GRP + 4 + k)
                head_rows(0)
                with self_.loop(0, GROUPS - 1, SSD_DVE_STEPS) as g:
                    group(g, False)
                group(GROUPS - 1, True)
                with self_.loop(0, KD, 1) as m:
                    next_u(2, m)

            def attention():
                stat(4)
                dve.wait_ge(att_const, 80)
                V.tensor_copy(rmp[:, 0:SEQ].rearrange("p (t a) -> p t a", t=DIL), perm(rms[:, 0:SEQ]))
                step(V.tensor_copy(rmp[:, SEQ:TOK], rms[:, SEQ:TOK]))

                def unit_out(k, u, b):
                    dve.wait_ge(unit_done, u + 1)
                    i = QKV_ORDER[k]
                    dst = stage[:, k - 3, :] if 3 <= k < 3 + AHEAD and b is None else qkv[:, i, :]
                    b = b or 0
                    views = ((two(dst[:, 0:SEQ]), ps[:, b:b + 2, 0:QTR], two(rmp[:, 0:SEQ])),
                             (dst[:, SEQ:TOK], ps[:, b + 1, QTR:QTR + SMP], rmp[:, SEQ:TOK]))
                    for d, src, r in views:
                        if i % 3 == 0:
                            ins = V.scalar_tensor_tensor(d, src, HD ** -0.5, r, ALU.mult, ALU.mult)
                        else:
                            ins = V.tensor_tensor(d, src, r, ALU.mult)
                    ins.then_inc(q_evac, 1)

                def sample_q(n):
                    dve.wait_ge(q_evac, n)
                    for g in range(AG):
                        for j in range(2):
                            r = slice(HD * j, HD * j + HD)
                            ins = V.tensor_copy(smp(qa[r, g, :], 2 * NS)[:, :, j * NS:(j + 1) * NS], smp(qkv[r, 3 * g, SEQ:TOK]))
                    ins.then_inc(qk_ready, 1)

                for k in range(9):
                    unit_out(k, U_ATT + k, 2 * (k % 2))
                dve.wait_ge(qa_zero, 1)
                sample_q(9)

                def turn(c, last):
                    def ahead(k):
                        unit_out(k, c * 10 + (U_ATT + 9 + k), None)

                    def softmax_in(e):
                        t, j = e // 2, e % 2
                        dve.wait_ge(sc_mm, c * 8 + (e + 1))
                        if e >= 2:
                            dve.wait_ge(pt_mm, c * 8 + (e - 1))
                        V.scalar_tensor_tensor(pr[:, j, 0:SEQ], d0[:, t, :], slp[:, bass.ds(c * 2 + j, 1)], ps[:, 4, :],
                                               ALU.mult, ALU.add)
                        if e == 1:
                            for g in range(AG):
                                k1 = KEYC + g * SMP
                                V.scalar_tensor_tensor(prs[:, k1:k1 + SMP], dsm[:, k1:k1 + SMP], sls[:, bass.ds(c * AG + g, 1)],
                                                       ps[:, 5, 2 * P + g * SMP:2 * P + (g + 1) * SMP], ALU.mult, ALU.add)
                        for g in (1, 2):
                            o = slice(SEQ + (g - 1) * P, SEQ + g * P)
                            ins = V.scalar_tensor_tensor(pr[:, j, o], d12[:, g - 1, :], slp[:, bass.ds(c * 2 + (AH * g + j), 1)],
                                                         ps[:, 5, (g - 1) * P:g * P], ALU.mult, ALU.add)
                        step(ins)
                        step(V.reduce_max(nmx[:, e:e + 1], pr[:, j, :], AX.X))
                        V.tensor_scalar(nmx[:, e:e + 1], nmx[:, e:e + 1], -1.0, None, ALU.mult).then_inc(max_done, 1)

                    def head_out(e):
                        dve.wait_ge(exp_done, c * 8 + (e + 1))
                        step(V.reciprocal(rcp[:, e:e + 1], den[:, e:e + 1]))
                        dve.wait_ge(pv_mm, c * 8 + (e + 1))
                        V.tensor_scalar(un[:, e // 2, HD * (e % 2):HD * (e % 2) + HD], ps[:, 2, 0:HD],
                                        rcp[:, e:e + 1], None, ALU.mult).then_inc(un_done, 1)

                    softmax_in(0)
                    dve.wait_ge(sst_mm, c + 1)
                    V.tensor_copy(pts[:, :, :].rearrange("p k r -> p (k r)"), ps[:, 6, :]).then_inc(sst_done, 1)
                    for e in range(8):
                        if e < 7:
                            softmax_in(e + 1)
                        if e == 1:
                            dve.wait_ge(ssc_mm, c + 1)
                            for g, (k0, n) in enumerate(KEYR):
                                ins = V.scalar_tensor_tensor(prs[:, k0:k0 + n], dsm[:, k0:k0 + n], sls[:, bass.ds(c * AG + g, 1)],
                                                             ps[:, 3, k0:k0 + n], ALU.mult, ALU.add)
                            step(ins)
                            step(V.reduce_max(nmx[:, 8:9], prs[:, :], AX.X))
                            V.tensor_scalar(nmx[:, 8:9], nmx[:, 8:9], -1.0, None, ALU.mult).then_inc(smax_done, 1)
                        if e == 2:
                            dve.wait_ge(sexp_done, c + 1)
                            step(V.reciprocal(rcp[:, 8:9], den[:, 8:9]))
                            V.tensor_scalar(prs[:, :], prs[:, :], rcp[:, 8:9], None, ALU.mult).then_inc(snorm_done, 1)
                        if e == 5:
                            dve.wait_ge(soh_done, c + 1)
                            for j in range(2):
                                r = slice(HD * j, HD * j + HD)
                                ins = V.tensor_tensor(smp(ol[r, SEQ:TOK]), smp(ps[r, 3, 0:P], 2 * NS)[:, :, j * NS:(j + 1) * NS],
                                                      smp(oh[r, SEQ:TOK]).bitcast(F32), ALU.subtract)
                            ins.then_inc(sol_done, 1)
                        if not last:
                            if e == 0:
                                dve.wait_ge(st_v, c * 48 + 48)
                            if e == 6:
                                dve.wait_ge(st_k, c * 48 + 48)
                            ahead(e)
                        head_out(e)
                    dve.wait_ge(oh_done, c + 1)
                    V.tensor_tensor(ol[:, 0:SEQ], ps[:, 3, :], oh[:, 0:SEQ].bitcast(F32), ALU.subtract).then_inc(ol_done, 1)
                    if not last:
                        for i in range(AHEAD):
                            ins = V.tensor_copy(qkv[:, QKV_ORDER[3 + i], :], stage[:, i, :])
                        step(ins)
                        ahead(8)
                        sample_q(c * 9 + 18)
                    for m in range(KD):
                        if m == KD - 1:
                            dve.wait_ge(unit_done, U_FFN[3] if last else c * 10 + (U_ATT + 19))
                        else:
                            dve.wait_ge(ao_mm, c * 7 + (m + 1))
                        b = 4 + 2 * (m % 2)
                        xm = x[:, m, 0:SEQ].rearrange("p (a h t) -> p h t a", h=2, t=2)
                        V.tensor_tensor(xm, xm, ps[:, b:b + 2, 0:QTR].rearrange("p h (t a) -> p h t a", t=2), ALU.add)
                        V.tensor_tensor(x[:, m, SEQ:TOK], x[:, m, SEQ:TOK], ps[:, b + 1, QTR:QTR + SMP],
                                        ALU.add).then_inc(ao_evac, 1)

                with self_.loop(0, PAIRS - 1, ATT_DVE_STEPS) as c:
                    turn(c, False)
                turn(PAIRS - 1, True)
                with self_.loop(0, KD, 1) as m:
                    next_u(5, m)

            for k, (s, by) in enumerate(((st_hs, 16), (st_nc, 16), (st_h, 16), (conv_done, 1),
                                         (u_ready, 1), (so_evac, 1), (ao_evac, 1), (x_done, 1), (h_ready, 1), (nc_ready, 1))):
                V.memset(rms[:, k:k + 1], 0.0).then_inc(s, by)
            dve.wait_ge(const_in, 64)
            step(V.memset(ssq[:, :], 0.0))
            V.memset(sqx[:, :], 0.0).then_inc(x_done, 1)
            with self_.loop(0, KD, 1) as m:
                next_u(0, m)
            ffn(0, 1)
            if phases > 1:
                ssd()
            if phases > 2:
                dve.wait_ge(st_h, 16 * GROUPS + 16)
                dve.wait_ge(st_hs, 16 * GROUPS + 16)
                dve.wait_ge(st_nc, 16 * GROUPS + 16)
                ffn(1, 3)
                ffn(2, 4)
            if phases > 3:
                attention()
            if phases > 4:
                dve.wait_ge(st_v, 16 * PAIRS * AG)
                dve.wait_ge(st_k, 16 * PAIRS * AG)
                ffn(3, 6)
                stat(last_norm)
                for m in range(KD):
                    V.scalar_tensor_tensor(x[:, m, :], x[:, m, :], gains[:, last_norm, m:m + 1], rms[:, :],
                                           ALU.mult, ALU.mult).then_inc(y_ready, 1)
            else:
                self_.wait()
                V.tensor_copy(dec[0:1, 0, 0:1], rms[0:1, 0:1]).then_inc(y_ready, KD)


def constants():
    a = np.arange(P)
    tok = DIL * a[:, None, None]
    keys = (DIL * a[None, :] + np.arange(DIL)[:, None]).reshape(-1)
    f = np.float32
    dist = (DIL * a[:, None, None] + np.arange(DIL)[None, :, None]) - keys[None, None, :]
    dist0 = np.where((dist >= 0) & (dist <= 128), dist, BIG).astype(f)
    d = a[:, None] - a[None, :]
    dist12 = np.stack([np.where(d >= 0, DIL * d, BIG), np.where((d >= 0) & (d % 4 == 0), DIL * d, BIG)], 1).astype(f)
    b, j, q = (v.reshape(-1, 1) for v in np.meshgrid(np.arange(NB), np.arange(2), np.arange(NS), indexing="ij"))
    cols = []
    for g, (win, dil) in enumerate(((128, 1), (512, 4), (2048, 16))):
        i = cached_keys(g)[None, :]
        dd = (128 if g == 0 else 256) + q - i
        cols.append(np.where((dd >= 0) & (dd % dil == 0) & (dd <= win), dd, BIG))
    kb, kq = (v.reshape(1, -1) for v in np.meshgrid(np.arange(NB), np.arange(NS), indexing="ij"))
    for g, dil in enumerate((1, 4, 16)):
        dd = q - kq
        cols.append(np.where((kb == b) & (dd >= 0) & (dd % dil == 0), dd, BIG))
    heads = np.arange(1, AG * AH + 1, dtype=np.float64)
    slopes = (-(2.0 ** (-8.0 * heads / (AG * AH)))).astype(f)
    sls = np.stack([slopes.reshape(AG, AH)[g, 2 * c + j[:, 0]] for c in range(PAIRS) for g in range(AG)], 1)
    s = np.arange(SMP)
    keep = np.ones(TOK, f)
    keep[0:SEQ:P] = 0
    keep[SEQ::NS] = 0
    return {
        "ones": np.ones((P, P), f), "ident": np.eye(P, dtype=f), "mask": np.triu(np.ones((P, P), f)),
        "mask_smp": (np.triu(np.ones((SMP, SMP))) * (s[:, None] // NS == s[None, :] // NS)).astype(f),
        "mask_block": (s[:, None] // NS == np.arange(NB)[None, :]).astype(f),
        "keep": np.tile(keep, (HEADS, 1)), "dist0": dist0, "dist12": dist12,
        "dist_smp": np.concatenate(cols, 1).astype(f), "slopes": np.tile(slopes, (P, 1)), "slopes_smp": sls.astype(f),
    }


def cached_keys(g):
    return np.arange((128, 256, 256)[g]) if g < 2 else np.flatnonzero(np.arange(256) % 16 < NS)


def laid_out(v):
    c = np.ascontiguousarray

    def feature_major(a):
        return a.T.reshape(-1, P, a.shape[0]).transpose(1, 0, 2)

    def per_feature(a):
        return a.reshape(-1, P).T

    def units(w):
        k, n = w.shape[0] // P, w.shape[1] // P
        return w.reshape(k, P, n, P).transpose(2, 1, 0, 3).reshape(n, P, k * P)

    x = np.concatenate([v["x_prompt"][0], v["x_sample"].reshape(SMP, D)])
    gains = np.concatenate([v["norm_w"].reshape(6, D), v["norm_f"][None]])
    w_in = []
    w_out = []
    for i in range(2):
        for j in range(2):
            u = units(v["w_ffn_in"][i, j])
            w_in.append(u.reshape(2, KF, P, UW).transpose(1, 0, 2, 3).reshape(2 * KF, P, UW))
            w_out.append(units(v["w_ffn_out"][i, j]).reshape(KD, P, 2, UF).transpose(0, 2, 1, 3))
    wi = v["ssm_w_in"][0]
    z, xbc, dt = units(wi[:, :DI]), units(wi[:, DI:DI + 4096]), wi[:, DI + 4096:]
    wo = v["ssm_w_out"][0].reshape(GROUPS, 2, P, KD, P).transpose(0, 3, 2, 1, 4)
    wo = wo.reshape(GROUPS, 2, 4, P, 2 * P).transpose(0, 1, 3, 2, 4).reshape(GROUPS, 2, P, UW)
    chunk_of = [[2 * g, 2 * g + 1, 16 + g, 24 + g] for g in range(GROUPS)]
    w_ssd = np.stack([np.concatenate([xbc[chunk_of[g]], z[2 * g:2 * g + 2], wo[g]]) for g in range(GROUPS)])
    dtp = np.zeros((D, P), np.float32)
    dtp[:, :HEADS] = dt
    conv = np.concatenate([v["ssm_conv_w"][0], v["ssm_conv_b"]]).reshape(CONV + 1, 32, P)[:, chunk_of]
    state = v["state_conv"][0].reshape(NB * (CONV - 1), 32, P)[:, chunk_of]
    wq = units(v["attn_w_qkv"][0]).reshape(AG, 3, PAIRS, P, UW).transpose(2, 0, 1, 3, 4).reshape(PAIRS, 9, P, UW)
    wq = wq[:, list(QKV_ORDER)]
    w_att = np.concatenate([wq, v["attn_w_o"][0].reshape(PAIRS, 1, P, D)], 1)
    kv = np.concatenate([v[f"cache_kv_g{g}"][0][:, cached_keys(g)] for g in range(AG)], 1)
    kv = kv.reshape(NB, KEYC, 2, PAIRS, P)
    out = {
        "xT": feature_major(x), "gains": per_feature(gains.reshape(-1)).reshape(P, 7, KD),
        "w_ffn_in": np.stack(w_in), "w_ffn_out": np.stack(w_out),
        "w_dt": units(dtp)[0], "w_ssd": w_ssd,
        "conv_w": conv.transpose(3, 1, 2, 0).reshape(P, GROUPS * 4 * (CONV + 1)),
        "conv_state": state.transpose(3, 1, 2, 0),
        "dt_bias": v["ssm_dt_bias"][0][:, None], "a_log": v["ssm_a_log"][0][:, None],
        "d_skip": np.repeat(v["ssm_d"][0].reshape(16, 2), PD, 1).T, "ssm_gain": per_feature(v["ssm_norm_w"][0]),
        "state": v["state_ssm"][0].reshape(NB, GROUPS, HPG * PD, NST).transpose(1, 3, 0, 2),
        "w_att": w_att,
        "k_cache": kv[:, :, 0].transpose(2, 3, 0, 1),
        "v_cache": kv[:, :, 1].reshape(NB, 4, P, PAIRS, P).transpose(3, 2, 0, 1, 4).reshape(PAIRS, P, NB * 4 * P),
    }
    return {k: c(a) for k, a in {**out, **constants()}.items()}


OUTPUTS = {
    "yT": (P, KD, TOK), "conv_new": (GROUPS, P, 4 * (NB + 1) * (CONV - 1)),
    "ssm_prompt": (GROUPS, P, HPG * PD), "ssm_sample": (GROUPS, P, NB, HPG * PD),
    "kv_new": (PAIRS, 2 * AG, P, TOK),
}


def returned(o):
    c = np.ascontiguousarray
    y = o["yT"].transpose(2, 1, 0).reshape(TOK, D)
    conv = o["conv_new"].reshape(GROUPS, P, 4, NB + 1, CONV - 1).transpose(3, 4, 0, 2, 1)
    conv = np.concatenate([conv[:, :, :, 0:2].reshape(NB + 1, 3, -1), conv[:, :, :, 2].reshape(NB + 1, 3, -1),
                           conv[:, :, :, 3].reshape(NB + 1, 3, -1)], 2)
    sp = o["ssm_prompt"].transpose(0, 2, 1).reshape(1, 1, HEADS, PD, NST)
    ss = o["ssm_sample"].transpose(2, 0, 3, 1).reshape(1, NB, HEADS, PD, NST)
    kv = o["kv_new"].reshape(PAIRS, AG, 2, 2, HD, TOK).transpose(1, 5, 2, 0, 3, 4).reshape(AG, TOK, 2, AH, HD)
    prompt = kv[:, :SEQ].reshape(AG, DIL, P, 2, AH, HD).transpose(0, 2, 1, 3, 4, 5).reshape(AG, SEQ, 2, AH, HD)
    sample = kv[:, SEQ:].reshape(AG, NB, NS, 2, AH, HD)
    out = [y[None, :SEQ], y[SEQ:].reshape(NB, NS, D), conv[None, :1], conv[None, 1:], sp, ss]
    for g, n in enumerate((128, SEQ, SEQ)):
        out += [prompt[g, SEQ - n:][None, None], sample[g][None]]
    return tuple(c(a) for a in out)


def kernel(**inputs):
    import concourse.bacc as bacc
    from concourse.bass_utils import run_bass_kernel_spmd

    nc = bacc.Bacc("TRN2", target_bir_lowering=False, num_devices=1)
    arrays = laid_out({k: np.asarray(a) for k, a in inputs.items()})
    io = {k: nc.dram_tensor(k, a.shape, mybir.dt.from_np(a.dtype), kind="ExternalInput").ap() for k, a in arrays.items()}
    for k, shape in OUTPUTS.items():
        io[k] = nc.dram_tensor(k, shape, F32, kind="ExternalOutput").ap()
    step_kernel(nc, io)
    r = run_bass_kernel_spmd(nc, [arrays], core_ids=[0])
    return returned(r.results[0])
```

```python
from contextlib import ExitStack, contextmanager

import numpy as np

import concourse.bass as bass
from concourse import mybir

F32 = mybir.dt.float32
F32R = mybir.dt.float32r
ALU = mybir.AluOpType
ACT = mybir.ActivationFunctionType
AX = mybir.AxisListType

P = 128
D = 1024
KD = D // P
SEQ, NB, NS = 512, 8, 8
SMP = NB * NS
TOK = SEQ + SMP
HALF = TOK // 2
QTR = SEQ // 2
FF = 2816
KF = FF // P
EPS = 1e-6
HEADS, GROUPS, HPG, PD, NST = 32, 8, 4, 64, 128
DI = HEADS * PD
H2 = 2 * HEADS
CH = SEQ // P
CONV = 4
XW = CONV - 1 + SEQ + NB * (CONV - 1 + NS)
XO = XW - (CONV - 1)
XS = CONV - 1 + SEQ
SW = CONV - 1 + NS
UW = 8 * P
UF = KF // 2 * P
AG, AH, HD, DIL = 3, 8, 64, 4
PAIRS = AH // 2
KEYC = 512
KEYR = ((0, 128), (128, 256), (384, 128))
BIG = 1e30

FFN_UNITS = 2 * KF + 2 * KD
U_SSD = FFN_UNITS
U_GRP = U_SSD + 1
U_FFN1 = U_SSD + 1 + 8 * GROUPS
U_ATT = U_FFN1 + 2 * FFN_UNITS
U_FFN = (0, U_FFN1, U_FFN1 + FFN_UNITS, U_ATT + 10 * PAIRS)
NORM_OF_FFN = (0, 2, 3, 5)
SSD_DVE_STEPS = 19
ATT_DVE_STEPS = 28
QKV_ORDER = (2, 5, 8, 0, 1, 3, 4, 6, 7)
AHEAD = 3


class Steps:

    def __init__(self, eng, sem):
        self.eng, self.sem, self.base, self.n = eng, sem, 0, 0

    def done(self, ins):
        ins.then_inc(self.sem, 1)
        self.n += 1

    def wait(self):
        self.eng.wait_ge(self.sem, self.base + self.n)

    @contextmanager
    def loop(self, first, last, per):
        start, self.n = self.n, 0
        with self.eng.Fori(first, last) as i:
            self.base = (i - first) * per + start
            yield i
        assert self.n == per, f"{self.n} signals in a turn, not {per}"
        self.base, self.n = 0, start + (last - first) * per


def step_kernel(nc, io):
    with ExitStack() as ctx:
        def sb(name, shape, dt=F32):
            return ctx.enter_context(nc.sbuf_tensor("sb_" + name, shape, dt))

        def sem(name):
            return ctx.enter_context(nc.semaphore(name))

        x = sb("x", [P, KD, TOK])
        uh = sb("uh", [P, KD, TOK], F32R)
        ul = sb("ul", [P, KD, TOK], F32R)
        raw = sb("raw", [P, 2, UF])
        wh = sb("wh", [P, 2, UF], F32R)
        wl = sb("wl", [P, 2, UF], F32R)
        rms = sb("rms", [P, TOK])
        ssq = sb("ssq", [P, TOK])
        sqx = sb("sqx", [P, TOK])
        sq2 = rms
        ones = sb("ones", [P, P])
        ident = sb("ident", [P, P])
        gains = sb("gains", [P, 7, KD])
        ps = ctx.enter_context(nc.psum_tensor("ps", [P, 8, 512], F32))

        with ExitStack() as region:
            def at(name, shape, dt=F32):
                return region.enter_context(nc.sbuf_tensor("sb_" + name, shape, dt))
            hh = at("hh", [P, KF, TOK], F32R)
            hl = at("hl", [P, KF, TOK], F32R)
            gate = at("gate", [P, TOK])
            up = at("up", [P, TOK])
        with ExitStack() as region:
            xp = at("xp", [P, 4, SEQ + (NB + 1) * SW + 1])
            acc = at("acc", [P, 2, XW + 1])
            xc = at("xc", [P, 4, TOK])
            zs = at("zs", [P, 2, TOK])
            er = at("er", [P, HPG * SEQ])
            ers = at("ers", [P, HPG * SMP])
            sg = at("sg", [P, HPG * SEQ])
            sgs = at("sgs", [SMP, HPG, SMP])
            xd = at("xd", [P, CH, HPG, PD])
            xds = at("xds", [SMP, HPG, PD])
            xw = at("xw", [P, CH, HPG, PD])
            xws = at("xws", [SMP, HPG, PD])
            bt = at("bt", [P, SEQ])
            bd = at("bd", [SMP, NB, NST])
            cbm = at("cbm", [P, SEQ])
            cbs = at("cbs", [SMP, SMP])
            hst = at("hst", [P, CH, HPG * PD])
            h0 = at("h0", [P, NB, HPG * PD])
            ysb = at("ysb", [P, 2, TOK])
            yof = at("yof", [P, 2, SMP])
            gh = at("gh", [P, 2, TOK], F32R)
            gl = at("gl", [P, 2, TOK], F32R)
            gr = at("gr", [P, TOK])
            keep = gr[0:H2, :]
            acT = at("acT", [H2, TOK])
            acm = at("acm", [H2, HPG, TOK], F32R)
            onr = at("onr", [H2, P], F32R)
            sel = at("sel", [H2, HEADS])
            tok = at("tok", [P, 3, CH + 1, HEADS])
            gtok = at("gtok", [P, 3, CH + 1, HPG])
            dec = at("dec", [P, HPG, CH])
            decs = at("decs", [P, HPG, NB])
            ncv = at("ncv", [P, 4, NB + 1, CONV - 1])
            cst = at("cst", [P, GROUPS, 4, NB * (CONV - 1)])
            cw = at("cw", [P, GROUPS * 4 * (CONV + 1)])
            dsk = at("dsk", [P, GROUPS * 2])
            ng = at("ng", [P, GROUPS * 2])
            dtb = at("dtb", [H2, 1])
            alog = at("alog", [H2, 1])
            ea = at("ea", [H2, 1])
            mask = at("mask", [P, P])
            masks = at("masks", [SMP, SMP])
            maskb = at("maskb", [SMP, NB])
        with ExitStack() as region:
            qkv = at("qkv", [P, 9, TOK])
            vt = at("vt", [P, AG, CH, P])
            vts = at("vts", [SMP, AG, P])
            pr = at("pr", [P, 2, 768])
            pt = at("pt", [P, 2, 768])
            un = at("un", [P, CH, P])
            oh = at("oh", [P, TOK], F32R)
            ol = at("ol", [P, TOK], F32R)
            kc = at("kc", [P, NB, KEYC])
            vc = at("vc", [P, NB, 4, P])
            qa = at("qa", [P, AG, P])
            qz = at("qz", [P, AG, NB * 32])
            so = at("so", [P, P])
            stage = at("stage", [P, AHEAD, TOK])
            prs = at("prs", [P, KEYC + AG * SMP])
            pts = at("pts", [P, 4, NB * 32])
            ptn = at("ptn", [SMP, AG, P])
            d0 = at("d0", [P, CH, SEQ])
            d12 = at("d12", [P, 2, P])
            dsm = at("dsm", [P, KEYC + AG * SMP])
            slp = at("slp", [P, AG * AH])
            sls = at("sls", [P, AG * PAIRS])
            nmx = at("nmx", [P, 16])
            den = at("den", [P, 16])
            rcp = at("rcp", [P, 16])
            rmp = sqx

        const_in = sem("const_in")
        x_in = [sem(f"x_in{i}") for i in range(4)]
        raw_in = [sem("raw_in0"), sem("raw_in1")]
        wh_done, wl_done, unit_done = sem("wh_done"), sem("wl_done"), sem("unit_done")
        x_done = sem("x_done")
        uh_done = sem("uh_done")
        sq_done = sem("sq_done")
        sq_used = sem("sq_used")
        u_ready = sem("u_ready")
        stat_mm, var_ready, sqrt_ready = sem("stat_mm"), sem("var_ready"), sem("sqrt_ready")
        rms_ready = sem("rms_ready")
        gate_scaled, silu_done, h_high, h_ready = sem("gate_scaled"), sem("silu_done"), sem("h_high"), sem("h_ready")
        dve_self = sem("dve_self")
        ssd_const, att_const = sem("ssd_const"), sem("att_const")
        dt_abs, dt_exp, ea_ready = sem("dt_abs"), sem("dt_exp"), sem("ea_ready")
        coef_in, coef_exp, dtok_in, dtok_mm = sem("coef_in"), sem("coef_exp"), sem("dtok_in"), sem("dtok_mm")
        state_in, cs_in, pj_evac, nc_ready = sem("state_in"), sem("cs_in"), sem("pj_evac"), sem("nc_ready")
        conv_done, xc_ready, zs_ready = sem("conv_done"), sem("xc_ready"), sem("zs_ready")
        acm_ready, rs_mm, r_mm = sem("acm_ready"), sem("rs_mm"), sem("r_mm")
        er_done, seg_done, ers_done, segs_done = sem("er_done"), sem("seg_done"), sem("ers_done"), sem("segs_done")
        e_done, es_done, dec_ready, cp_done = sem("e_done"), sem("es_done"), sem("dec_ready"), sem("cp_done")
        t_mm, xd_done, xs_done, bt_done = sem("t_mm"), sem("xd_done"), sem("xs_done"), sem("bt_done")
        cb_mm, cbm_done, w_done = sem("cb_mm"), sem("cbm_done"), sem("w_done")
        st_mm, hst_done, y_mm, y_evac = sem("st_mm"), sem("hst_done"), sem("y_mm"), sem("y_evac")
        hm_done, ss_mm, ss_evac = sem("hm_done"), sem("ss_mm"), sem("ss_evac")
        gsq_done, gn_mm, gvar_ready, gsqrt_ready = sem("gsq_done"), sem("gn_mm"), sem("gvar_ready"), sem("gsqrt_ready")
        gz_ready = sem("gz_ready")
        gsum_done = sem("gsum_done")
        gn_ready, gh_done, g_ready = sem("gn_ready"), sem("gh_done"), sem("g_ready")
        so_mm, so_evac = sem("so_mm"), sem("so_evac")
        st_h, st_hs, st_nc = sem("st_h"), sem("st_hs"), sem("st_nc")
        q_evac, vt_mm, vt_done = sem("q_evac"), sem("vt_mm"), sem("vt_done")
        qk_ready, sc_mm, max_done, exp_done = sem("qk_ready"), sem("sc_mm"), sem("max_done"), sem("exp_done")
        pt_mm, pt_done, pv_mm, un_done = sem("pt_mm"), sem("pt_done"), sem("pv_mm"), sem("un_done")
        ssc_mm, smax_done, sexp_done, snorm_done = sem("ssc_mm"), sem("smax_done"), sem("sexp_done"), sem("snorm_done")
        spt_mm, spt_done, spv_mm = sem("spt_mm"), sem("spt_done"), sem("spv_mm")
        ot_mm, oh_done, ol_done = sem("ot_mm"), sem("oh_done"), sem("ol_done")
        ao_mm, ao_evac, qa_zero = sem("ao_mm"), sem("ao_evac"), sem("qa_zero")
        st_v, st_k, kc_in, vc_in = sem("st_v"), sem("st_k"), sem("kc_in"), sem("vc_in")
        so_done, sot_mm, soh_done, sol_done = sem("so_done"), sem("sot_mm"), sem("soh_done"), sem("sol_done")
        y_ready, st_y = sem("y_ready"), sem("st_y")

        HALVES = ((0, HALF), (HALF, HALF))
        SPLIT = ((0, QTR), (QTR, TOK - QTR))
        last_norm = 6

        def one(i):
            return slice(i, i + 1) if isinstance(i, int) else bass.ds(i, 1)

        def smp(ap, q=NS):
            return ap.rearrange("p (b q) -> p b q", q=q)

        def two(ap):
            return ap.rearrange("p (h n) -> p h n", h=2)

        def perm(ap):
            return ap.rearrange("p (a t) -> p t a", t=DIL)

        def rows(c):
            return slice(c * P, (c + 1) * P)

        def score_bank(e, last):
            return 0 if last and e % 2 else 4

        block = ctx.enter_context(nc.Block())

        @block.sync
        def _(sp):
            def unit(u, parity, src, width):
                if not (isinstance(u, int) and u < 2):
                    sp.wait_ge(wl_done, u - 1)
                sp.dma_start(raw[:, parity, 0:width], src).then_inc(raw_in[parity], 16)

            def load(dst, src, signal):
                sp.dma_start(dst, src).then_inc(signal, 16)

            load(gains[:, :, :], io["gains"][:, :, :], const_in)
            for i in range(4):
                load(x[:, 2 * i:2 * i + 2, :], io["xT"][:, 2 * i:2 * i + 2, :], x_in[i])
                if i == 0:
                    unit(0, 0, io["w_ffn_in"][0, 0], UW)
            load(ones[:, :], io["ones"][:, :], const_in)
            load(ident[:, :], io["ident"][:, :], const_in)

            def ffn(f):
                u0 = U_FFN[f]
                def four(i, skip=0):
                    for k in range(skip, 4):
                        unit(i * 4 + (u0 + k), (u0 + k) % 2, io["w_ffn_in"][f, i * 4 + k], UW)

                four(0, 1 if f == 0 else 0)
                with sp.Fori(1, KF // 2) as i:
                    four(i)
                with sp.Fori(0, KD) as m:
                    for k in range(2):
                        u = u0 + 2 * KF + k
                        unit(m * 2 + u, u % 2, io["w_ffn_out"][f, m, k], UF)

            def ssd():
                unit(U_SSD, U_SSD % 2, io["w_dt"][:, :], UW)
                unit(U_GRP, U_GRP % 2, io["w_ssd"][0, 0], UW)
                sp.wait_ge(unit_done, U_SSD)
                for dst, name in ((cst, "conv_state"), (cw, "conv_w"), (dsk, "d_skip"), (ng, "ssm_gain"),
                                  (dtb, "dt_bias"), (alog, "a_log"), (mask, "mask"), (masks, "mask_smp"),
                                  (maskb, "mask_block"), (keep, "keep"), (sel, "one_head")):
                    ap = dst[:, :, :, :] if len(dst.shape) == 4 else dst[:, :]
                    src = io[name][:, :, :, :] if len(dst.shape) == 4 else io[name][:, :]
                    load(ap, src, ssd_const)
                for k in range(1, 6):
                    unit(U_GRP + k, (U_GRP + k) % 2, io["w_ssd"][0, k], UW)
                load(h0[:, :, :], io["state"][0], state_in)

                def stores(g):
                    sp.wait_ge(hst_done, g + 1)
                    sp.dma_start(io["ssm_prompt"][g], hst[:, CH - 1, :]).then_inc(st_h, 16)
                    sp.wait_ge(ss_evac, g * 4 + 4)
                    sp.dma_start(io["ssm_sample"][g], h0[:, :, :]).then_inc(st_hs, 16)

                def store_conv(g):
                    sp.wait_ge(nc_ready, g + 1 + 1)
                    sp.dma_start(io["conv_new"][g], ncv[:, :, :, :].rearrange("p t b k -> p (t b k)")).then_inc(st_nc, 16)

                store_conv(0)
                with sp.Fori(0, GROUPS - 1) as g:
                    for k in range(8):
                        u = U_GRP + 6 + k
                        unit(g * 8 + u, u % 2, io["w_ssd"][g + 1, k] if k < 6 else io["w_ssd"][g, k], UW)
                        if k == 6:
                            stores(g)
                    store_conv(g + 1)
                    sp.wait_ge(st_hs, g * 16 + 32)
                    load(h0[:, :, :], io["state"][g + 1], state_in)
                for k in range(2):
                    u = U_GRP + 8 * GROUPS - 2 + k
                    unit(u, u % 2, io["w_ssd"][GROUPS - 1, 6 + k], UW)
                stores(GROUPS - 1)

            def attention():
                def load_k(c, i):
                    load(kc[:, 2 * i:2 * i + 2, :], io["k_cache"][c, :, 2 * i:2 * i + 2, :], kc_in)

                def load_v(c, i):
                    load(vc[:, 4 * i:4 * i + 4, :, :].rearrange("p b k f -> p (b k f)"),
                         io["v_cache"][c, :, i * NB * KEYC // 2:(i + 1) * NB * KEYC // 2], vc_in)

                def store_v(c):
                    for g in range(AG):
                        sp.dma_start(io["kv_new"][c, g * 2 + 1], qkv[:, 3 * g + 2, :]).then_inc(st_v, 16)

                def store_k(c):
                    sp.wait_ge(qk_ready, c + 1)
                    for g in range(AG):
                        sp.dma_start(io["kv_new"][c, g * 2], qkv[:, 3 * g + 1, :]).then_inc(st_k, 16)

                for k in range(2):
                    unit(U_ATT + k, (U_ATT + k) % 2, io["w_att"][0, k], UW)
                sp.wait_ge(unit_done, U_ATT)
                for dst, name in ((slp, "slopes"), (sls, "slopes_smp"), (dsm, "dist_smp")):
                    load(dst[:, :], io[name][:, :], att_const)
                load(d12[:, :, :], io["dist12"][:, :, :], att_const)
                load(d0[:, :, :], io["dist0"][:, :, :], att_const)
                for k in range(2, 9):
                    unit(U_ATT + k, (U_ATT + k) % 2, io["w_att"][0, k], UW)
                    if k < 6:
                        load_k(0, k - 2)
                    elif k < 8:
                        load_v(0, k - 6)
                sp.wait_ge(q_evac, 3)
                store_v(0)
                with sp.Fori(0, PAIRS - 1) as c:
                    for k in range(10):
                        u = U_ATT + 9 + k
                        unit(c * 10 + u, u % 2, io["w_att"][c + 1, k] if k < 9 else io["w_att"][c, k], UW)
                        if k == 1:
                            store_k(c)
                        if k == 2:
                            sp.wait_ge(ssc_mm, c + 1)
                        if 2 <= k < 6:
                            load_k(c + 1, k - 2)
                        if k == 6:
                            sp.wait_ge(q_evac, c * 9 + 12)
                            store_v(c + 1)
                        if k == 8:
                            sp.wait_ge(spv_mm, c + 1)
                            load_v(c + 1, 0)
                        if k == 9:
                            load_v(c + 1, 1)
                u = U_FFN[3] - 1
                unit(u, u % 2, io["w_att"][PAIRS - 1, 9], UW)
                store_k(PAIRS - 1)

            ffn(0)
            ssd()
            ffn(1)
            ffn(2)
            attention()
            ffn(3)
            for m in range(KD):
                sp.wait_ge(y_ready, m + 1)
                sp.dma_start(io["yT"][:, m, :], x[:, m, :]).then_inc(st_y, 16)
            sp.wait_ge(st_y, 16 * KD)
            sp.wait_ge(st_h, 16 * GROUPS + 16)
            sp.wait_ge(st_hs, 16 * GROUPS + 16)
            sp.wait_ge(st_nc, 16 * GROUPS + 16)
            sp.wait_ge(st_v, 16 * PAIRS * AG)
            sp.wait_ge(st_k, 16 * PAIRS * AG)

        @block.gpsimd
        def _(pool):
            def low_part(u, parity, width):
                pool.wait_ge(wh_done, u + 1)
                pool.tensor_tensor(wl[:, parity, 0:width], raw[:, parity, 0:width],
                                   wh[:, parity, 0:width].bitcast(F32), ALU.subtract).then_inc(wl_done, 1)

            def ffn(f):
                u0 = U_FFN[f]
                with pool.Fori(0, KF // 2) as i:
                    for k in range(4):
                        low_part(i * 4 + (u0 + k), (u0 + k) % 2, UW)
                with pool.Fori(0, KD) as m:
                    for k in range(2):
                        u = u0 + 2 * KF + k
                        low_part(m * 2 + u, u % 2, UF)

            def ssd():
                low_part(U_SSD, U_SSD % 2, UW)
                pool.wait_ge(ssd_const, 176)
                for t in range(4):
                    pool.memset(xp[:, t, 0:CONV - 1], 0.0)

                def conv_state(g):
                    pool.wait_ge(conv_done, g * 4 + 1)
                    for t in range(4):
                        dst = xp[:, t, XS:XS + NB * SW].rearrange("p (b s) -> p b s", s=SW)[:, :, 0:CONV - 1]
                        src = cst[:, g, t, :].rearrange("p (b s) -> p b s", s=CONV - 1)
                        pool.tensor_copy(dst, src).then_inc(cs_in, 1)

                def new_conv_state(g, low):
                    pool.wait_ge(pj_evac, g * 6 + 4)
                    pool.wait_ge(st_nc, g * 16 + 16)
                    low()
                    for t in range(4):
                        src = xp[:, t, SEQ:SEQ + (NB + 1) * SW].rearrange("p (b s) -> p b s", s=SW)[:, :, 0:CONV - 1]
                        ins = pool.tensor_copy(ncv[:, t, :, :], src)
                    ins.then_inc(nc_ready, 1)

                def part(g, k):
                    u = U_GRP + 6 + k
                    low_part(g * 8 + u, u % 2, UW)

                def group(g, last):
                    if not last:
                        conv_state(g + 1)
                        for k in range(1, 3):
                            part(g, k)
                    pool.wait_ge(dec_ready, g + 1)
                    pool.wait_ge(xc_ready, g * 4 + 4)
                    for j in range(HPG):
                        e = er[:, j * SEQ:(j + 1) * SEQ]
                        pool.tensor_tensor(e, e, xc[:, 3, 0:SEQ], ALU.mult).then_inc(cp_done, 1)
                    if not last:
                        for k in range(3, 5):
                            part(g, k)
                    pool.wait_ge(y_mm, g * 2 + 2)
                    for b in range(NB):
                        hv = h0[:, b, :].rearrange("p (j d) -> p j d", j=HPG)
                        dv = decs[:, :, b:b + 1].broadcast_to([P, HPG, PD])
                        pool.tensor_tensor(hv, hv, dv, ALU.mult).then_inc(hm_done, 1)
                    if not last:
                        new_conv_state(g + 1, lambda: part(g, 5))
                        for k in range(6, 9):
                            part(g, k)
                    else:
                        low_part(U_FFN1 - 1, (U_FFN1 - 1) % 2, UW)

                conv_state(0)
                for k in range(5):
                    low_part(U_GRP + k, (U_GRP + k) % 2, UW)
                new_conv_state(0, lambda: low_part(U_GRP + 5, (U_GRP + 5) % 2, UW))
                low_part(U_GRP + 6, (U_GRP + 6) % 2, UW)
                with pool.Fori(0, GROUPS - 1) as g:
                    group(g, False)
                group(GROUPS - 1, True)

            def attention():
                for k in range(9):
                    low_part(U_ATT + k, (U_ATT + k) % 2, UW)
                    if k == 1:
                        pool.wait_ge(att_const, 80)
                        pool.memset(qz[:, :, :].rearrange("p g r -> p (g r)"), 0.0)
                        pool.memset(pts[:, :, :].rearrange("p g r -> p (g r)"), 0.0)
                        pool.memset(qa[:, :, :].rearrange("p g r -> p (g r)"), 0.0).then_inc(qa_zero, 1)
                with pool.Fori(0, PAIRS - 1) as c:
                    for k in range(10):
                        u = U_ATT + 9 + k
                        low_part(c * 10 + u, u % 2, UW)
                low_part(U_FFN[3] - 1, (U_FFN[3] - 1) % 2, UW)

            ffn(0)
            ssd()
            ffn(1)
            ffn(2)
            attention()
            ffn(3)

        @block.scalar
        def _(act):
            def high_part(i, per, u, width):
                act.wait_ge(raw_in[u % 2], i * (8 * per) + 16 * (u // 2 + 1))
                if not isinstance(i, int) or u + per * i >= 2:
                    act.wait_ge(unit_done, i * per + (u - 1))
                nc.scalar.copy(wh[:, u % 2, 0:width], raw[:, u % 2, 0:width]).then_inc(wh_done, 1)

            def stat(n):
                act.wait_ge(var_ready, n + 1)
                nc.scalar.activation(rms[:, :], rms[:, :], ACT.Sqrt).then_inc(sqrt_ready, 1)

            def high_u(n, m):
                if n == 4:
                    dst = uh[:, m, 0:SEQ].rearrange("p (t a) -> p t a", t=DIL)
                    nc.scalar.activation(dst, perm(x[:, m, 0:SEQ]), ACT.Copy, scale=gains[:, n, one(m)])
                    nc.scalar.activation(uh[:, m, SEQ:TOK], x[:, m, SEQ:TOK], ACT.Copy,
                                         scale=gains[:, n, one(m)]).then_inc(uh_done, 1)
                elif n != last_norm:
                    nc.scalar.activation(uh[:, m, :], x[:, m, :], ACT.Copy, scale=gains[:, n, one(m)]).then_inc(uh_done, 1)

            def square(m, dst):
                nc.scalar.activation(dst[:, :], x[:, m, :], ACT.Square).then_inc(sq_done, 1)

            def squares(n, u):
                for m in range(KD):
                    if m == 1:
                        high_part(0, 4, u, UW)
                    act.wait_ge(sq_used, 8 * n + max(m, 1))
                    square(m, (sqx, sq2)[m % 2])

            def ffn(f, next_n):
                u0 = U_FFN[f]

                def pairs(i, first, last):
                    for p in range(2):
                        if not first or (p == 0 and f == 2):
                            high_part(i, 4, u0 + 2 * p + 1, UW)
                        high_part(i, 4, u0 + 2 * p + 2, UF if last and p == 1 else UW)
                        if first and p == 0:
                            stat(NORM_OF_FFN[f])
                            high_part(i, 4, u0 + 3, UW)
                        act.wait_ge(gate_scaled, i * 2 + (KF * f + p + 1))
                        nc.scalar.activation(gate[:, :], gate[:, :], ACT.Silu).then_inc(silu_done, 1)

                pairs(0, True, False)
                with act.Fori(1, KF // 2 - 1) as i:
                    pairs(i, False, False)
                pairs(KF // 2 - 1, False, True)

                def outs(m, last):
                    u = u0 + 2 * KF
                    high_part(m, 2, u + 1, UF)
                    if not last or f < 3:
                        high_part(m, 2, u + 2, UW if last else UF)
                    act.wait_ge(x_done, m + (8 * f + 2) + 1)
                    act.wait_ge(sq_used, m + (8 * next_n + 1))
                    high_u(next_n, m)
                    square(m, sqx)

                with act.Fori(0, KD - 1) as m:
                    outs(m, False)
                outs(KD - 1, True)

            def ssd():
                high_part(0, 8, U_SSD + 1, UW)
                stat(1)
                act.wait_ge(ssd_const, 176)
                nc.scalar.activation(ea[:, :], alog[:, :], ACT.Exp).then_inc(ea_ready, 1)
                t1, t2 = er[0:H2, TOK:2 * TOK], er[0:H2, 2 * TOK:3 * TOK]

                def conv_out(g, k):
                    act.wait_ge(conv_done, g * 4 + (k + 1) + 1)
                    bias = cw[:, one(g * 20 + (k * 5 + 4))]
                    nc.scalar.activation(xc[:, k, 0:SEQ], acc[:, k % 2, 0:SEQ], ACT.Silu, bias=bias)
                    nc.scalar.activation(smp(xc[:, k, SEQ:TOK]), smp(acc[:, k % 2, XS:XW], SW)[:, :, 0:NS],
                                         ACT.Silu, bias=bias).then_inc(xc_ready, 1)

                def gate_out(g, k):
                    act.wait_ge(pj_evac, g * 6 + (k + 5))
                    nc.scalar.activation(zs[:, k, :], zs[:, k, :], ACT.Silu).then_inc(zs_ready, 1)

                def part(g, k):
                    high_part(g, 8, U_GRP + 6 + k, UW)

                def group(g, last):
                    if last:
                        high_part(0, 8, U_FFN1 - 1, UW)
                    else:
                        part(g, 1)
                    def exp_cum(j):
                        act.wait_ge(seg_done, g * 4 + (j + 1))
                        nc.scalar.activation(er[:, j * SEQ:(j + 1) * SEQ], ps[:, 4 + j, :],
                                             ACT.Exp).then_inc(er_done, 1)

                    def exp_seg(j):
                        e = sg[:, j * SEQ:(j + 1) * SEQ]
                        nc.scalar.activation(e, e, ACT.Exp).then_inc(e_done, 1)

                    for j in range(HPG):
                        exp_cum(j)
                    for j in range(HPG):
                        exp_seg(j)
                    act.wait_ge(segs_done, g + 1)
                    nc.scalar.activation(ers[:, :], ps[:, 4, 0:HPG * SMP], ACT.Exp).then_inc(ers_done, 1)
                    s2 = sgs[:, :, :].rearrange("p j q -> p (j q)")
                    nc.scalar.activation(s2, s2, ACT.Exp).then_inc(es_done, 1)
                    if not last:
                        part(g, 2)
                    act.wait_ge(t_mm, g * 4 + 3)
                    nc.scalar.copy(bt[:, :], ps[:, 7, :]).then_inc(bt_done, 1)
                    if not last:
                        part(g, 3)
                        part(g, 4)
                    for i in range(2):
                        act.wait_ge(gz_ready, g * 2 + (i + 1))
                        nc.scalar.activation(zs[:, i, :], ysb[:, i, :], ACT.Square).then_inc(gsq_done, 1)
                    if not last:
                        conv_out(g + 1, 0)
                        conv_out(g + 1, 1)
                        part(g, 5)
                    act.wait_ge(gvar_ready, g + 1)
                    nc.scalar.activation(gr[:, :], gr[:, :], ACT.Sqrt).then_inc(gsqrt_ready, 1)
                    if not last:
                        part(g, 6)
                    for i in range(2):
                        act.wait_ge(gn_ready, g * 2 + (i + 1))
                        nc.scalar.copy(gh[:, i, :], ysb[:, i, :]).then_inc(gh_done, 1)
                    if not last:
                        gate_out(g + 1, 0)
                        part(g, 7)
                        conv_out(g + 1, 2)
                        gate_out(g + 1, 1)
                        part(g, 8)
                        conv_out(g + 1, 3)
                high_part(0, 8, U_GRP + 1, UW)
                act.wait_ge(dt_abs, 1)
                nc.scalar.activation(t1, t1, ACT.Exp, scale=-1.0).then_inc(dt_exp, 1)
                for k in range(1, 4):
                    high_part(0, 8, U_GRP + 1 + k, UW)
                act.wait_ge(coef_in, 1)
                nc.scalar.activation(t2, t2, ACT.Exp).then_inc(coef_exp, 1)
                conv_out(0, 0)
                high_part(0, 8, U_GRP + 5, UW)
                conv_out(0, 1)
                gate_out(0, 0)
                conv_out(0, 2)
                high_part(0, 8, U_GRP + 6, UW)
                gate_out(0, 1)
                conv_out(0, 3)
                with act.Fori(0, GROUPS - 1) as g:
                    group(g, False)
                group(GROUPS - 1, True)
                for m in range(KD):
                    act.wait_ge(so_evac, KD * (GROUPS - 1) + m + 2)
                    high_u(2, m)
                    if m == 3:
                        high_part(0, 8, U_FFN1, UW)
                squares(2, U_FFN[1] + 1)

            def attention():
                stat(4)
                for k in range(9):
                    high_part(0, 10, U_ATT + k + 1, UW)

                def turn(c, last):
                    def ahead(k):
                        high_part(c, 10, U_ATT + 9 + k, UW)

                    def v_out(g):
                        act.wait_ge(vt_mm, c * 4 + (g + 1))
                        nc.scalar.copy(vt[:, g, :, :].rearrange("p t f -> p (t f)"), ps[:, g, :]).then_inc(vt_done, 1)

                    def exps(e):
                        act.wait_ge(max_done, c * 8 + (e + 1))
                        nc.scalar.activation(pr[:, e % 2, :], pr[:, e % 2, :], ACT.Exp, bias=nmx[:, e:e + 1],
                                             accum_out=den[:, e:e + 1]).then_inc(exp_done, 1)

                    for g in range(AG):
                        v_out(g)
                    act.wait_ge(vt_mm, c * 4 + 4)
                    nc.scalar.copy(vts[:, :, :].rearrange("p g f -> p (g f)"), ps[0:SMP, 3, 0:AG * P]).then_inc(vt_done, 1)
                    exps(0)
                    def probs_out(e):
                        act.wait_ge(pt_mm, c * 8 + (e + 1))
                        if e >= 2:
                            act.wait_ge(pv_mm, c * 8 + (e - 1))
                        nc.scalar.copy(pt[:, e % 2, 0:512], ps[:, 6, :])
                        nc.scalar.copy(pt[:, e % 2, 512:768], ps[:, 7, 0:256]).then_inc(pt_done, 1)

                    def blocks_out(k0, n):
                        for s in range(2):
                            dst = pts[:, k0:k0 + n, :].rearrange("p k (c w) -> p (k c) w", w=64)[:, :, 48 * s:48 * s + 2 * NS]
                            src = ps[:, 3, 0:n * P].rearrange("p (c s i) -> p c s i", s=2, i=2 * NS)[:, :, s, :]
                            nc.scalar.copy(dst, src)

                    def sample_step(e):
                        if e == 1:
                            act.wait_ge(smax_done, c + 1)
                            nc.scalar.activation(prs[:, :], prs[:, :], ACT.Exp, bias=nmx[:, 8:9],
                                                 accum_out=den[:, 8:9]).then_inc(sexp_done, 1)
                        if e == 2:
                            act.wait_ge(spt_mm, c * 2 + 1)
                            blocks_out(0, 3)
                            nc.scalar.copy(ptn[:, 0, :], ps[0:SMP, 3, rows(3)]).then_inc(spt_done, 1)
                        if e == 3:
                            act.wait_ge(spt_mm, c * 2 + 2)
                            blocks_out(3, 1)
                            nc.scalar.copy(ptn[:, 1:3, :].rearrange("p g r -> p (g r)"),
                                           ps[0:SMP, 3, P:3 * P]).then_inc(spt_done, 1)
                        if e == 4:
                            act.wait_ge(spv_mm, c + 1)
                            nc.scalar.copy(so[:, :], ps[:, 3, 0:P]).then_inc(so_done, 1)
                        if e == 5:
                            act.wait_ge(sot_mm, c + 1)
                            for j in range(2):
                                r = slice(HD * j, HD * j + HD)
                                ins = nc.scalar.copy(smp(oh[r, SEQ:TOK]), smp(ps[r, 3, 0:P], 2 * NS)[:, :, j * NS:(j + 1) * NS])
                            ins.then_inc(soh_done, 1)

                    for e in range(8):
                        if last:
                            if e < 7:
                                exps(e + 1)
                            probs_out(e)
                            sample_step(e - 1)
                        else:
                            probs_out(e)
                            ahead(e + 1)
                            if e < 7:
                                exps(e + 1)
                            sample_step(e)
                    act.wait_ge(ot_mm, c + 1)
                    nc.scalar.copy(oh[:, 0:SEQ], ps[:, 3, :]).then_inc(oh_done, 1)
                    if last:
                        high_part(0, 10, U_FFN[3], UW)
                    else:
                        ahead(9)
                        ahead(10)

                with act.Fori(0, PAIRS - 1) as c:
                    turn(c, False)
                turn(PAIRS - 1, True)
                for m in range(KD):
                    act.wait_ge(ao_evac, KD * (PAIRS - 1) + m + 2)
                    high_u(5, m)
                squares(5, U_FFN[3] + 1)

            act.wait_ge(const_in, 16)
            for m in range(KD):
                act.wait_ge(x_in[m // 2], 16)
                high_u(0, m)
                if m == 0:
                    high_part(0, 4, 0, UW)
            act.wait_ge(x_done, 1 + 1)
            squares(0, 1)
            ffn(0, 1)
            ssd()
            ffn(1, 3)
            ffn(2, 4)
            attention()
            ffn(3, 6)
            stat(last_norm)

        @block.tensor
        def _(pe):
            def product(u, parity, nk, rh, rl, banks, split, first=True, last=True, chunk=None):
                pe.wait_ge(wh_done, u + 1)
                for k in range(nk):
                    if chunk is not None:
                        pe.wait_ge(u_ready, chunk + k + 1 + 1)
                    w = wh[:, parity, k * P:(k + 1) * P]
                    for b, (t0, n) in zip(banks, split):
                        pe.matmul(ps[:, b, 0:n], w, rh[:, k, t0:t0 + n], start=first and k == 0, stop=False)
                        pe.matmul(ps[:, b, 0:n], w, rl[:, k, t0:t0 + n], start=False, stop=False)
                pe.wait_ge(wl_done, u + 1)
                for k in range(nk):
                    w = wl[:, parity, k * P:(k + 1) * P]
                    for b, (t0, n) in zip(banks, split):
                        ins = pe.matmul(ps[:, b, 0:n], w, rh[:, k, t0:t0 + n], start=False,
                                        stop=last and k == nk - 1)
                ins.then_inc(unit_done, 1)

            def stat(n):
                pe.wait_ge(sq_used, 8 * n + KD + 1)
                for h, (t0, n) in enumerate(HALVES):
                    ins = pe.matmul(ps[:, 6 + h, 0:n], ones[:, :], ssq[:, t0:t0 + n], start=True, stop=True)
                ins.then_inc(stat_mm, 1)

            def ffn(f):
                u0, n = U_FFN[f], NORM_OF_FFN[f]

                def pairs(i, first):
                    for p in range(2):
                        for k in range(2):
                            if not first and k == 0:
                                pe.wait_ge(h_ready, i * 2 + (KF * f + p - 1) + 1)
                            if first and p == 1 and k == 1:
                                pe.wait_ge(var_ready, n + 1)
                            product(i * 4 + (u0 + 2 * p + k), (u0 + 2 * p + k) % 2, KD, uh, ul,
                                    (4 * p + 2 * k, 4 * p + 2 * k + 1), HALVES,
                                    chunk=8 * n if first and p == 0 and k == 0 else None)
                            if first and p == 0 and k == 1:
                                if f == 0:
                                    pe.wait_ge(const_in, 48)
                                stat(n)

                pairs(0, True)
                with pe.Fori(1, KF // 2) as i:
                    pairs(i, False)

                pe.wait_ge(h_ready, KF * (f + 1))
                with pe.Fori(0, KD // 2) as i:
                    for p in range(2):
                        pe.wait_ge(x_done, i * 2 + (8 * f + p) + 1)
                        for k in range(2):
                            if k == 1:
                                pe.wait_ge(h_ready, KF * (f + 1) + 1)
                            u = u0 + 2 * KF + 2 * p + k
                            r = slice(k * KF // 2, (k + 1) * KF // 2)
                            product(i * 4 + u, u % 2, KF // 2, hh[:, r, :], hl[:, r, :], (2 * p, 2 * p + 1), HALVES,
                                    first=k == 0, last=k == 1)

            def ssd():
                product(U_SSD, U_SSD % 2, KD, uh, ul, (4, 5), HALVES, chunk=8)
                stat(1)
                def project(g, k, u):
                    if k == 0:
                        pe.wait_ge(so_evac, (g - 1) * 8 + 1 if not isinstance(g, int) else 1)
                    if k >= 2:
                        pe.wait_ge(pj_evac, g * 6 + (k - 1))
                    product(u, (U_GRP + k) % 2, KD, uh, ul, (2 * (k % 2), 2 * (k % 2) + 1), SPLIT)

                def decays(g):
                    pe.wait_ge(acm_ready, g * 4 + 4)
                    for j in range(HPG):
                        pe.matmul(ps[:, 4 + j, :], onr[:, :], acm[:, j, 0:SEQ], start=True, stop=True).then_inc(r_mm, 1)

                def turn(g):
                    pe.wait_ge(er_done, g * 4 + 1)
                    pe.matmul(ps[:, 4, 0:HPG * SMP].rearrange("p (j q) -> p j q", j=HPG), onr[:, :], acm[:, :, SEQ:TOK],
                              start=True, stop=True).then_inc(rs_mm, 1)
                    for i in range(3):
                        pe.wait_ge(xc_ready, g * 4 + (i + 1))
                        pe.wait_ge(er_done, g * 4 + (i + 2))
                        if i == 2:
                            pe.wait_ge(ers_done, g + 1)
                        for c in range(CH):
                            ins = pe.transpose(ps[:, 5 + i, rows(c)], xc[:, i, rows(c)], ident[:, :])
                        ins.then_inc(t_mm, 1)
                    for i in range(3):
                        ins = pe.transpose(ps[0:SMP, 4, rows(i)], xc[:, i, SEQ:TOK], ident[:, :])
                    ins.then_inc(t_mm, 1)

                def chunk_sums(g):
                    pe.wait_ge(xc_ready, g * 4 + 4)
                    pe.wait_ge(xd_done, g * 2 + 1)
                    for c in range(CH):
                        pe.matmul(ps[:, 5, rows(c)], xc[:, 2, rows(c)], xc[:, 3, rows(c)], start=True, stop=True)
                    pe.wait_ge(xs_done, g + 1)
                    pe.matmul(ps[0:SMP, 4, 0:SMP], xc[:, 2, SEQ:TOK], xc[:, 3, SEQ:TOK],
                              start=True, stop=True).then_inc(cb_mm, 1)
                    pe.wait_ge(xd_done, g * 2 + 2)
                    pe.wait_ge(bt_done, g + 1)
                    for c in range(CH):
                        ins = pe.matmul(ps[:, 6 + c // 2, (c % 2) * 256:(c % 2) * 256 + 256], bt[:, rows(c)],
                                        xw[:, c, :, :].rearrange("p j d -> p (j d)"), start=True, stop=True)
                        if c % 2:
                            ins.then_inc(st_mm, 1)

                def outputs(g):
                    pe.wait_ge(w_done, g + 1)
                    pe.wait_ge(cp_done, g * 4 + 4)
                    pe.wait_ge(hst_done, g + 1)
                    pe.wait_ge(state_in, g * 16 + 16)
                    for i in range(2):
                        for c in range(CH):
                            for jj in range(2):
                                j = 2 * i + jj
                                out = ps[PD * jj:PD * jj + PD, 5 + i, rows(c)]
                                pe.matmul(out, xd[:, c, j, :], sg[:, j * SEQ + c * P:j * SEQ + (c + 1) * P],
                                          start=True, stop=c == 0)
                                if c:
                                    pe.matmul(out, hst[:, c - 1, j * PD:(j + 1) * PD],
                                              er[:, j * SEQ + c * P:j * SEQ + (c + 1) * P], start=False, stop=True)
                        for jj in range(2):
                            j = 2 * i + jj
                            pe.matmul(ps[PD * jj:PD * jj + PD, 4, 2 * i * SMP:(2 * i + 1) * SMP], xds[:, j, :],
                                      sgs[:, j, :], start=True, stop=True)
                        for b in range(NB):
                            col = (2 * i + 1) * SMP + b * NS
                            ins = pe.matmul(ps[:, 4, col:col + NS], h0[:, b, i * P:(i + 1) * P],
                                            xc[:, 3, SEQ + b * NS:SEQ + (b + 1) * NS], start=True, stop=True)
                        ins.then_inc(y_mm, 1)

                def states(g, first, last):
                    for k in range(first, last):
                        bank = 7 - k % 2
                        if k == 1:
                            pe.wait_ge(y_evac, g * 2 + 2)
                        if k >= 2:
                            pe.wait_ge(ss_evac, g * 4 + k - 1)
                        for b in (2 * k, 2 * k + 1):
                            ins = pe.matmul(ps[:, bank, (b % 2) * 256:(b % 2) * 256 + 256], bd[:, b, :],
                                            xws[:, :, :].rearrange("p j d -> p (j d)"), start=True, stop=True)
                        ins.then_inc(ss_mm, 1)

                def group_sums(g):
                    pe.wait_ge(gsum_done, g + 1)
                    for h, (t0, n) in enumerate(HALVES):
                        ins = pe.matmul(ps[:, 4 + h, 0:n], ones[:, :], zs[:, 0, t0:t0 + n], start=True, stop=True)
                    ins.then_inc(gn_mm, 1)

                def project_out(g, u0, bank=0):
                    pe.wait_ge(g_ready, g * 2 + 2)
                    for m in range(KD):
                        u = u0 + m // 4
                        if m < 2:
                            pe.wait_ge(pj_evac, g * 6 + 11 + m if not isinstance(g, int) else 6 * GROUPS)
                        else:
                            pe.wait_ge(so_evac, g * 8 + (m - 1) + 1)
                        pe.wait_ge(wh_done, u + 1)
                        pe.wait_ge(wl_done, u + 1)
                        for k in range(2):
                            w = slice(((m % 4) * 2 + k) * P, ((m % 4) * 2 + k + 1) * P)
                            for h, (t0, n) in enumerate(SPLIT):
                                out = ps[:, bank + 2 * (m % 2) + h, 0:n]
                                pe.matmul(out, wh[:, (U_GRP + m // 4) % 2, w], gh[:, k, t0:t0 + n], start=k == 0, stop=False)
                                pe.matmul(out, wh[:, (U_GRP + m // 4) % 2, w], gl[:, k, t0:t0 + n], start=False, stop=False)
                                ins = pe.matmul(out, wl[:, (U_GRP + m // 4) % 2, w], gh[:, k, t0:t0 + n], start=False, stop=k == 1)
                        ins.then_inc(unit_done if m % 4 == 3 else so_mm, 1)

                for k in range(6):
                    project(0, k, U_GRP + k)
                pe.wait_ge(dtok_in, 1)
                srcs = (acT[0:HEADS, :], er[0:HEADS, 0:TOK], er[0:HEADS, 2 * TOK:3 * TOK])
                for q, src in enumerate(srcs):
                    for c in range(CH + 1):
                        n = P if c < CH else SMP
                        col = (q * (CH + 1) + c) * HEADS
                        ins = pe.transpose(ps[0:n, 4, col:col + HEADS], src[:, c * P:c * P + n], ident[0:HEADS, 0:HEADS])
                ins.then_inc(dtok_mm, 1)
                with pe.Fori(0, GROUPS - 1) as g:
                    def ahead(k):
                        project(g + 1, k, g * 8 + (U_GRP + 6 + k))

                    decays(g)
                    ahead(0)
                    turn(g)
                    ahead(1)
                    chunk_sums(g)
                    ahead(2)
                    outputs(g)
                    ahead(3)
                    states(g, 0, 2)
                    group_sums(g)
                    ahead(4)
                    states(g, 2, 4)
                    ahead(5)
                    project_out(g, g * 8 + (U_GRP + 12))
                g = GROUPS - 1
                for stage in (decays, turn, chunk_sums, outputs):
                    stage(g)
                states(g, 0, 2)
                group_sums(g)
                states(g, 2, 4)
                project_out(g, U_FFN1 - 2, 4)

            def attention():
                pe.wait_ge(ao_evac, 1)
                for k in range(9):
                    if k >= 2:
                        pe.wait_ge(q_evac, k - 1)
                    product(U_ATT + k, (U_ATT + k) % 2, KD, uh, ul, (2 * (k % 2), 2 * (k % 2) + 1), SPLIT,
                            chunk=32 if k == 0 else None)
                    if k == 0:
                        stat(4)

                def turn(c, last):
                    def ahead(k):
                        u = U_ATT + 9 + k
                        product(c * 10 + u, u % 2, KD, uh, ul, (0, 1), SPLIT)

                    def scores(e):
                        t, r, bank = e // 2, slice(HD * (e % 2), HD * (e % 2) + HD), score_bank(e, last)
                        if e > int(last):
                            pe.wait_ge(max_done, c * 8 + e - last)
                        pe.matmul(ps[:, bank, :], qkv[r, 0, rows(t)], qkv[r, 1, 0:SEQ], start=True, stop=True)
                        if e == 1:
                            for g in range(AG):
                                pe.matmul(ps[:, bank + 1, 2 * P + g * SMP:2 * P + (g + 1) * SMP], qa[:, g, :],
                                          qkv[:, 3 * g + 1, SEQ:TOK], start=True, stop=True)
                        pe.matmul(ps[:, bank + 1, 0:P], qkv[r, 3, rows(t)], qkv[r, 4, rows(t)], start=True, stop=True)
                        pe.matmul(ps[:, bank + 1, P:2 * P], qkv[r, 6, rows(t)], qkv[r, 7, rows(t)],
                                  start=True, stop=True).then_inc(sc_mm, 1)

                    pe.wait_ge(q_evac, c * 9 + 9)
                    for g in range(AG):
                        for t in range(CH):
                            ins = pe.transpose(ps[:, g, rows(t)], qkv[:, 3 * g + 2, rows(t)], ident[:, :])
                        ins.then_inc(vt_mm, 1)
                    for g in range(AG):
                        ins = pe.transpose(ps[0:SMP, 3, rows(g)], qkv[:, 3 * g + 2, SEQ:TOK], ident[:, :])
                    ins.then_inc(vt_mm, 1)
                    def sample_scores():
                        pe.wait_ge(vt_done, c * 4 + 4)
                        pe.wait_ge(qk_ready, c + 1)
                        pe.wait_ge(kc_in, c * 64 + 64)
                        for b in range(NB):
                            for g, (k0, n) in enumerate(KEYR):
                                ins = pe.matmul(ps[32 * (b // 2):32 * (b // 2) + 32, 3, k0:k0 + n],
                                                qz[:, g, 32 * b:32 * b + 32], kc[:, b, k0:k0 + n],
                                                start=b % 2 == 0 and g == 0, stop=b % 2 == 1, skip_group_check=True)
                        ins.then_inc(ssc_mm, 1)

                    pe.wait_ge(ao_evac, c * 8 + 1)
                    scores(0)
                    if last:
                        pe.wait_ge(vt_done, c * 4 + 2)
                        pe.wait_ge(qk_ready, c + 1)
                        scores(1)
                    sample_scores()

                    def transposes(e):
                        pe.wait_ge(exp_done, c * 8 + (e + 1))
                        if e and last:
                            pe.wait_ge(pt_done, c * 8 + e)
                        for k in range(6):
                            ins = pe.transpose(ps[:, 6 + k // 4, rows(k % 4)], pr[:, e % 2, rows(k)], ident[:, :])
                        ins.then_inc(pt_mm, 1)

                    def values(e):
                        t, r = e // 2, slice(HD * (e % 2), HD * (e % 2) + HD)
                        if e == 0:
                            pe.wait_ge(vt_done, c * 4 + 4)
                        else:
                            pe.wait_ge(un_done, c * 8 + e)
                        pe.wait_ge(pt_done, c * 8 + (e + 1))
                        for k in range(6):
                            v = vt[:, max(0, k - 3), k if k < 4 else t, r]
                            ins = pe.matmul(ps[:, 2, 0:HD], pt[:, e % 2, rows(k)], v, start=k == 0, stop=k == 5)
                        ins.then_inc(pv_mm, 1)
                        if e == 2 or e == 3:
                            if e == 2:
                                pe.wait_ge(snorm_done, c + 1)
                            else:
                                pe.wait_ge(spt_done, c * 2 + 1)
                            blocks = (0, 1, 2, 4) if e == 2 else (3, 5, 6)
                            for i, k in enumerate(blocks):
                                if k < 4:
                                    ins = pe.transpose(ps[:, 3, rows(i)], prs[:, rows(k)], ident[:, :])
                                else:
                                    own = slice(KEYC + (k - 4) * SMP, KEYC + (k - 3) * SMP)
                                    ins = pe.transpose(ps[0:SMP, 3, rows(i)], prs[:, own], ident[:, :])
                            ins.then_inc(spt_mm, 1)
                        if e == 4:
                            pe.wait_ge(spt_done, c * 2 + 2)
                            pe.wait_ge(vc_in, c * 32 + 32)
                            for g in range(AG):
                                pe.matmul(ps[:, 3, 0:P], ptn[:, g, :], vts[:, g, :], start=g == 0, stop=False, skip_group_check=True)
                            for b in range(NB):
                                out = ps[32 * (b // 2):32 * (b // 2) + 32, 3, 0:P]
                                for k in range(4):
                                    ins = pe.matmul(out, pts[:, k, 32 * b:32 * b + 32], vc[:, b, k, :], start=False,
                                                    stop=b % 2 == 1 and k == 3, skip_group_check=True)
                            ins.then_inc(spv_mm, 1)
                        if e == 5:
                            pe.wait_ge(so_done, c + 1)
                            pe.transpose(ps[:, 3, 0:P], so[:, :], ident[:, :]).then_inc(sot_mm, 1)

                    if last:
                        for e in range(8):
                            transposes(e)
                            if e:
                                values(e - 1)
                            if e < 6:
                                scores(e + 2)
                        values(7)
                    else:
                        for e in range(8):
                            if e < 7:
                                scores(e + 1)
                            transposes(e)
                            if e == 0:
                                pe.wait_ge(vt_done, c * 4 + 2)
                            else:
                                pe.wait_ge(q_evac, c * 9 + (9 + e))
                            ahead(e)
                            values(e)
                    pe.wait_ge(sol_done, c + 1)
                    pe.wait_ge(un_done, c * 8 + 8)
                    for t in range(CH):
                        ins = pe.transpose(ps[:, 3, rows(t)], un[:, t, :], ident[:, :])
                    ins.then_inc(ot_mm, 1)
                    if not last:
                        pe.wait_ge(q_evac, c * 9 + 17)
                        ahead(8)
                    u = U_FFN[3] - 1 if last else c * 10 + (U_ATT + 18)
                    parity = (U_ATT + 18) % 2 if not last else u % 2
                    pe.wait_ge(wh_done, u + 1)
                    pe.wait_ge(wl_done, u + 1)
                    pe.wait_ge(ol_done, c + 1)
                    for m in range(KD):
                        if m >= 2:
                            pe.wait_ge(ao_evac, c * 8 + (m - 1) + 1)
                        for h, (t0, n) in enumerate(SPLIT):
                            out = ps[:, 4 + 2 * (m % 2) + h, 0:n]
                            pe.matmul(out, wh[:, parity, rows(m)], oh[:, t0:t0 + n], start=True, stop=False)
                            pe.matmul(out, wh[:, parity, rows(m)], ol[:, t0:t0 + n], start=False, stop=False)
                            ins = pe.matmul(out, wl[:, parity, rows(m)], oh[:, t0:t0 + n], start=False, stop=True)
                        ins.then_inc(unit_done if m == KD - 1 else ao_mm, 1)

                with pe.Fori(0, PAIRS - 1) as c:
                    turn(c, False)
                turn(PAIRS - 1, True)

            ffn(0)
            ssd()
            ffn(1)
            ffn(2)
            attention()
            ffn(3)
            stat(last_norm)

        @block.vector
        def _(dve):
            self_ = Steps(dve, dve_self)
            V = nc.vector

            def step(ins):
                self_.done(ins)
                self_.wait()

            def low_u(n, m):
                dve.wait_ge(uh_done, m + (8 * n + 1))
                g = gains[:, n, one(m)]
                if n == 4:
                    for v in ((lambda a: perm(a[:, m, 0:SEQ]), lambda a: a[:, m, 0:SEQ].rearrange("p (t a) -> p t a", t=DIL)),
                              (lambda a: a[:, m, SEQ:TOK],) * 2):
                        ins = V.scalar_tensor_tensor(v[1](ul), v[0](x), g, v[1](uh).bitcast(F32), ALU.mult, ALU.subtract)
                    ins.then_inc(u_ready, 1)
                else:
                    V.scalar_tensor_tensor(ul[:, m, :], x[:, m, :], g, uh[:, m, :].bitcast(F32),
                                           ALU.mult, ALU.subtract).then_inc(u_ready, 1)

            def add_square(n, m, src):
                dve.wait_ge(sq_done, m + (8 * n + 1))
                dve.wait_ge(sq_used, m + (8 * n + 1))
                V.tensor_tensor(ssq[:, :], ssq[:, :], src[:, :], ALU.add).then_inc(sq_used, 1)

            def add_squares(n):
                for m in range(KD):
                    add_square(n, m, (sqx, sq2)[m % 2])

            def stat(n):
                dve.wait_ge(stat_mm, n + 1)
                V.tensor_scalar(two(rms[:, :]), ps[:, 6:8, 0:HALF], 1.0 / D, EPS, ALU.mult, ALU.add).then_inc(var_ready, 1)
                V.memset(ssq[:, :], 0.0)
                dve.wait_ge(sqrt_ready, n + 1)
                V.reciprocal(rms[:, :], rms[:, :]).then_inc(rms_ready, 1)
                dve.wait_ge(rms_ready, n + 1)

            def ffn(f, next_n):
                u0 = U_FFN[f]
                stat(NORM_OF_FFN[f])
                with self_.loop(0, KF // 2, 4) as i:
                    for p in range(2):
                        u = u0 + 2 * p
                        dve.wait_ge(unit_done, i * 4 + (u + 1))
                        dve.wait_ge(h_ready, i * 2 + (KF * f + p) + 1)
                        V.tensor_tensor(two(gate[:, :]), ps[:, 4 * p:4 * p + 2, 0:HALF], two(rms[:, :]),
                                        ALU.mult).then_inc(gate_scaled, 1)
                        dve.wait_ge(unit_done, i * 4 + (u + 2))
                        step(V.tensor_tensor(two(up[:, :]), ps[:, 4 * p + 2:4 * p + 4, 0:HALF], two(rms[:, :]), ALU.mult))
                        dve.wait_ge(silu_done, i * 2 + (KF * f + p + 1))
                        step(V.tensor_tensor(up[:, :], up[:, :], gate[:, :], ALU.mult))
                        j = bass.ds(i * 2 + p, 1)
                        hi = hh[:, j, :].rearrange("p j t -> p (j t)")
                        lo = hl[:, j, :].rearrange("p j t -> p (j t)")
                        V.tensor_copy(hi, up[:, :]).then_inc(h_high, 1)
                        dve.wait_ge(h_high, i * 2 + (KF * f + p + 1))
                        V.tensor_tensor(lo, up[:, :], hi.bitcast(F32), ALU.subtract).then_inc(h_ready, 1)
                with dve.Fori(0, KD // 2) as i:
                    for p in range(2):
                        m = i * 2 + p
                        dve.wait_ge(unit_done, i * 4 + (u0 + 2 * KF + 2 * p + 2))
                        xm = x[:, bass.ds(m, 1), :].rearrange("p j (h n) -> p (j h) n", h=2)
                        V.scalar_tensor_tensor(xm, ps[:, 2 * p:2 * p + 2, 0:HALF], 0.5, xm,
                                               ALU.mult, ALU.add).then_inc(x_done, 1)
                        if next_n != last_norm:
                            low_u(next_n, m)
                        add_square(next_n, m, sqx)

            def ssd():
                t0, t1, t2 = (er[0:H2, k * TOK:(k + 1) * TOK] for k in range(3))
                t3, t4, t5 = (sg[0:H2, k * TOK:(k + 1) * TOK] for k in range(3))
                def raw_dt():
                    dve.wait_ge(ssd_const, 176)
                    step(V.tensor_tensor(two(t0), ps[0:H2, 4:6, 0:HALF], two(rms[0:H2, :]), ALU.mult))
                    step(V.tensor_scalar(t0, t0, dtb[:, 0:1], None, ALU.add))
                    V.scalar_tensor_tensor(t1, t0, -1.0, t0, ALU.mult, ALU.max).then_inc(dt_abs, 1)
                    V.memset(tok[:, :, :, :].rearrange("p q c h -> p (q c h)"), 0.0)
                    V.tensor_copy(onr[:, :], ones[0:H2, :])
                    dve.wait_ge(dt_exp, 1)
                    step(V.tensor_scalar(t2, t1, 2.0, None, ALU.add))
                    step(V.reciprocal(t2, t2))

                def log_series():
                    step(V.tensor_tensor(t3, t1, t2, ALU.mult))
                    step(V.tensor_tensor(t4, t3, t3, ALU.mult))
                    step(V.tensor_scalar(t5, t4, 1.0 / 17, None, ALU.mult))
                    for k in range(7, 0, -1):
                        step(V.scalar_tensor_tensor(t5, t5, 1.0 / (2 * k + 1), t4, ALU.add, ALU.mult))

                def dt_and_sums():
                    step(V.scalar_tensor_tensor(t5, t5, 1.0, t3, ALU.add, ALU.mult))
                    step(V.tensor_scalar(t0, t0, 0.0, None, ALU.max))
                    step(V.scalar_tensor_tensor(t0, t5, 2.0, t0, ALU.mult, ALU.add))
                    dve.wait_ge(ea_ready, 1)
                    step(V.tensor_scalar(t3, t0, ea[:, 0:1], -1.0, ALU.mult, ALU.mult))
                    step(V.tensor_tensor_scan(acT[:, :], keep[:, :], t3, 0.0, ALU.mult, ALU.add))
                    for a, b, n in ((0, SEQ, P), (SEQ, TOK, NS)):
                        v, o = smp(acT[:, a:b], n), smp(t2[:, a:b], n)
                        ins = V.tensor_tensor(o, v[:, :, n - 1:n].broadcast_to([H2, (b - a) // n, n]), v, ALU.subtract)
                    ins.then_inc(coef_in, 1)

                def state_coefs():
                    dve.wait_ge(coef_exp, 1)
                    V.tensor_tensor(t2, t2, t0, ALU.mult).then_inc(dtok_in, 1)
                    hi = acm[:, 0, :]
                    step(V.tensor_copy(hi, acT[:, :]))
                    lo = acm[HEADS:H2, 0, :]
                    step(V.tensor_tensor(lo, acT[HEADS:H2, :], lo.bitcast(F32), ALU.subtract))

                def token_major():
                    dve.wait_ge(dtok_mm, 1)
                    v = ps[:, 4, 0:3 * (CH + 1) * HEADS].rearrange("p (q c h) -> p q c h", q=3, c=CH + 1)
                    V.tensor_copy(tok[:, :, 0:CH, :], v[:, :, 0:CH, :])
                    V.tensor_copy(tok[0:SMP, :, CH, :], v[0:SMP, :, CH, :])
                    step(V.tensor_copy(acT[:, :], acm[:, 0, :].bitcast(F32)))

                def conv_in(g, k, u):
                    dve.wait_ge(unit_done, u + 1)
                    b = 2 * (k % 2)
                    if k == 0:
                        dve.wait_ge(nc_ready, g + 1)
                    V.tensor_tensor(two(xp[:, k, CONV - 1:XS]), ps[:, b:b + 2, 0:QTR], two(rms[:, 0:SEQ]), ALU.mult)
                    V.tensor_tensor(smp(xp[:, k, XS:XW], SW)[:, :, CONV - 1:SW], smp(ps[:, b + 1, QTR:QTR + SMP]),
                                    smp(rms[:, SEQ:TOK]), ALU.mult).then_inc(pj_evac, 1)

                def conv(g, k, tap=None):
                    if not tap:
                        dve.wait_ge(pj_evac, g * 6 + (k + 1))
                        dve.wait_ge(cs_in, g * 4 + (k + 1))
                        if k >= 2:
                            dve.wait_ge(xc_ready, g * 4 + (k - 1))
                    out = acc[:, k % 2, 0:XO]
                    for t in range(CONV) if tap is None else (tap,):
                        w = cw[:, one(g * 20 + (k * 5 + t))]
                        if t == 0:
                            step(V.tensor_scalar(out, xp[:, k, 0:XO], w, None, ALU.mult))
                        else:
                            ins = V.scalar_tensor_tensor(out, xp[:, k, t:t + XO], w, out, ALU.mult, ALU.add)
                            if t < CONV - 1:
                                step(ins)
                            else:
                                ins.then_inc(conv_done, 1)

                def gate_in(g, k, u):
                    dve.wait_ge(unit_done, u + 1)
                    b = 2 * (k % 2)
                    V.tensor_tensor(two(zs[:, k, 0:SEQ]), ps[:, b:b + 2, 0:QTR], two(rms[:, 0:SEQ]), ALU.mult)
                    V.tensor_tensor(zs[:, k, SEQ:TOK], ps[:, b + 1, QTR:QTR + SMP], rms[:, SEQ:TOK],
                                    ALU.mult).then_inc(pj_evac, 1)

                def head_rows(g):
                    step(V.tensor_copy(gtok[:, :, :, :].rearrange("p q c j -> p (q c) j"),
                                       tok[:, :, :, bass.ds(g * HPG, HPG)].rearrange("p q c j -> p (q c) j")))
                    for j in range(HPG):
                        V.tensor_scalar(acm[:, j, :], acT[:, :], sel[:, one(g * HPG + j)], None,
                                        ALU.mult).then_inc(acm_ready, 1)

                def seg(g, j):
                    dve.wait_ge(r_mm, g * 4 + (j + 1))
                    for c in range(CH):
                        ins = V.tensor_scalar(sg[:, j * SEQ + c * P:j * SEQ + (c + 1) * P],
                                              ps[:, 4 + j, c * P:(c + 1) * P], gtok[:, 0, c, j:j + 1],
                                              0.0, ALU.subtract, ALU.min)
                    ins.then_inc(seg_done, 1)

                def group(g, last):
                    def ahead(k):
                        u = g * 8 + (U_GRP + 6 + k)
                        if k < 4:
                            conv_in(g + 1, k, u)
                        else:
                            gate_in(g + 1, k - 4, u)

                    for j in range(HPG):
                        seg(g, j)
                    if not last:
                        ahead(0)
                    dve.wait_ge(rs_mm, g + 1)
                    for j in range(HPG):
                        ins = V.tensor_scalar(sgs[:, j, :], ps[0:SMP, 4, j * SMP:(j + 1) * SMP], gtok[0:SMP, 0, CH, j:j + 1],
                                              0.0, ALU.subtract, ALU.min)
                    ins.then_inc(segs_done, 1)
                    if not last:
                        conv(g + 1, 0)
                    dve.wait_ge(er_done, g * 4 + 4)
                    V.tensor_copy(dec[:, :, :], er[:, :].rearrange("p (j c q) -> p j c q", j=HPG, c=CH)[:, :, :, P - 1])
                    dve.wait_ge(ers_done, g + 1)
                    V.tensor_copy(decs[:, :, :], ers[:, :].rearrange("p (j b q) -> p j b q", j=HPG, b=NB)[:, :, :, NS - 1]
                                  ).then_inc(dec_ready, 1)
                    for i in range(2):
                        dve.wait_ge(t_mm, g * 4 + (i + 1))
                        src = ps[:, 5 + i, :].rearrange("p (c d) -> p c d", c=CH)
                        for q, dst in ((1, xd), (2, xw)):
                            for jj in range(2):
                                j = 2 * i + jj
                                ins = V.tensor_tensor(dst[:, :, j, :], src[:, :, jj * PD:(jj + 1) * PD],
                                                      gtok[:, q, 0:CH, j:j + 1].broadcast_to([P, CH, PD]), ALU.mult)
                        ins.then_inc(xd_done, 1)
                    dve.wait_ge(t_mm, g * 4 + 4)
                    for q, dst in ((1, xds), (2, xws)):
                        V.tensor_tensor(dst[:, :, :], ps[0:SMP, 4, 0:2 * P].rearrange("p (j d) -> p j d", j=HPG),
                                        gtok[0:SMP, q, CH, :].unsqueeze(2).broadcast_to([SMP, HPG, PD]), ALU.mult)
                    V.tensor_tensor(bd[:, :, :], ps[0:SMP, 4, 2 * P:3 * P].unsqueeze(1).broadcast_to([SMP, NB, NST]),
                                    maskb[:, :].unsqueeze(2).broadcast_to([SMP, NB, NST]), ALU.mult).then_inc(xs_done, 1)
                    if not last:
                        ahead(1)
                    dve.wait_ge(cb_mm, g + 1)
                    V.tensor_tensor(cbs[:, :], ps[0:SMP, 4, 0:SMP], masks[:, :], ALU.mult)
                    V.tensor_tensor(cbm[:, :].rearrange("p (c q) -> p c q", c=CH), ps[:, 5, :].rearrange("p (c q) -> p c q", c=CH),
                                    mask[:, :].unsqueeze(1).broadcast_to([P, CH, P]), ALU.mult).then_inc(cbm_done, 1)
                    dve.wait_ge(cbm_done, g + 1)
                    for j in range(HPG):
                        dve.wait_ge(e_done, g * 4 + (j + 1))
                        e = sg[:, j * SEQ:(j + 1) * SEQ]
                        V.tensor_tensor(e, e, cbm[:, :], ALU.mult)
                    dve.wait_ge(es_done, g + 1)
                    V.tensor_tensor(sgs[:, :, :], sgs[:, :, :], cbs[:, :].unsqueeze(1).broadcast_to([SMP, HPG, SMP]),
                                    ALU.mult).then_inc(w_done, 1)
                    dve.wait_ge(st_mm, g * 2 + 1)
                    dve.wait_ge(st_h, g * 16 + 16)
                    step(V.tensor_copy(hst[:, 0, :], ps[:, 6, 0:256]))
                    for c in range(1, CH):
                        if c == 2:
                            dve.wait_ge(st_mm, g * 2 + 2)
                        for j in range(HPG):
                            d = slice(j * PD, (j + 1) * PD)
                            ins = V.scalar_tensor_tensor(hst[:, c, d], hst[:, c - 1, d], dec[:, j, c:c + 1],
                                                         ps[:, 6 + c // 2, (c % 2) * 256 + j * PD:(c % 2) * 256 + (j + 1) * PD],
                                                         ALU.mult, ALU.add)
                        if c < CH - 1:
                            step(ins)
                    ins.then_inc(hst_done, 1)
                    if not last:
                        conv(g + 1, 1)
                        ahead(2)
                        head_rows(g + 1)
                    for i in range(2):
                        dve.wait_ge(y_mm, g * 2 + 2)
                        dk = dsk[:, one(g * 2 + i)]
                        for jj in range(2):
                            r = slice(PD * jj, PD * jj + PD)
                            j = 2 * i + jj
                            V.tensor_tensor(yof[r, i, :], ps[r, 4, (2 * i + 1) * SMP:(2 * i + 2) * SMP],
                                            ers[r, j * SMP:(j + 1) * SMP], ALU.mult)
                        V.scalar_tensor_tensor(ysb[:, i, 0:SEQ], xc[:, i, 0:SEQ], dk, ps[:, 5 + i, :], ALU.mult, ALU.add)
                        ins = V.scalar_tensor_tensor(ysb[:, i, SEQ:TOK], xc[:, i, SEQ:TOK], dk,
                                                     ps[:, 4, 2 * i * SMP:(2 * i + 1) * SMP], ALU.mult, ALU.add)
                        ins.then_inc(y_evac, 1)
                        dve.wait_ge(y_evac, g * 2 + (i + 1))
                        step(V.tensor_tensor(ysb[:, i, SEQ:TOK], ysb[:, i, SEQ:TOK], yof[:, i, :], ALU.add))
                        dve.wait_ge(zs_ready, g * 2 + (i + 1))
                        V.tensor_tensor(ysb[:, i, :], ysb[:, i, :], zs[:, i, :], ALU.mult).then_inc(gz_ready, 1)
                    if not last:
                        ahead(3)

                    def sample_states(first, last):
                        for k in range(first, last):
                            dve.wait_ge(ss_mm, g * 4 + (k + 1))
                            dve.wait_ge(hm_done, g * 8 + (2 * k + 2))
                            V.tensor_tensor(h0[:, 2 * k:2 * k + 2, :], h0[:, 2 * k:2 * k + 2, :],
                                            two(ps[:, 7 - k % 2, :]), ALU.add).then_inc(ss_evac, 1)

                    dve.wait_ge(gsq_done, g * 2 + 2)
                    V.tensor_tensor(zs[:, 0, :], zs[:, 0, :], zs[:, 1, :], ALU.add).then_inc(gsum_done, 1)
                    sample_states(0, 2)
                    dve.wait_ge(gn_mm, g + 1)
                    V.tensor_scalar(two(gr[:, :]), ps[:, 4:6, 0:HALF], 1.0 / (2 * P), EPS, ALU.mult, ALU.add).then_inc(gvar_ready, 1)
                    dve.wait_ge(gsqrt_ready, g + 1)
                    dve.wait_ge(gz_ready, g * 2 + 2)
                    step(V.reciprocal(gr[:, :], gr[:, :]))
                    for i in range(2):
                        V.scalar_tensor_tensor(ysb[:, i, :], ysb[:, i, :], ng[:, one(g * 2 + i)], gr[:, :],
                                               ALU.mult, ALU.mult).then_inc(gn_ready, 1)
                    sample_states(2, 4)
                    if not last:
                        ahead(4)
                    for i in range(2):
                        dve.wait_ge(gn_ready, g * 2 + (i + 1))
                        dve.wait_ge(gh_done, g * 2 + (i + 1))
                        V.tensor_tensor(gl[:, i, :], ysb[:, i, :], gh[:, i, :].bitcast(F32), ALU.subtract).then_inc(g_ready, 1)
                    if not last:
                        conv(g + 1, 2)
                        ahead(5)
                    for m in range(KD):
                        if m % 4 == 3:
                            dve.wait_ge(unit_done, (U_FFN1 - 1 if last else g * 8 + (U_GRP + 13)) + m // 4)
                        else:
                            dve.wait_ge(so_mm, g * 6 + (m - m // 4 + 1))
                        b = 2 * (m % 2) + (4 if last else 0)
                        V.tensor_tensor(two(x[:, m, 0:SEQ]), two(x[:, m, 0:SEQ]), ps[:, b:b + 2, 0:QTR], ALU.add)
                        V.tensor_tensor(x[:, m, SEQ:TOK], x[:, m, SEQ:TOK], ps[:, b + 1, QTR:QTR + SMP],
                                        ALU.add).then_inc(so_evac, 1)
                        if last and m:
                            low_u(2, m - 1)
                        if last and m == KD - 1:
                            low_u(2, m)
                        if not last and m < CONV:
                            conv(g + 1, 3, m)

                stat(1)
                conv_in(0, 0, U_GRP)
                raw_dt()
                conv_in(0, 1, U_GRP + 1)
                log_series()
                conv_in(0, 2, U_GRP + 2)
                dt_and_sums()
                conv_in(0, 3, U_GRP + 3)
                conv(0, 0)
                state_coefs()
                conv(0, 1)
                gate_in(0, 0, U_GRP + 4)
                conv(0, 2)
                gate_in(0, 1, U_GRP + 5)
                token_major()
                head_rows(0)
                conv(0, 3)
                with self_.loop(0, GROUPS - 1, SSD_DVE_STEPS) as g:
                    group(g, False)
                group(GROUPS - 1, True)
                add_squares(2)

            def attention():
                stat(4)
                dve.wait_ge(att_const, 80)
                V.tensor_copy(rmp[:, 0:SEQ].rearrange("p (t a) -> p t a", t=DIL), perm(rms[:, 0:SEQ]))
                step(V.tensor_copy(rmp[:, SEQ:TOK], rms[:, SEQ:TOK]))

                def unit_out(k, u, b):
                    dve.wait_ge(unit_done, u + 1)
                    i = QKV_ORDER[k]
                    dst = stage[:, k - 3, :] if 3 <= k < 3 + AHEAD and b is None else qkv[:, i, :]
                    b = b or 0
                    views = ((two(dst[:, 0:SEQ]), ps[:, b:b + 2, 0:QTR], two(rmp[:, 0:SEQ])),
                             (dst[:, SEQ:TOK], ps[:, b + 1, QTR:QTR + SMP], rmp[:, SEQ:TOK]))
                    for d, src, r in views:
                        if i % 3 == 0:
                            ins = V.scalar_tensor_tensor(d, src, HD ** -0.5, r, ALU.mult, ALU.mult)
                        else:
                            ins = V.tensor_tensor(d, src, r, ALU.mult)
                    ins.then_inc(q_evac, 1)

                def sample_q(n):
                    dve.wait_ge(q_evac, n)
                    for g in range(AG):
                        for j in range(2):
                            r = slice(HD * j, HD * j + HD)
                            src = smp(qkv[r, 3 * g, SEQ:TOK])
                            for s in range(2):
                                dst = qz[r, g, :].rearrange("p (c w) -> p c w", w=64)
                                V.tensor_copy(dst[:, :, 48 * s + j * NS:48 * s + (j + 1) * NS],
                                              src.rearrange("p (c s) q -> p c s q", s=2)[:, :, s, :])
                            ins = V.tensor_copy(smp(qa[r, g, :], 2 * NS)[:, :, j * NS:(j + 1) * NS], src)
                    ins.then_inc(qk_ready, 1)

                for k in range(9):
                    unit_out(k, U_ATT + k, 2 * (k % 2))
                dve.wait_ge(qa_zero, 1)
                sample_q(9)

                def turn(c, last):
                    def ahead(k):
                        unit_out(k, c * 10 + (U_ATT + 9 + k), None)

                    def softmax_in(e):
                        t, j, bank = e // 2, e % 2, score_bank(e, last)
                        dve.wait_ge(sc_mm, c * 8 + (e + 1))
                        if e >= 2:
                            dve.wait_ge(pt_mm, c * 8 + (e - 1))
                        V.scalar_tensor_tensor(pr[:, j, 0:SEQ], d0[:, t, :], slp[:, bass.ds(c * 2 + j, 1)], ps[:, bank, :],
                                               ALU.mult, ALU.add)
                        if e == 1:
                            for g in range(AG):
                                k1 = KEYC + g * SMP
                                V.scalar_tensor_tensor(prs[:, k1:k1 + SMP], dsm[:, k1:k1 + SMP], sls[:, bass.ds(c * AG + g, 1)],
                                                       ps[:, bank + 1, 2 * P + g * SMP:2 * P + (g + 1) * SMP], ALU.mult, ALU.add)
                        for g in (1, 2):
                            o = slice(SEQ + (g - 1) * P, SEQ + g * P)
                            ins = V.scalar_tensor_tensor(pr[:, j, o], d12[:, g - 1, :], slp[:, bass.ds(c * 2 + (AH * g + j), 1)],
                                                         ps[:, bank + 1, (g - 1) * P:g * P], ALU.mult, ALU.add)
                        step(ins)
                        step(V.reduce_max(nmx[:, e:e + 1], pr[:, j, :], AX.X))
                        V.tensor_scalar(nmx[:, e:e + 1], nmx[:, e:e + 1], -1.0, None, ALU.mult).then_inc(max_done, 1)

                    def head_out(e):
                        dve.wait_ge(exp_done, c * 8 + (e + 1))
                        step(V.reciprocal(rcp[:, e:e + 1], den[:, e:e + 1]))
                        dve.wait_ge(pv_mm, c * 8 + (e + 1))
                        V.tensor_scalar(un[:, e // 2, HD * (e % 2):HD * (e % 2) + HD], ps[:, 2, 0:HD],
                                        rcp[:, e:e + 1], None, ALU.mult).then_inc(un_done, 1)

                    softmax_in(0)
                    if last:
                        softmax_in(1)
                    for e in range(8):
                        if e + 1 + last < 8:
                            softmax_in(e + 1 + last)
                        if e == 1:
                            dve.wait_ge(ssc_mm, c + 1)
                            for g, (k0, n) in enumerate(KEYR):
                                ins = V.scalar_tensor_tensor(prs[:, k0:k0 + n], dsm[:, k0:k0 + n], sls[:, bass.ds(c * AG + g, 1)],
                                                             ps[:, 3, k0:k0 + n], ALU.mult, ALU.add)
                            step(ins)
                            step(V.reduce_max(nmx[:, 8:9], prs[:, :], AX.X))
                            V.tensor_scalar(nmx[:, 8:9], nmx[:, 8:9], -1.0, None, ALU.mult).then_inc(smax_done, 1)
                        if e == 2:
                            dve.wait_ge(sexp_done, c + 1)
                            step(V.reciprocal(rcp[:, 8:9], den[:, 8:9]))
                            V.tensor_scalar(prs[:, :], prs[:, :], rcp[:, 8:9], None, ALU.mult).then_inc(snorm_done, 1)
                        if e == 6 + last:
                            dve.wait_ge(soh_done, c + 1)
                            for j in range(2):
                                r = slice(HD * j, HD * j + HD)
                                ins = V.tensor_tensor(smp(ol[r, SEQ:TOK]), smp(ps[r, 3, 0:P], 2 * NS)[:, :, j * NS:(j + 1) * NS],
                                                      smp(oh[r, SEQ:TOK]).bitcast(F32), ALU.subtract)
                            ins.then_inc(sol_done, 1)
                        if not last:
                            if e == 0:
                                dve.wait_ge(st_v, c * 48 + 48)
                            if e == 6:
                                dve.wait_ge(st_k, c * 48 + 48)
                            ahead(e)
                        head_out(e)
                    dve.wait_ge(oh_done, c + 1)
                    V.tensor_tensor(ol[:, 0:SEQ], ps[:, 3, :], oh[:, 0:SEQ].bitcast(F32), ALU.subtract).then_inc(ol_done, 1)
                    if not last:
                        for i in range(AHEAD):
                            ins = V.tensor_copy(qkv[:, QKV_ORDER[3 + i], :], stage[:, i, :])
                        step(ins)
                        ahead(8)
                    for m in range(KD):
                        if m == KD - 1:
                            dve.wait_ge(unit_done, U_FFN[3] if last else c * 10 + (U_ATT + 19))
                        else:
                            dve.wait_ge(ao_mm, c * 7 + (m + 1))
                        b = 4 + 2 * (m % 2)
                        xm = x[:, m, 0:SEQ].rearrange("p (a h t) -> p h t a", h=2, t=2)
                        V.tensor_tensor(xm, xm, ps[:, b:b + 2, 0:QTR].rearrange("p h (t a) -> p h t a", t=2), ALU.add)
                        V.tensor_tensor(x[:, m, SEQ:TOK], x[:, m, SEQ:TOK], ps[:, b + 1, QTR:QTR + SMP],
                                        ALU.add).then_inc(ao_evac, 1)
                        if last and m:
                            low_u(5, m - 1)
                        if last and m == KD - 1:
                            low_u(5, m)
                    if not last:
                        sample_q(c * 9 + 18)

                with self_.loop(0, PAIRS - 1, ATT_DVE_STEPS) as c:
                    turn(c, False)
                turn(PAIRS - 1, True)
                add_squares(5)

            for k, (s, by) in enumerate(((st_hs, 16), (st_nc, 16), (st_h, 16), (conv_done, 1),
                                         (u_ready, 1), (sq_used, 1), (so_evac, 1), (ao_evac, 1), (x_done, 1), (h_ready, 1), (nc_ready, 1))):
                V.memset(rms[:, k:k + 1], 0.0).then_inc(s, by)
            step(V.memset(ssq[:, :], 0.0))
            V.memset(sqx[:, 0:1], 0.0).then_inc(x_done, 1)
            for m in range(KD):
                low_u(0, m)
            add_squares(0)
            dve.wait_ge(const_in, 48)
            ffn(0, 1)
            ssd()
            dve.wait_ge(st_h, 16 * GROUPS + 16)
            dve.wait_ge(st_hs, 16 * GROUPS + 16)
            dve.wait_ge(st_nc, 16 * GROUPS + 16)
            ffn(1, 3)
            ffn(2, 4)
            attention()
            dve.wait_ge(st_v, 16 * PAIRS * AG)
            dve.wait_ge(st_k, 16 * PAIRS * AG)
            ffn(3, 6)
            stat(last_norm)
            for m in range(KD):
                V.scalar_tensor_tensor(x[:, m, :], x[:, m, :], gains[:, last_norm, m:m + 1], rms[:, :],
                                       ALU.mult, ALU.mult).then_inc(y_ready, 1)


def constants():
    a = np.arange(P)
    keys = (DIL * a[None, :] + np.arange(DIL)[:, None]).reshape(-1)
    f = np.float32
    dist = (DIL * a[:, None, None] + np.arange(DIL)[None, :, None]) - keys[None, None, :]
    dist0 = np.where((dist >= 0) & (dist <= 128), dist, BIG).astype(f)
    d = a[:, None] - a[None, :]
    dist12 = np.stack([np.where(d >= 0, DIL * d, BIG), np.where((d >= 0) & (d % 4 == 0), DIL * d, BIG)], 1).astype(f)
    b, j, q = (v.reshape(-1, 1) for v in np.meshgrid(np.arange(NB), np.arange(2), np.arange(NS), indexing="ij"))
    cols = []
    for g, (win, dil) in enumerate(((128, 1), (512, 4), (2048, 16))):
        i = cached_keys(g)[None, :]
        dd = (128 if g == 0 else 256) + q - i
        cols.append(np.where((dd >= 0) & (dd % dil == 0) & (dd <= win), dd, BIG))
    kb, kq = (v.reshape(1, -1) for v in np.meshgrid(np.arange(NB), np.arange(NS), indexing="ij"))
    for g, dil in enumerate((1, 4, 16)):
        dd = q - kq
        cols.append(np.where((kb == b) & (dd >= 0) & (dd % dil == 0), dd, BIG))
    heads = np.arange(1, AG * AH + 1, dtype=np.float64)
    slopes = (-(2.0 ** (-8.0 * heads / (AG * AH)))).astype(f)
    sls = np.stack([slopes.reshape(AG, AH)[g, 2 * c + j[:, 0]] for c in range(PAIRS) for g in range(AG)], 1)
    s = np.arange(SMP)
    keep = np.ones(TOK, f)
    keep[0:SEQ:P] = 0
    keep[SEQ::NS] = 0
    return {
        "ones": np.ones((P, P), f), "ident": np.eye(P, dtype=f), "mask": np.triu(np.ones((P, P), f)),
        "mask_smp": (np.triu(np.ones((SMP, SMP))) * (s[:, None] // NS == s[None, :] // NS)).astype(f),
        "mask_block": (s[:, None] // NS == np.arange(NB)[None, :]).astype(f),
        "keep": np.tile(keep, (H2, 1)), "one_head": np.tile(np.eye(HEADS, dtype=f), (2, 1)), "dist0": dist0, "dist12": dist12,
        "dist_smp": np.concatenate(cols, 1).astype(f), "slopes": np.tile(slopes, (P, 1)), "slopes_smp": sls.astype(f),
    }


def cached_keys(g):
    return np.arange((128, 256, 256)[g]) if g < 2 else np.flatnonzero(np.arange(256) % 16 < NS)


def laid_out(v):
    c = np.ascontiguousarray

    def feature_major(a):
        return a.T.reshape(-1, P, a.shape[0]).transpose(1, 0, 2)

    def per_feature(a):
        return a.reshape(-1, P).T

    def units(w):
        k, n = w.shape[0] // P, w.shape[1] // P
        return w.reshape(k, P, n, P).transpose(2, 1, 0, 3).reshape(n, P, k * P)

    x = np.concatenate([v["x_prompt"][0], v["x_sample"].reshape(SMP, D)])
    gains = np.concatenate([v["norm_w"].reshape(6, D), v["norm_f"][None]])
    w_in = []
    w_out = []
    for i in range(2):
        for j in range(2):
            u = units(v["w_ffn_in"][i, j])
            w_in.append(u.reshape(2, KF, P, UW).transpose(1, 0, 2, 3).reshape(2 * KF, P, UW))
            w_out.append(units(v["w_ffn_out"][i, j]).reshape(KD, P, 2, UF).transpose(0, 2, 1, 3))
    wi = v["ssm_w_in"][0]
    z, xbc, dt = units(wi[:, :DI]), units(wi[:, DI:DI + 4096]), wi[:, DI + 4096:]
    wo = v["ssm_w_out"][0].reshape(GROUPS, 2, P, KD, P).transpose(0, 3, 2, 1, 4)
    wo = wo.reshape(GROUPS, 2, 4, P, 2 * P).transpose(0, 1, 3, 2, 4).reshape(GROUPS, 2, P, UW)
    chunk_of = [[2 * g, 2 * g + 1, 16 + g, 24 + g] for g in range(GROUPS)]
    w_ssd = np.stack([np.concatenate([xbc[chunk_of[g]], z[2 * g:2 * g + 2], wo[g]]) for g in range(GROUPS)])
    dtp = np.zeros((D, P), np.float32)
    dtp[:, :HEADS] = dtp[:, HEADS:H2] = dt
    conv = np.concatenate([v["ssm_conv_w"][0], v["ssm_conv_b"]]).reshape(CONV + 1, 32, P)[:, chunk_of]
    state = v["state_conv"][0].reshape(NB * (CONV - 1), 32, P)[:, chunk_of]
    wq = units(v["attn_w_qkv"][0]).reshape(AG, 3, PAIRS, P, UW).transpose(2, 0, 1, 3, 4).reshape(PAIRS, 9, P, UW)
    wq = wq[:, list(QKV_ORDER)]
    w_att = np.concatenate([wq, v["attn_w_o"][0].reshape(PAIRS, 1, P, D)], 1)
    kv = np.concatenate([v[f"cache_kv_g{g}"][0][:, cached_keys(g)] for g in range(AG)], 1)
    kv = kv.reshape(NB, KEYC, 2, PAIRS, P)
    out = {
        "xT": feature_major(x), "gains": per_feature(gains.reshape(-1)).reshape(P, 7, KD),
        "w_ffn_in": np.stack(w_in), "w_ffn_out": np.stack(w_out),
        "w_dt": units(dtp)[0], "w_ssd": w_ssd,
        "conv_w": conv.transpose(3, 1, 2, 0).reshape(P, GROUPS * 4 * (CONV + 1)),
        "conv_state": state.transpose(3, 1, 2, 0),
        "dt_bias": np.tile(v["ssm_dt_bias"][0], 2)[:, None], "a_log": np.tile(v["ssm_a_log"][0], 2)[:, None],
        "d_skip": np.repeat(v["ssm_d"][0].reshape(16, 2), PD, 1).T, "ssm_gain": per_feature(v["ssm_norm_w"][0]),
        "state": v["state_ssm"][0].reshape(NB, GROUPS, HPG * PD, NST).transpose(1, 3, 0, 2),
        "w_att": w_att,
        "k_cache": kv[:, :, 0].transpose(2, 3, 0, 1),
        "v_cache": kv[:, :, 1].reshape(NB, 4, P, PAIRS, P).transpose(3, 2, 0, 1, 4).reshape(PAIRS, P, NB * 4 * P),
    }
    return {k: c(a) for k, a in {**out, **constants()}.items()}


OUTPUTS = {
    "yT": (P, KD, TOK), "conv_new": (GROUPS, P, 4 * (NB + 1) * (CONV - 1)),
    "ssm_prompt": (GROUPS, P, HPG * PD), "ssm_sample": (GROUPS, P, NB, HPG * PD),
    "kv_new": (PAIRS, 2 * AG, P, TOK),
}


def returned(o):
    c = np.ascontiguousarray
    y = o["yT"].transpose(2, 1, 0).reshape(TOK, D)
    conv = o["conv_new"].reshape(GROUPS, P, 4, NB + 1, CONV - 1).transpose(3, 4, 0, 2, 1)
    conv = np.concatenate([conv[:, :, :, 0:2].reshape(NB + 1, 3, -1), conv[:, :, :, 2].reshape(NB + 1, 3, -1),
                           conv[:, :, :, 3].reshape(NB + 1, 3, -1)], 2)
    sp = o["ssm_prompt"].transpose(0, 2, 1).reshape(1, 1, HEADS, PD, NST)
    ss = o["ssm_sample"].transpose(2, 0, 3, 1).reshape(1, NB, HEADS, PD, NST)
    kv = o["kv_new"].reshape(PAIRS, AG, 2, 2, HD, TOK).transpose(1, 5, 2, 0, 3, 4).reshape(AG, TOK, 2, AH, HD)
    prompt = kv[:, :SEQ].reshape(AG, DIL, P, 2, AH, HD).transpose(0, 2, 1, 3, 4, 5).reshape(AG, SEQ, 2, AH, HD)
    sample = kv[:, SEQ:].reshape(AG, NB, NS, 2, AH, HD)
    out = [y[None, :SEQ], y[SEQ:].reshape(NB, NS, D), conv[None, :1], conv[None, 1:], sp, ss]
    for g, n in enumerate((128, SEQ, SEQ)):
        out += [prompt[g, SEQ - n:][None, None], sample[g][None]]
    return tuple(c(a) for a in out)


def kernel(**inputs):
    import concourse.bacc as bacc
    from concourse.bass_utils import run_bass_kernel_spmd

    nc = bacc.Bacc("TRN2", target_bir_lowering=False, num_devices=1)
    arrays = laid_out({k: np.asarray(a) for k, a in inputs.items()})
    io = {k: nc.dram_tensor(k, a.shape, mybir.dt.from_np(a.dtype), kind="ExternalInput").ap() for k, a in arrays.items()}
    for k, shape in OUTPUTS.items():
        io[k] = nc.dram_tensor(k, shape, F32, kind="ExternalOutput").ap()
    step_kernel(nc, io)
    r = run_bass_kernel_spmd(nc, [arrays], core_ids=[0])
    return returned(r.results[0])
```
